# Optimizing a Trainium2 kernel written in Bass

```python
import math
import jax
import jax.numpy as jnp
from jax import lax
import numpy as np
import jax, jax.numpy as jnp

D_MODEL = 1024
BATCH = 1
SEQ = 256
DEPTH = 1

CHUNK = 64
Q_BLOCK = 128
MEM_LEN = 256
EPS = 1e-6

MLA_HEADS = 4
MLA_Q_RANK = 256
MLA_KV_RANK = 128
MLA_NOPE = 64
MLA_ROPE = 32
MLA_V = 128
ROPE_THETA = 10000.0
FOX_HEADS = 4
FOX_DIM = 64
CHK_HEADS = 4
CHK_DIM = 64
CHK_LEFT = 8
BAND = (CHK_LEFT + 1) * CHUNK
REL_MAX = 128
REL_SIZE = (CHUNK - 1) + REL_MAX + 1

A_WIDTH = MLA_HEADS * MLA_V
B_WIDTH = FOX_HEADS * FOX_DIM
C_WIDTH = CHK_HEADS * CHK_DIM
MIX_WIDTH = A_WIDTH + B_WIDTH + C_WIDTH

IN_SIZES = (MLA_Q_RANK, MLA_KV_RANK, MLA_ROPE,
            B_WIDTH, B_WIDTH, B_WIDTH, FOX_HEADS,
            C_WIDTH, C_WIDTH, C_WIDTH)
IN_WIDTH = sum(IN_SIZES)
IN_SPLIT_POINTS = tuple(int(v) for v in np.cumsum(IN_SIZES)[:-1])

CROSS_HEADS = 4
CROSS_DIM = 128
CROSS_WIDTH = CROSS_HEADS * CROSS_DIM

FFN_HIDDEN = ((-(-(8 * D_MODEL) // 3) + 255) // 256) * 256


def _rmsnorm(x, g):
    xf = x.astype(jnp.float32)
    y = xf * lax.rsqrt(jnp.mean(xf * xf, axis=-1, keepdims=True) + EPS)
    return (y * g.astype(jnp.float32)).astype(x.dtype)

def _rope_tables(seq):
    pos = jnp.arange(seq, dtype=jnp.float32)
    inv = ROPE_THETA ** (-jnp.arange(0, MLA_ROPE, 2, dtype=jnp.float32) / MLA_ROPE)
    ang = pos[:, None] * inv[None, :]
    return jnp.cos(ang), jnp.sin(ang)

def _rope(x, cos, sin):
    xf = x.astype(jnp.float32)
    x1, x2 = jnp.split(xf, 2, axis=-1)
    return jnp.concatenate([x1 * cos - x2 * sin, x1 * sin + x2 * cos], axis=-1).astype(x.dtype)

def _split_blocks(a, block):
    b, s = a.shape[:2]
    return jnp.moveaxis(a.reshape((b, s // block, block) + a.shape[2:]), 1, 0)

def _merge_blocks(a):
    nb, b, blk = a.shape[:3]
    return jnp.moveaxis(a, 0, 1).reshape(b, nb * blk, -1)

def _mla(c_q, c_kv, k_rope, q_norm, w_uq, kv_norm, w_ukv, cos, sin):
    b, s, _ = c_q.shape
    q = (_rmsnorm(c_q, q_norm) @ w_uq).reshape(b, s, MLA_HEADS, MLA_NOPE + MLA_ROPE)
    q_nope, q_pe = jnp.split(q, [MLA_NOPE], axis=-1)
    q = jnp.concatenate([q_nope, _rope(q_pe, cos[:, None], sin[:, None])], axis=-1)
    kv = (_rmsnorm(c_kv, kv_norm) @ w_ukv).reshape(b, s, MLA_HEADS, MLA_NOPE + MLA_V)
    k_nope, v = jnp.split(kv, [MLA_NOPE], axis=-1)
    k_pe = _rope(k_rope, cos, sin)
    k = jnp.concatenate(
        [k_nope, jnp.broadcast_to(k_pe[:, :, None, :], (b, s, MLA_HEADS, MLA_ROPE))], axis=-1)
    scale = (MLA_NOPE + MLA_ROPE) ** -0.5
    k_chunk = jnp.arange(s) // CHUNK

    def attend(args):
        qb, idx = args
        q_chunk = (idx * Q_BLOCK + jnp.arange(Q_BLOCK)) // CHUNK
        sc = jnp.einsum('bqhd,bkhd->bhqk', qb, k, preferred_element_type=jnp.float32) * scale
        sc = jnp.where(k_chunk[None, :] <= q_chunk[:, None], sc, -jnp.inf)
        p = jax.nn.softmax(sc, axis=-1).astype(v.dtype)
        return jnp.einsum('bhqk,bkhd->bqhd', p, v)

    out = lax.map(attend, (_split_blocks(q, Q_BLOCK), jnp.arange(s // Q_BLOCK)))
    return _merge_blocks(out)

def _fox(q, k, v, f_logit, f_bias):
    b, s, _ = q.shape
    q = q.reshape(b, s, FOX_HEADS, FOX_DIM)
    k = k.reshape(b, s, FOX_HEADS, FOX_DIM)
    v = v.reshape(b, s, FOX_HEADS, FOX_DIM)
    log_f = jax.nn.log_sigmoid(f_logit.astype(jnp.float32) + f_bias.astype(jnp.float32))
    cum = jnp.cumsum(log_f, axis=1)
    cum_k = jnp.transpose(cum, (0, 2, 1))
    scale = FOX_DIM ** -0.5
    k_pos = jnp.arange(s)

    def attend(args):
        qb, cq, idx = args
        q_pos = idx * Q_BLOCK + jnp.arange(Q_BLOCK)
        sc = jnp.einsum('bqhd,bkhd->bhqk', qb, k, preferred_element_type=jnp.float32) * scale
        sc = sc + jnp.transpose(cq, (0, 2, 1))[..., None] - cum_k[:, :, None, :]
        sc = jnp.where(k_pos[None, :] <= q_pos[:, None], sc, -jnp.inf)
        p = jax.nn.softmax(sc, axis=-1).astype(v.dtype)
        return jnp.einsum('bhqk,bkhd->bqhd', p, v)

    out = lax.map(attend, (_split_blocks(q, Q_BLOCK), _split_blocks(cum, Q_BLOCK),
                           jnp.arange(s // Q_BLOCK)))
    return _merge_blocks(out)

def _chunk_rel(q, k, v, rel_table):
    b, s, _ = q.shape
    q = q.reshape(b, s, CHK_HEADS, CHK_DIM)
    k = k.reshape(b, s, CHK_HEADS, CHK_DIM)
    v = v.reshape(b, s, CHK_HEADS, CHK_DIM)
    pad = CHK_LEFT * CHUNK
    kp = jnp.pad(k, ((0, 0), (pad, 0), (0, 0), (0, 0)))
    vp = jnp.pad(v, ((0, 0), (pad, 0), (0, 0), (0, 0)))
    qi = jnp.arange(CHUNK)
    ki = jnp.arange(BAND)
    rel = qi[:, None] + pad - ki[None, :]
    rel_idx = jnp.clip(rel, -(CHUNK - 1), REL_MAX) + (CHUNK - 1)
    bias = rel_table[:, rel_idx].astype(jnp.float32)
    scale = CHK_DIM ** -0.5

    def attend(args):
        qc, idx = args
        start = idx * CHUNK
        kb = lax.dynamic_slice_in_dim(kp, start, BAND, axis=1)
        vb = lax.dynamic_slice_in_dim(vp, start, BAND, axis=1)
        valid = (start - pad + ki) >= 0
        sc = jnp.einsum('bqhd,bkhd->bhqk', qc, kb, preferred_element_type=jnp.float32) * scale
        sc = jnp.where(valid, sc + bias[None], -jnp.inf)
        p = jax.nn.softmax(sc, axis=-1).astype(vb.dtype)
        return jnp.einsum('bhqk,bkhd->bqhd', p, vb)

    out = lax.map(attend, (_split_blocks(q, CHUNK), jnp.arange(s // CHUNK)))
    return _merge_blocks(out)

def _cross(h, m, w_cq, w_ckv, w_co):
    b, s, _ = h.shape
    n = m.shape[1]
    q = (h @ w_cq).reshape(b, s, CROSS_HEADS, CROSS_DIM)
    k, v = jnp.split(m @ w_ckv, 2, axis=-1)
    k = k.reshape(b, n, CROSS_HEADS, CROSS_DIM)
    v = v.reshape(b, n, CROSS_HEADS, CROSS_DIM)
    sc = jnp.einsum('bshd,bmhd->bhsm', q, k, preferred_element_type=jnp.float32) * (CROSS_DIM ** -0.5)
    p = jax.nn.softmax(sc, axis=-1).astype(v.dtype)
    o = jnp.einsum('bhsm,bmhd->bshd', p, v).reshape(b, s, CROSS_WIDTH)
    return o @ w_co

def first_inputs(seed: int = 0) -> dict:
    key = jax.random.key(seed)
    ks = jax.random.split(key, 24)

    def nrm(k, shape, fan_in):
        return jax.random.normal(k, shape, jnp.float32) * (fan_in ** -0.5)

    def gain(k, shape):
        return 1.0 + 0.05 * jax.random.normal(k, shape, jnp.float32)

    L = DEPTH
    return {
        'x': jax.random.normal(ks[0], (BATCH, SEQ, D_MODEL), jnp.float32),
        'mem': jax.random.normal(ks[1], (BATCH, MEM_LEN, D_MODEL), jnp.float32),
        'norm_mix': gain(ks[2], (L, D_MODEL)),
        'w_in': nrm(ks[3], (L, D_MODEL, IN_WIDTH), D_MODEL),
        'q_norm': gain(ks[4], (L, MLA_Q_RANK)),
        'w_uq': nrm(ks[5], (L, MLA_Q_RANK, MLA_HEADS * (MLA_NOPE + MLA_ROPE)), MLA_Q_RANK),
        'kv_norm': gain(ks[6], (L, MLA_KV_RANK)),
        'w_ukv': nrm(ks[7], (L, MLA_KV_RANK, MLA_HEADS * (MLA_NOPE + MLA_V)), MLA_KV_RANK),
        'f_bias': jax.random.uniform(ks[8], (L, FOX_HEADS), jnp.float32, minval=1.0, maxval=4.0),
        'rel_bias': 0.3 * jax.random.normal(ks[9], (L, CHK_HEADS, REL_SIZE), jnp.float32),
        'out_norm': gain(ks[10], (L, MIX_WIDTH)),
        'w_o': nrm(ks[11], (L, MIX_WIDTH, D_MODEL), MIX_WIDTH),
        'norm_cross': gain(ks[12], (L, D_MODEL)),
        'norm_mem': gain(ks[13], (L, D_MODEL)),
        'w_cq': nrm(ks[14], (L, D_MODEL, CROSS_WIDTH), D_MODEL),
        'w_ckv': nrm(ks[15], (L, D_MODEL, 2 * CROSS_WIDTH), D_MODEL),
        'w_co': nrm(ks[16], (L, CROSS_WIDTH, D_MODEL), CROSS_WIDTH),
        'norm_ffn': gain(ks[17], (L, D_MODEL)),
        'w_gu': nrm(ks[18], (L, D_MODEL, 2 * FFN_HIDDEN), D_MODEL),
        'w_down': nrm(ks[19], (L, FFN_HIDDEN, D_MODEL), FFN_HIDDEN),
        'final_norm': gain(ks[20], (D_MODEL,)),
    }

def first_block(x, mem, norm_mix, w_in, q_norm, w_uq, kv_norm, w_ukv, f_bias, rel_bias,
              out_norm, w_o, norm_cross, norm_mem, w_cq, w_ckv, w_co, norm_ffn, w_gu,
              w_down, final_norm):
    s = x.shape[1]
    cos, sin = _rope_tables(s)
    for l in range(DEPTH):
        h = _rmsnorm(x, norm_mix[l])
        proj = h @ w_in[l]
        (c_q, c_kv, k_rope, fq, fk, fv, f_logit, cq, ck, cv) = jnp.split(
            proj, IN_SPLIT_POINTS, axis=-1)
        ya = _mla(c_q, c_kv, k_rope, q_norm[l], w_uq[l], kv_norm[l], w_ukv[l], cos, sin)
        yb = _fox(fq, fk, fv, f_logit, f_bias[l])
        yc = _chunk_rel(cq, ck, cv, rel_bias[l])
        ga, gb, gc = jnp.split(out_norm[l], [A_WIDTH, A_WIDTH + B_WIDTH])
        y = jnp.concatenate([_rmsnorm(ya, ga), _rmsnorm(yb, gb), _rmsnorm(yc, gc)], axis=-1)
        x = x + y @ w_o[l]
        x = x + _cross(_rmsnorm(x, norm_cross[l]), _rmsnorm(mem, norm_mem[l]),
                       w_cq[l], w_ckv[l], w_co[l])
        h = _rmsnorm(x, norm_ffn[l])
        gate, up = jnp.split(h @ w_gu[l], 2, axis=-1)
        x = x + (jax.nn.silu(gate) * up) @ w_down[l]
    return _rmsnorm(x, final_norm)


DEPTH_2 = 2

N_EVEN = (DEPTH_2 + 1) // 2
N_ODD = DEPTH_2 // 2

GM_GROUPS = 4
GM_CH = D_MODEL // 8
GM_WIDTH = GM_GROUPS * GM_CH
GM_CHUNK = 128
POOL_WINDOWS = (2, 4, 8, 16)
POOL_GROUPS = len(POOL_WINDOWS)
POOL_CH = D_MODEL // 8
POOL_WIDTH = POOL_GROUPS * POOL_CH
POOL_MAXW = max(POOL_WINDOWS)
EVEN_IN = 2 * GM_WIDTH + POOL_WIDTH
EVEN_MIX = GM_WIDTH + POOL_WIDTH

DA_HEADS = D_MODEL // 128
DA_QK_DIM = 64
DA_V_DIM = 2 * DA_QK_DIM
DA_Q_WIDTH = DA_HEADS * 2 * DA_QK_DIM
DA_V_WIDTH = DA_HEADS * DA_V_DIM
ODD_IN = 2 * DA_Q_WIDTH + DA_V_WIDTH

PEER_HEADS = 8
PEER_NKEYS = 128
PEER_EXPERTS = PEER_NKEYS * PEER_NKEYS
PEER_QDIM = 256
PEER_HALF = PEER_QDIM // 2
PEER_TOPK = 16
PEER_TOKEN_BLOCK = 128


def rmsnorm(x, g):
    xf = x.astype(jnp.float32)
    y = xf * lax.rsqrt(jnp.mean(xf * xf, axis=-1, keepdims=True) + EPS) * g
    return y.astype(x.dtype)

def apply_rope(t, cos, sin):
    t1, t2 = jnp.split(t, 2, axis=-1)
    return jnp.concatenate([t1 * cos - t2 * sin, t2 * cos + t1 * sin], axis=-1)

def chunked_spatial_gating(u, v, w_s, b_s, g_v):
    B, S, _ = v.shape
    vf = v.astype(jnp.float32)
    mu = jnp.mean(vf, axis=-1, keepdims=True)
    var = jnp.mean((vf - mu) ** 2, axis=-1, keepdims=True)
    vn = ((vf - mu) * lax.rsqrt(var + EPS) * g_v).astype(v.dtype)
    vn = vn.reshape(B, S // GM_CHUNK, GM_CHUNK, GM_GROUPS, GM_CH)
    causal = jnp.tril(jnp.ones((GM_CHUNK, GM_CHUNK), dtype=bool))
    w = jnp.where(causal[None], w_s, 0)
    sv = jnp.einsum('gts,bnsgc->bntgc', w, vn) + b_s.T[None, None, :, :, None]
    return u * sv.reshape(B, S, GM_WIDTH)

def multiscale_pool(p, w_pool, ls):
    B, S, _ = p.shape
    pf = p.astype(jnp.float32)
    cs = jnp.cumsum(pf, axis=1)
    cs_pad = jnp.pad(cs, ((0, 0), (POOL_MAXW, 0), (0, 0)))
    t = jnp.arange(S)
    outs = []
    for g, w in enumerate(POOL_WINDOWS):
        sl = slice(g * POOL_CH, (g + 1) * POOL_CH)
        lag = cs_pad[:, POOL_MAXW - w:POOL_MAXW - w + S, sl]
        cnt = jnp.minimum(t + 1, w).astype(jnp.float32)[None, :, None]
        outs.append((cs[..., sl] - lag) / cnt - pf[..., sl])
    pooled = jnp.stack(outs, axis=2).astype(p.dtype)
    mixed = jnp.einsum('bsgc,gcd->bsgd', pooled, w_pool).reshape(B, S, POOL_WIDTH)
    return mixed * ls

def diff_attention(h, w_in, lam_q1, lam_k1, lam_q2, lam_k2, g_sub, w_out, cos, sin, lam_init):
    B, S, _ = h.shape
    proj = h @ w_in
    q = proj[..., :DA_Q_WIDTH].reshape(B, S, DA_HEADS, 2, DA_QK_DIM)
    k = proj[..., DA_Q_WIDTH:2 * DA_Q_WIDTH].reshape(B, S, DA_HEADS, 2, DA_QK_DIM)
    v = proj[..., 2 * DA_Q_WIDTH:].reshape(B, S, DA_HEADS, DA_V_DIM)
    q = apply_rope(q, cos, sin)
    k = apply_rope(k, cos, sin)
    lam = (jnp.exp(jnp.sum(lam_q1.astype(jnp.float32) * lam_k1.astype(jnp.float32)))
           - jnp.exp(jnp.sum(lam_q2.astype(jnp.float32) * lam_k2.astype(jnp.float32)))
           + lam_init)
    scale = DA_QK_DIM ** -0.5
    outs = []
    for i in range(S // Q_BLOCK):
        kv_len = (i + 1) * Q_BLOCK
        q_i = q[:, i * Q_BLOCK:kv_len]
        s = jnp.einsum('bqhmd,bkhmd->bhmqk', q_i, k[:, :kv_len]).astype(jnp.float32) * scale
        q_pos = i * Q_BLOCK + jnp.arange(Q_BLOCK)
        mask = jnp.arange(kv_len)[None, :] <= q_pos[:, None]
        s = jnp.where(mask, s, -jnp.inf)
        pr = jax.nn.softmax(s, axis=-1)
        a = pr[:, :, 0] - lam * pr[:, :, 1]
        outs.append(jnp.einsum('bhqk,bkhd->bqhd', a.astype(v.dtype), v[:, :kv_len]))
    o = jnp.concatenate(outs, axis=1).astype(jnp.float32)
    o = o * lax.rsqrt(jnp.mean(o * o, axis=-1, keepdims=True) + EPS) * g_sub * (1.0 - lam_init)
    return o.astype(h.dtype).reshape(B, S, DA_V_WIDTH) @ w_out

def peer(h, w_q, sub_keys, u_emb, v_emb):
    B, S, D = h.shape
    T = PEER_TOKEN_BLOCK
    K = PEER_TOPK
    hb = h.reshape(B * S // T, T, D)

    def block(x_t):
        q = jnp.einsum('td,dhk->thk', x_t, w_q).reshape(T, PEER_HEADS, 2, PEER_HALF)
        s = jnp.einsum('thpk,hpnk->thpn', q, sub_keys).astype(jnp.float32)
        sv, si = lax.top_k(s, K)
        cand = (sv[:, :, 0, :, None] + sv[:, :, 1, None, :]).reshape(T, PEER_HEADS, K * K)
        cidx = (si[:, :, 0, :, None] * PEER_NKEYS + si[:, :, 1, None, :]).reshape(T, PEER_HEADS, K * K)
        fv, fpos = lax.top_k(cand, K)
        eidx = jnp.take_along_axis(cidx, fpos, axis=-1)
        gate = jax.nn.softmax(fv, axis=-1)
        u = u_emb[eidx]
        v = v_emb[eidx]
        act = jax.nn.gelu(jnp.einsum('thkd,td->thk', u, x_t).astype(jnp.float32), approximate=False)
        return jnp.einsum('thk,thkd->td', (gate * act).astype(x_t.dtype), v)

    return lax.map(block, hb).reshape(B, S, D)

def second_inputs(seed: int = 0) -> dict:
    key = jax.random.key(seed)
    ks = jax.random.split(key, 32)
    f32 = jnp.float32
    D = D_MODEL

    def nrm(k, shape, scale):
        return jax.random.normal(k, shape, f32) * scale

    def gain(k, shape):
        return 1.0 + 0.02 * jax.random.normal(k, shape, f32)

    return {
        "x": nrm(ks[0], (BATCH, SEQ, D), 1.0),
        "c": nrm(ks[1], (BATCH, D), 1.0),
        "positions": jnp.tile(jnp.arange(SEQ, dtype=jnp.int32)[None, :], (BATCH, 1)),
        "ada_w": nrm(ks[2], (DEPTH_2, D, 6 * D), 0.5 * D ** -0.5),
        "ada_b": nrm(ks[3], (DEPTH_2, 6 * D), 0.02),
        "norm_mix": gain(ks[4], (DEPTH_2, D)),
        "norm_ffn": gain(ks[5], (DEPTH_2, D)),
        "ev_w_in": nrm(ks[6], (N_EVEN, D, EVEN_IN), D ** -0.5),
        "ev_g_v": gain(ks[7], (N_EVEN, GM_WIDTH)),
        "ev_w_s": nrm(ks[8], (N_EVEN, GM_GROUPS, GM_CHUNK, GM_CHUNK), GM_CHUNK ** -0.5),
        "ev_b_s": gain(ks[9], (N_EVEN, GM_GROUPS, GM_CHUNK)),
        "ev_w_pool": nrm(ks[10], (N_EVEN, POOL_GROUPS, POOL_CH, POOL_CH), POOL_CH ** -0.5),
        "ev_pool_scale": gain(ks[11], (N_EVEN, POOL_WIDTH)),
        "ev_w_out": nrm(ks[12], (N_EVEN, EVEN_MIX, D), EVEN_MIX ** -0.5),
        "od_w_in": nrm(ks[13], (N_ODD, D, ODD_IN), D ** -0.5),
        "od_lam_q1": nrm(ks[14], (N_ODD, DA_QK_DIM), 0.1),
        "od_lam_k1": nrm(ks[15], (N_ODD, DA_QK_DIM), 0.1),
        "od_lam_q2": nrm(ks[16], (N_ODD, DA_QK_DIM), 0.1),
        "od_lam_k2": nrm(ks[17], (N_ODD, DA_QK_DIM), 0.1),
        "od_g_sub": gain(ks[18], (N_ODD, DA_V_DIM)),
        "od_w_out": nrm(ks[19], (N_ODD, DA_V_WIDTH, D), DA_V_WIDTH ** -0.5),
        "peer_w_q": nrm(ks[20], (DEPTH_2, D, PEER_HEADS, PEER_QDIM), D ** -0.5),
        "peer_sub_keys": nrm(ks[21], (DEPTH_2, PEER_HEADS, 2, PEER_NKEYS, PEER_HALF), PEER_HALF ** -0.5),
        "peer_u": nrm(ks[22], (DEPTH_2, PEER_EXPERTS, D), D ** -0.5),
        "peer_v": nrm(ks[23], (DEPTH_2, PEER_EXPERTS, D), PEER_HEADS ** -0.5),
        "final_norm": gain(ks[24], (D,)),
    }

def second_block(x, c, positions, ada_w, ada_b, norm_mix, norm_ffn,
              ev_w_in, ev_g_v, ev_w_s, ev_b_s, ev_w_pool, ev_pool_scale, ev_w_out,
              od_w_in, od_lam_q1, od_lam_k1, od_lam_q2, od_lam_k2, od_g_sub, od_w_out,
              peer_w_q, peer_sub_keys, peer_u, peer_v, final_norm):
    B, S, D = x.shape
    inv_freq = 1.0 / (ROPE_THETA ** (jnp.arange(0, DA_QK_DIM, 2, dtype=jnp.float32) / DA_QK_DIM))
    ang = positions.astype(jnp.float32)[..., None] * inv_freq
    cos = jnp.cos(ang)[:, :, None, None, :].astype(x.dtype)
    sin = jnp.sin(ang)[:, :, None, None, :].astype(x.dtype)
    c_act = jax.nn.silu(c)
    for l in range(DEPTH_2):
        mod = (c_act @ ada_w[l] + ada_b[l]).reshape(B, 6, D)[:, :, None, :]
        sh1, sc1, g1, sh2, sc2, g2 = (mod[:, i] for i in range(6))
        h = rmsnorm(x, norm_mix[l]) * (1 + sc1) + sh1
        if l % 2 == 0:
            e = l // 2
            proj = h @ ev_w_in[e]
            z = jax.nn.gelu(proj[..., :2 * GM_WIDTH], approximate=False)
            ya = chunked_spatial_gating(z[..., :GM_WIDTH], z[..., GM_WIDTH:],
                                        ev_w_s[e], ev_b_s[e], ev_g_v[e])
            yb = multiscale_pool(proj[..., 2 * GM_WIDTH:], ev_w_pool[e], ev_pool_scale[e])
            y = jnp.concatenate([ya, yb], axis=-1) @ ev_w_out[e]
        else:
            o = l // 2
            lam_init = 0.8 - 0.6 * math.exp(-0.3 * l)
            y = diff_attention(h, od_w_in[o], od_lam_q1[o], od_lam_k1[o], od_lam_q2[o],
                               od_lam_k2[o], od_g_sub[o], od_w_out[o], cos, sin, lam_init)
        x = x + g1 * y
        h = rmsnorm(x, norm_ffn[l]) * (1 + sc2) + sh2
        x = x + g2 * peer(h, peer_w_q[l], peer_sub_keys[l], peer_u[l], peer_v[l])
    return rmsnorm(x, final_norm)


def setup_inputs(seed=0):
    out = dict(first_inputs(seed))
    for name, value in second_inputs(seed + 1).items():
        if name != "x":
            out[name + "_2"] = value
    return out


def reference(
    x, mem, norm_mix, w_in, q_norm, w_uq, kv_norm, w_ukv, f_bias, rel_bias, out_norm, w_o,
    norm_cross, norm_mem, w_cq, w_ckv, w_co, norm_ffn, w_gu, w_down, final_norm, c_2,
    positions_2, ada_w_2, ada_b_2, norm_mix_2, norm_ffn_2, ev_w_in_2, ev_g_v_2, ev_w_s_2,
    ev_b_s_2, ev_w_pool_2, ev_pool_scale_2, ev_w_out_2, od_w_in_2, od_lam_q1_2, od_lam_k1_2,
    od_lam_q2_2, od_lam_k2_2, od_g_sub_2, od_w_out_2, peer_w_q_2, peer_sub_keys_2, peer_u_2,
    peer_v_2, final_norm_2,
):
    x = first_block(
        x, mem, norm_mix, w_in, q_norm, w_uq, kv_norm, w_ukv, f_bias, rel_bias, out_norm, w_o,
        norm_cross, norm_mem, w_cq, w_ckv, w_co, norm_ffn, w_gu, w_down, final_norm,
    )
    return second_block(
        x, c_2, positions_2, ada_w_2, ada_b_2, norm_mix_2, norm_ffn_2, ev_w_in_2, ev_g_v_2,
        ev_w_s_2, ev_b_s_2, ev_w_pool_2, ev_pool_scale_2, ev_w_out_2, od_w_in_2, od_lam_q1_2,
        od_lam_k1_2, od_lam_q2_2, od_lam_k2_2, od_g_sub_2, od_w_out_2, peer_w_q_2,
        peer_sub_keys_2, peer_u_2, peer_v_2, final_norm_2,
    )


_drawn_inputs = setup_inputs


def setup_inputs(seed=0):
    import zlib

    import numpy as np

    out = dict(_drawn_inputs(seed))
    spreads = {}
    factors = {'norm_cross': 8.0,
     'norm_mem': 6.01,
     'norm_mix_2': 5.898,
     'norm_ffn_2': 38.6,
     'ev_g_v_2': 41.723,
     'ev_b_s_2': 30.842,
     'ev_pool_scale_2': 22.169,
     'od_lam_q1_2': 64.0,
     'od_lam_k1_2': 64.0,
     'od_lam_q2_2': 131.375,
     'od_lam_k2_2': 7.397,
     'od_g_sub_2': 200.0,
     'final_norm_2': 22.5,
     'norm_ffn': 5.046}
    for name, (base, spread) in spreads.items():
        noise = np.random.default_rng([zlib.crc32(name.encode()), seed]).standard_normal(out[name].shape)
        drawn = base * np.exp(spread * noise) if base else spread * noise
        out[name] = jnp.asarray(drawn.astype(out[name].dtype))
    for name, factor in factors.items():
        out[name] = (out[name] * factor).astype(out[name].dtype)
    return out
```

```python
from contextlib import ExitStack

import numpy as np

import concourse.bass as bass
from concourse import mybir

P = 128
D = 1024
KT = D // P
T = 256
NB = T // P
EPS = 1e-6
NEG = -1e30

MLA_H, NOPE, ROPE, MLA_V = 4, 64, 32, 128
QK = NOPE + ROPE
FFN = 2816
FT = FFN // P
HEADS8, TOPK, NKEYS = 8, 16, 128
SETS = 2 * HEADS8
TILES = NKEYS
SUB = 2.0 ** -40
SUB_MAX = 2.0 ** 26
SUM_MAX = 3.4028234663852886e38 * SUB * SUB
LAM_INIT = 0.8 - 0.6 * float(np.exp(-0.3))
WINDOWS = (2, 4, 8, 16)

F32 = mybir.dt.float32
I32 = mybir.dt.int32
U32 = mybir.dt.uint32
F32R = mybir.dt.float32r
ALU = mybir.AluOpType
ACT = mybir.ActivationFunctionType
AX = mybir.AxisListType.X

SLOTS = 3
SLOT = 4096
E_SLOTS = 3
STEP = 6
GROUP = 4

COLS = {}
_at = 0
for _name, _n in (("norm_mix", 8), ("q_norm", 2), ("kv_norm", 1), ("out_norm", 8), ("norm_cross", 8),
                  ("norm_mem", 8), ("norm_ffn", 8), ("final_norm", 8), ("c", 8), ("ada_b", 96),
                  ("norm_mix_2", 16), ("norm_ffn_2", 16), ("g_v", 4), ("pool_scale", 4), ("b_s", 4),
                  ("g_sub", 1), ("final_norm_2", 8), ("f_bias", 4)):
    COLS[_name] = (_at, _n)
    _at += _n
NCOLS = _at

def _plan():
    ada = [("ada", l, j) for l in range(2) for j in range(12)]
    order = [("win", i) for i in range(5)] + [("mla",), ("ck",), ("cv",)]
    for name in [("wo", 0), ("wo", 1), ("wcq",), ("wco",)] + [("gu", i) for i in range(FT // 2)] + [("down", i) for i in range(6)]:
        order += [name, ada.pop(0)]
    for name in [("ev", 0), ("ev", 1), ("ev", 2)]:
        order += [name, ada.pop(0)]
    order += [("evs",), ("evo", 0), ("evo", 1)] + [("pq", 0, i) for i in range(4)] + [("keys", 0)]
    order += [("od", i) for i in range(6)] + [("odo", 0), ("odo", 1)] + [("pq", 1, i) for i in range(4)] + [("keys", 1)]
    return order


STREAM = _plan()
WIN = (0, 416, 928, 1188, 1700, 1956)
SIZE = {("mla",): 2 * 384 + 768, ("evs",): 1024, ("down", 5): 2048, ("keys", 0): 2048, ("keys", 1): 2048}
SIZE |= {("win", i): KT * (WIN[i + 1] - WIN[i]) for i in range(5)}
BEFORE_EXPERTS = {("keys", 0): 0, ("keys", 1): 1}


def program(nc, d, out, probes=None, upto=99):
    ctx = ExitStack()
    with ctx:
        def sb(name, n, dt=F32):
            return ctx.enter_context(nc.sbuf_tensor(name, [P, n], dt))

        sems = {}

        def sem(name):
            if name not in sems:
                sems[name] = ctx.enter_context(nc.semaphore(name))
            return sems[name]

        X = sb("X", NB * D)[:, :].rearrange("p (b n) -> p b n", b=NB)
        cols = sb("cols", NCOLS)
        ident = sb("ident", P)[:, :]
        iota = sb("iota", P)[:, :]
        MOD = sb("MOD", 96)
        vec = sb("vec", 64)
        stat = sb("stat", 3 * 80)
        small = sb("small", 64)
        slots_t = sb("slots_t", 3 * T)[:, :].rearrange("p (a t) -> p a t", a=3)
        arena = sb("arena", T * NKEYS)
        pos_i = sb("pos_i", NB, I32)
        ps = ctx.enter_context(nc.psum_tensor("ps", [P, 8, 512], F32))

        def col(name, i=0, n=None):
            a, w = COLS[name]
            return cols[:, a + i:a + i + (w if n is None else n)]

        class Region:
            def __init__(self, at=0):
                self.at = at

            def take(self, n, dt=None):
                a = arena[:, self.at:self.at + n]
                self.at += n
                assert self.at <= T * NKEYS, self.at
                return a if dt is None else a.bitcast(dt)

        def r3(a, n):
            return a.rearrange("p (a b) -> p a b", a=n)

        one = Region()
        causal = r3(one.take(2 * T), NB)
        chunked = r3(one.take(2 * T), NB)
        tri = r3(one.take(2 * T), NB)
        rot = r3(one.take(2 * ROPE), NB)
        relb = one.take(2 * 4 * T).rearrange("p (b h k) -> p b h k", b=2, h=4)
        start_reuse = one.at
        pa = r3(one.take(2 * 416), NB)
        fqk = r3(one.take(4 * T), 4)
        pc = r3(one.take(2 * 260), NB)
        cqk = r3(one.take(4 * T), 4)
        pe_ = r3(one.take(2 * 256), NB)
        lat_n = r3(one.take(2 * 384), NB)
        lat_t = r3(one.take(3 * T), 3)
        mq = r3(one.take(2 * 384), NB)
        mq_t = r3(one.take(4 * T), 4)
        mkv = r3(one.take(2 * 768), NB)
        mk = r3(one.take(2 * 384), NB)
        mk_t = r3(one.take(4 * T), 4)
        rtmp = r3(one.take(4 * 64), 4)
        flb = one.take(2 * 4 * T).rearrange("p (b h k) -> p b h k", b=2, h=4)
        nfl = one.take(2 * 4 * P).rearrange("p (b h k) -> p b h k", b=2, h=4)
        ymix = r3(one.take(2 * D), NB)
        s_buf = one.take(2 * D).rearrange("p (u m k) -> p u m k", u=2, m=4)
        p_buf = one.take(2 * D).rearrange("p (u m k) -> p u m k", u=2, m=4)
        pt_buf = one.take(2 * D).rearrange("p (u m a q) -> p u m a q", u=2, m=4, a=2)
        mem_t = r3(one.take(KT * T), KT)
        mem = r3(one.take(2 * D), NB)
        acc_ada = r3(mem.rearrange("p b n -> p (b n)"), 4)
        cross_k = r3(one.take(4 * T), 4)
        cross_v = r3(one.take(2 * 512), NB)
        cross_q, cross_t = fqk, mq_t
        cross_o = r3(cqk.rearrange("p a b -> p (a b)"), NB)
        ffn = Region(start_reuse)
        act_t = r3(ffn.take(FT * T), FT)
        silu_g = r3(ffn.take(2 * 512), 2)
        diag_f = ffn.take(D)

        two = Region()
        ug_t = r3(two.take(4 * T), 4)
        vg = r3(two.take(2 * 512), NB)
        vn = r3(two.take(2 * 512), NB)
        pl = r3(two.take(2 * 512), NB)
        bs_row = r3(two.take(4 * P), 4)
        pl_t = r3(two.take(4 * T), 4)
        ws_m = r3(two.take(4 * P), 4)
        diag_2 = two.take(D)
        bn = two.take(2 * 8)
        two.at = max(two.at, 20480)
        pool_mat = two.take(2 * 4 * T).rearrange("p (s g t) -> p s g t", s=2, g=4)
        tri_2 = two.take(P)

        three = Region()
        causal_3 = r3(three.take(2 * T), NB)
        inv_f = three.take(32)
        lam_in = r3(three.take(4 * 64), 4)
        lam_p = r3(three.take(2 * 64), 2)
        ang = three.take(6 * 64).rearrange("p (a b f) -> p a b f", a=6, b=2)
        proj = r3(three.take(2 * 3072), NB)
        rt3 = r3(three.take(4 * 512), 4)
        dqk = three.take(2 * 2 * D).rearrange("p (a b n) -> p a b n", a=2, b=2)
        dq_t = r3(three.take(8 * T), 8)
        dk_t = r3(three.take(8 * T), 8)
        do = r3(three.take(2 * D), NB)
        dtmp = r3(three.take(2 * 512), 2)
        s_buf3 = three.take(2 * D).rearrange("p (u m k) -> p u m k", u=2, m=4)
        p_buf3 = three.take(2 * D).rearrange("p (u m k) -> p u m k", u=2, m=4)
        pt_buf3 = three.take(2 * D).rearrange("p (u m a q) -> p u m a q", u=2, m=4, a=2)
        diag_3 = three.take(D)

        ch = Region()
        pq_t = r3(ch.take(SETS * T), SETS)
        sc = ch.take(2 * SETS * P).rearrange("p (b s n) -> p b s n", b=2, s=SETS)
        sw = ch.take(2 * SETS * P).rearrange("p (b s n) -> p b s n", b=2, s=SETS)
        top_v = ch.take(2 * SETS * TOPK).rearrange("p (b s k) -> p b s k", b=2, s=SETS)
        top_i = ch.take(2 * SETS * TOPK, U32).rearrange("p (b s k) -> p b s k", b=2, s=SETS)
        top_f = ch.take(2 * SETS * TOPK).rearrange("p (b s k) -> p b s k", b=2, s=SETS)
        cand = ch.take(2 * 2048).rearrange("p (b h n) -> p b h n", b=2, h=8)
        cw = ch.take(2 * 2048).rearrange("p (b h n) -> p b h n", b=2, h=8)
        fin_v = ch.take(2 * P).rearrange("p (b h k) -> p b h k", b=2, h=8)
        fin_p = ch.take(2 * P, U32).rearrange("p (b h k) -> p b h k", b=2, h=8)
        fin_ij = ch.take(4 * P, U32).rearrange("p (a b h k) -> p a b h k", a=2, b=2, h=8)
        fin_f = ch.take(4 * P).rearrange("p (a b h k) -> p a b h k", a=2, b=2, h=8)
        eq = ch.take(2 * 2048).rearrange("p (a n) -> p a n", a=2)
        chosen = ch.take(6 * P).rearrange("p (b a h k) -> p b a h k", b=2, a=3, h=8)
        gsum = ch.take(2 * 16).rearrange("p (b a h) -> p b a h", b=2, a=2)
        gates = arena[:, :].rearrange("p (t i) -> p t i", i=NKEYS)

        ones = sb("ones", P)[:, :]
        eps = small[:, 0:1]
        unit = small[:, 1:2]
        fz = r3(small[:, 2:34], 4).rearrange("p a (b h) -> p a b h", b=2)
        mx = r3(small[:, 34:42], 2)
        sums = r3(small[:, 42:50], 2)
        rinv = r3(small[:, 50:58], 2)
        coef = small[:, 58:62]
        lam2 = small[:, 62:64]
        wcoef = r3(stat[:, 228:236], 2)
        posf = stat[:, 236:238]
        cact = sb("cact", 8)
        newton = sb("newton", 32)
        shared = (("HN", NB * D), ("HT", KT * T), ("ring", SLOTS * SLOT))
        with ExitStack() as whole_floats:
            hn_flat, ht_flat, ring = [whole_floats.enter_context(nc.sbuf_tensor(name, [P, n], F32))[:, :] for name, n in shared]
        hn_r, ht_r, ring_r = [sb(f"{name}_rounded", n, F32R)[:, :] for name, n in shared]
        HN = hn_flat.rearrange("p (b n) -> p b n", b=NB)
        HT = ht_flat.rearrange("p (k t) -> p k t", k=KT)

        def norm(src, dst, segs, junk=None):
            return dict(src=src, dst=dst, segs=segs, junk=junk or dst)

        whole = [(0, D)]
        NORMS = {
            "mix": norm(lambda b: X[:, b, :], lambda b: HN[:, b, :], whole),
            "mem": norm(lambda b: mem[:, b, :], lambda b: mem[:, b, :], whole,
                        lambda b: mem_t.rearrange("p k t -> p (k t)")[:, b * D:(b + 1) * D]),
            "lat": norm(lambda b: pa[:, b, 0:384], lambda b: lat_n[:, b, :], [(0, 256), (256, 384)]),
            "y": norm(lambda b: ymix[:, b, :], lambda b: HN[:, b, :], [(0, 512), (512, 768), (768, 1024)]),
            "cross": norm(lambda b: X[:, b, :], lambda b: HN[:, b, :], whole),
            "ffn": norm(lambda b: X[:, b, :], lambda b: HN[:, b, :], whole),
            "end1": norm(lambda b: X[:, b, :], lambda b: HN[:, b, :], whole),
            "mix_0": norm(lambda b: X[:, b, :], lambda b: HN[:, b, :], whole),
            "peer_0": norm(lambda b: X[:, b, :], lambda b: HN[:, b, :], whole),
            "mix_1": norm(lambda b: X[:, b, :], lambda b: HN[:, b, :], whole),
            "sub": norm(lambda b: do[:, b, :], lambda b: HN[:, b, :], [(128 * h, 128 * h + 128) for h in range(8)]),
            "peer_1": norm(lambda b: X[:, b, :], lambda b: HN[:, b, :], whole),
            "end2": norm(lambda b: X[:, b, :], lambda b: HN[:, b, :], whole),
        }
        at = 0
        for k, (name, n) in enumerate(NORMS.items()):
            n["no"], n["col"] = k, at
            at += 2 * len(n["segs"])
        assert at <= 76, at
        ss, rms, rstd = stat[:, 0:76], stat[:, 76:152], stat[:, 152:228]

        def widths(segs):
            groups = []
            for i, (lo, hi) in enumerate(segs):
                if groups and groups[-1][2] == hi - lo:
                    groups[-1][1] += 1
                else:
                    groups.append([i, i + 1, hi - lo])
            return groups

        PAIRED = (0, 2, 1, 3)

        def unit_of(kind, b, g=0):
            u = dict(kind=kind, b=b)
            if kind == "mla":
                u["qk"] = [[(mq_t[0:QK, h, b * P:(b + 1) * P], mk_t[0:QK, h, :])] for h in range(4)]
                u["v"] = lambda kb, h: mkv[:, kb, h * 192 + 64:(h + 1) * 192]
                u["scale"], u["dv"], u["mask"] = float(QK) ** -0.5, 128, chunked
                u["out"] = ymix[:, b, 0:512]
            elif kind == "fox":
                u["qk"] = []
                for h in PAIRED:
                    q = slice(64 * (h % 2), 64 * (h % 2) + 64)
                    pairs = [(fqk[q, h // 2, b * P:(b + 1) * P], fqk[q, 2 + h // 2, :])]
                    for s in range(NB):
                        pairs.append((tri[:, s, b * P:(b + 1) * P], flb[:, s, h, :]))
                        pairs.append((nfl[:, s, h, :], tri[:, s, :]))
                    u["qk"].append(pairs)
                u["v"] = lambda kb, m: pc[:, kb, PAIRED[m] * 64:(PAIRED[m] + 1) * 64]
                u["scale"], u["dv"], u["mask"] = 0.125, 64, causal
                u["out"] = ymix[:, b, 512:768]
            elif kind == "chk":
                u["qk"] = []
                for h in PAIRED:
                    q = slice(64 * (h % 2), 64 * (h % 2) + 64)
                    u["qk"].append([(cqk[q, h // 2, b * P:(b + 1) * P], cqk[q, 2 + h // 2, :])])
                u["v"] = lambda kb, m: pe_[:, kb, PAIRED[m] * 64:(PAIRED[m] + 1) * 64]
                u["scale"], u["dv"], u["mask"] = 0.125, 64, "rel"
                u["out"] = ymix[:, b, 768:1024]
            elif kind == "cross":
                u["qk"] = [[(cross_q[:, h, b * P:(b + 1) * P], cross_k[:, h, :])] for h in range(4)]
                u["v"] = lambda kb, h: cross_v[:, kb, h * P:(h + 1) * P]
                u["scale"], u["dv"], u["mask"] = float(P) ** -0.5, 128, None
                u["out"] = cross_o[:, b, :]
            else:
                u["qk"] = []
                for i in range(4):
                    h, q = 2 * g + i % 2, slice(64 * (i // 2), 64 * (i // 2) + 64)
                    u["qk"].append([(dq_t[q, h, b * P:(b + 1) * P], dk_t[q, h, :])])
                u["v"] = lambda kb, i: proj[:, kb, 2048 + (2 * g + i % 2) * P:2048 + (2 * g + i % 2 + 1) * P]
                u["scale"], u["dv"], u["mask"] = 0.125, 128, causal_3
                u["out"] = do[:, b, 2 * g * P:(2 * g + 2) * P]
            return u

        ATT = {"self": [unit_of(k, b) for k in ("mla", "fox", "chk") for b in range(NB)],
               "cross": [unit_of("cross", b) for b in range(NB)],
               "diff": [unit_of("diff", b, g) for g in range(4) for b in range(NB)]}
        n = 0
        for units in ATT.values():
            for u in units:
                u["no"] = n
                sbuf, pbuf, ptbuf = (s_buf3, p_buf3, pt_buf3) if u["kind"] == "diff" else (s_buf, p_buf, pt_buf)
                u["s"], u["p"], u["pt"] = sbuf[:, n % 2], pbuf[:, n % 2], ptbuf[:, n % 2]
                n += 1

        tile_no = {}
        chunk_no = {name: i for i, name in enumerate(STREAM)}
        released = {}

        def weights(name):
            s = chunk_no[name] % SLOTS
            return ring[:, s * SLOT:s * SLOT + SIZE.get(name, SLOT)]

        def wait_weights(eng, name):
            i = chunk_no[name]
            eng.wait_ge(sem(f"arrived{i % SLOTS}"), 16 * (i // SLOTS + 1))

        def tile(name):
            return ps[:, tile_no[name] % 8, :]

        def wait_tile(eng, name):
            i = tile_no[name]
            eng.wait_ge(sem(f"filled{i % 8}"), i // 8 + 1)
            return tile(name)

        def drained(ins, name):
            ins.then_inc(sem(f"drained{tile_no[name] % 8}"), 1)

        exp_u = r3(ring[:, 0:3 * D], E_SLOTS)
        exp_v = r3(ring[:, 3 * D:6 * D], E_SLOTS)
        exp_ul = r3(ring_r[:, 0:3 * D], E_SLOTS)
        exp_vl = r3(ring_r[:, 3 * D:6 * D], E_SLOTS)
        exp_uh = r3(ring_r[:, 6 * D:8 * D], 2)
        exp_vh = r3(ring_r[:, 8 * D:10 * D], 2)
        ht_high = r3(ring_r[:, 10 * D:12 * D], KT)
        ht_low = r3(ht_r, KT)
        act_e = r3(hn_flat[:, 0:512], 2)
        act_l = r3(hn_r[:, 0:512], 2)
        act_h = r3(hn_r[:, 512:1024], 2)
        g2_row = hn_flat[:, 1024:2048]
        hot = hn_flat.rearrange("p (u a t n) -> p u a t n", u=2, a=2, t=GROUP)
        NG = T // GROUP

        block = ctx.enter_context(nc.Block())

        @block.tensor
        def _(pe):
            def claim(name):
                i = len(tile_no)
                tile_no[name] = i
                if i >= 8:
                    pe.wait_ge(sem(f"drained{i % 8}"), i // 8)
                return ps[:, i % 8, :]

            def publish(ins, name):
                ins.then_inc(sem(f"filled{tile_no[name] % 8}"), 1)
                return sem(f"filled{tile_no[name] % 8}"), tile_no[name] // 8 + 1

            def rows(chunk, name, src, w, n, nk=KT):
                for b in range(NB):
                    t = claim((name, b))
                    for k in range(nk):
                        mm = pe.matmul(t[:, 0:n], src[:, k, b * P:(b + 1) * P], w[:, k, :],
                                       start=(k == 0), stop=(k == nk - 1))
                    released[chunk] = publish(mm, (name, b))

            def turned(chunk, name, src, w, n):
                for i in range(n // 256):
                    t = claim((name, i))
                    for j in range(2):
                        for k in range(KT):
                            mm = pe.matmul(t[:, j * T:(j + 1) * T], w[:, k, i * 256 + j * P:i * 256 + (j + 1) * P],
                                           src[:, k, :], start=(k == 0), stop=(k == KT - 1))
                    released[chunk] = publish(mm, (name, i))

            def turn(norm, nk=KT, src=None, waits=True):
                n = NORMS[norm]
                pe.wait_ge(sem("normed"), n["no"] + 1)
                for b in range(NB):
                    for i in range(0, nk, 4):
                        t = claim((norm, b, i))
                        for k in range(i, min(i + 4, nk)):
                            mm = pe.transpose(t[:, (k - i) * P:(k - i + 1) * P], n["dst"](b)[:, k * P:(k + 1) * P], ident)
                        publish(mm, (norm, b, i))

            def turn_heads(name, src, width, heads):
                for b in range(NB):
                    for i in range(0, heads, 4):
                        t = claim((name, b, i))
                        for h in range(i, i + 4):
                            mm = pe.transpose(t[0:width, (h - i) * P:(h - i + 1) * P],
                                              src[:, b, h * width:(h + 1) * width], ident)
                        publish(mm, (name, b, i))

            def scores(u):
                for half in range(2):
                    t = claim(("s", u["no"], half))
                    for m in range(2):
                        pairs = u["qk"][2 * half + m]
                        for i, (q, k) in enumerate(pairs):
                            mm = pe.matmul(t[:, m * T:(m + 1) * T], q, k, start=(i == 0), stop=(i == len(pairs) - 1))
                    publish(mm, ("s", u["no"], half))

            def turn_probs(u):
                pe.wait_ge(sem("probs"), u["no"] + 1)
                for half in range(2):
                    t = claim(("pt", u["no"], half))
                    for m in range(2):
                        for kb in range(NB):
                            mm = pe.transpose(t[:, (2 * m + kb) * P:(2 * m + kb + 1) * P],
                                              u["p"][:, 2 * half + m, kb * P:(kb + 1) * P], ident)
                    publish(mm, ("pt", u["no"], half))

            def values(u):
                pe.wait_ge(sem("probs_turned"), u["no"] + 1)
                t = claim(("o", u["no"]))
                for m in range(4):
                    for kb in range(NB):
                        mm = pe.matmul(t[:, m * u["dv"]:(m + 1) * u["dv"]], u["pt"][:, m, kb, :], u["v"](kb, m),
                                       start=(kb == 0), stop=(kb == NB - 1))
                publish(mm, ("o", u["no"]))

            def attention(units):
                scores(units[0])
                for i, u in enumerate(units):
                    if i + 1 < len(units):
                        scores(units[i + 1])
                    turn_probs(u)
                    values(u)

            def fold(l, j):
                i = 12 * l + j
                pe.wait_ge(sem("ada_summed"), i + 1)
                t = claim(("ada", l, j))
                for c in range(4):
                    mm = pe.matmul(t[:, c:c + 1], acc_ada[:, i % 4, c * P:(c + 1) * P], ones[:, 0:1], start=True, stop=True)
                publish(mm, ("ada", l, j))

            ada_left = [(l, j) for l in range(2) for j in range(12)]

            def next_fold():
                fold(*ada_left.pop(0))

            def spread(name, diag, n=8):
                pe.wait_ge(sem("diag"), SPREADS[name] + 1)
                for i in range(0, n, 4):
                    t = claim(("spread", name, i))
                    for k in range(i, i + 4):
                        mm = pe.matmul(t[:, (k - i) * P:(k - i + 1) * P], ones, diag[:, k * P:(k + 1) * P], start=True, stop=True)
                    publish(mm, ("spread", name, i))

            pe.wait_ge(sem("consts"), 48)
            pe.wait_ge(sem("made"), 3)
            turn("mix")
            pe.wait_ge(sem("h_ready"), H_READY["mix"])
            names = {0: "a", 1: "b", 2: "c", 3: "d", 4: "e"}
            for i in range(5):
                wait_weights(pe, ("win", i))
                n = WIN[i + 1] - WIN[i]
                w = r3(weights(("win", i)), KT)
                (turned if i in (1, 3) else rows)(("win", i), ("win", i), HT, w, n)
                if i == 1:
                    turn("lat", 3)
                if i == 2:
                    turn("mem")
            pe.wait_ge(sem("h_ready"), H_READY["lat"])
            wait_weights(pe, ("mla",))
            w = weights(("mla",))
            rows(("mla",), "mq", lat_t, r3(w[:, 0:768], 2), 384, 2)
            for half in range(2):
                for b in range(NB):
                    t = claim(("mkv", half, b))
                    mm = pe.matmul(t[:, 0:384], lat_t[:, 2, b * P:(b + 1) * P], w[:, 768 + half * 384:768 + (half + 1) * 384],
                                   start=True, stop=True)
                    released[("mla",)] = publish(mm, ("mkv", half, b))
            pe.wait_ge(sem("h_ready"), H_READY["mem"])
            wait_weights(pe, ("ck",))
            turned(("ck",), "ck", mem_t, r3(weights(("ck",)), KT), 512)
            pe.wait_ge(sem("roped"), 1)
            turn_heads("mq_t", mq, QK, 4)
            turn_heads("mk_t", mk, QK, 4)
            wait_weights(pe, ("cv",))
            rows(("cv",), "cv", mem_t, r3(weights(("cv",)), KT), 512)
            pe.wait_ge(sem("heads_turned"), 4)
            pe.wait_ge(sem("stored"), STORED["win"])
            pe.wait_ge(sem("forget"), 1)
            pe.wait_ge(sem("masks"), 64)
            attention(ATT["self"])
            turn("y")
            pe.wait_ge(sem("h_ready"), H_READY["y"])
            for i in range(2):
                wait_weights(pe, ("wo", i))
                rows(("wo", i), ("wo", i), HT, r3(weights(("wo", i)), KT), 512)
                if i:
                    next_fold()
            turn("cross")
            pe.wait_ge(sem("h_ready"), H_READY["cross"])
            wait_weights(pe, ("wcq",))
            turned(("wcq",), "wcq", HT, r3(weights(("wcq",)), KT), 512)
            next_fold()
            pe.wait_ge(sem("stored"), STORED["wcq"])
            attention(ATT["cross"])
            pe.wait_ge(sem("cross_out"), 1)
            turn_heads("cross_t", cross_o, P, 4)
            pe.wait_ge(sem("heads_turned"), 6)
            wait_weights(pe, ("wco",))
            w = r3(weights(("wco",)), 4)
            next_fold()
            for b in range(NB):
                for half in range(2):
                    t = claim(("wco", b, half))
                    for k in range(4):
                        mm = pe.matmul(t, cross_t[:, k, b * P:(b + 1) * P], w[:, k, half * 512:(half + 1) * 512],
                                       start=(k == 0), stop=(k == 3))
                    released[("wco",)] = publish(mm, ("wco", b, half))
            turn("ffn")
            pe.wait_ge(sem("h_ready"), H_READY["ffn"])
            for i in range(FT // 2):
                name = ("gu", i)
                wait_weights(pe, name)
                turned(name, name, HT, r3(weights(name), KT), 512)
                next_fold()
            pe.wait_ge(sem("act_ready"), FT // 2)
            down = [claim(("down", b, half)) for b in range(NB) for half in range(2)]
            for c in range(6):
                name = ("down", c)
                wait_weights(pe, name)
                nk = 4 if c < 5 else 2
                w = r3(weights(name), nk)
                for k in range(nk):
                    kt = 4 * c + k
                    for b in range(NB):
                        for half in range(2):
                            mm = pe.matmul(down[2 * b + half], act_t[:, kt, b * P:(b + 1) * P], w[:, k, half * 512:(half + 1) * 512],
                                           start=(kt == 0), stop=(kt == FT - 1))
                            if kt == FT - 1:
                                released[name] = publish(mm, ("down", b, half))
                if c < 5:
                    mm.then_inc(sem("down_read"), 1)
                    released[name] = (sem("down_read"), c + 1)
                if c < 4:
                    next_fold()
            for _ in range(2):
                next_fold()
            spread("end1", diag_f)

            def experts(l):
                turn(f"peer_{l}")
                pe.wait_ge(sem("h_ready"), H_READY[f"peer_{l}"])
                for i in range(4):
                    name = ("pq", l, i)
                    wait_weights(pe, name)
                    turned(name, name, HT, r3(weights(name), KT), 512)
                name = ("keys", l)
                wait_weights(pe, name)
                keys = r3(weights(name), SETS)
                pe.wait_ge(sem("stored"), STORED[f"pq_{l}"])
                for b in range(NB):
                    for i in range(0, SETS, 4):
                        t = claim((f"sc_{l}", b, i))
                        for s in range(i, i + 4):
                            mm = pe.matmul(t[:, (s - i) * P:(s - i + 1) * P], pq_t[:, s, b * P:(b + 1) * P], keys[:, s, :],
                                           start=True, stop=True)
                        released[name] = publish(mm, (f"sc_{l}", b, i))
                for b in range(NB):
                    pe.wait_ge(sem("chosen"), 2 * l + b + 1)
                    t = claim((f"slots_{l}", b))
                    for a in range(3):
                        mm = pe.transpose(t[:, a * P:(a + 1) * P], chosen[:, b, a].rearrange("p h k -> p (h k)"), ident)
                    publish(mm, (f"slots_{l}", b))
                for bank in range(8):
                    pe.wait_ge(sem(f"drained{bank}"), (len(tile_no) - 1 - bank) // 8 + 1)

                def gate_products(u, ready, stored):
                    pe.wait_ge(sem("hot"), ready)
                    if stored is not None:
                        pe.wait_ge(sem("gates_stored"), stored)
                    for t in range(GROUP):
                        mm = pe.matmul(ps[:, 6 + u, t * P:(t + 1) * P], hot[:, u, 1, t, :], hot[:, u, 0, t, :],
                                       start=True, stop=True)
                    mm.then_inc(sem("gates_made"), 1)

                for u in range(2):
                    gate_products(u, l * NG + u + 1, None)
                with pe.Fori(1, NG // 2) as i:
                    for u in range(2):
                        gate_products(u, i * 2 + (l * NG + u + 1), i * 2 + (l * NG + u - 1))
                spread(f"g2_{l}", hn_flat)
                pe.wait_ge(sem("g2_row"), l + 1)
                for bank in range(8):
                    pe.wait_ge(sem(f"drained{bank}"), (len(tile_no) - 1 - bank) // 8 + 1)

                def split_product(out_, w, x, first=True, last=True):
                    parts = ((w[0], x[0]), (w[0], x[1]), (w[1], x[0]))
                    for i, (p, q) in enumerate(parts):
                        mm = pe.matmul(out_, p, q, start=(first and i == 0), stop=(last and i == 2))
                    return mm

                def expert_scores(j, ready):
                    pe.wait_ge(sem("expert_u"), ready)
                    for k in range(KT):
                        c = slice(k * P, (k + 1) * P)
                        mm = split_product(ps[:, 4 + j % 2, 0:T], (exp_uh[:, j % 2, c], exp_ul[:, j % E_SLOTS, c]),
                                           (ht_high[:, k, :], ht_low[:, k, :]), k == 0, k == KT - 1)
                    mm.then_inc(sem("expert_scored"), 1)

                def expert_values(j, ready, first=False, last=False):
                    pe.wait_ge(sem("expert_gated"), ready)
                    pe.wait_ge(sem("expert_v"), ready)
                    for b in range(NB):
                        for half in range(2):
                            t, c = slice(b * P, (b + 1) * P), slice(half * 512, (half + 1) * 512)
                            mm = split_product(ps[:, 2 * b + half, :], (act_h[:, j % 2, t], act_l[:, j % 2, t]),
                                               (exp_vh[:, j % 2, c], exp_vl[:, j % E_SLOTS, c]), first, last)
                    mm.then_inc(sem("expert_used"), 1)

                base = l * TILES
                pe.wait_ge(sem("ht_split"), l + 1)
                pe.sem_inc(sem("expert_used"), 1)
                for n in range(2):
                    expert_scores(n, base + n + 1)
                expert_values(0, base + 1, first=True)
                turns = (TILES - 2) // STEP - 1
                with pe.Fori(0, turns) as i:
                    for j in range(1, STEP + 1):
                        expert_scores(j + 1, i * STEP + (base + j + 2))
                        expert_values(j, i * STEP + (base + j + 1))
                for n in range(turns * STEP + 1, TILES):
                    if n + 1 < TILES:
                        expert_scores(n + 1, base + n + 2)
                    expert_values(n, base + n + 1, last=(n == TILES - 1))

            turn("mix_0")
            pe.wait_ge(sem("h_ready"), H_READY["mix_0"])
            wait_weights(pe, ("ev", 0))
            turned(("ev", 0), ("ev", 0), HT, r3(weights(("ev", 0)), KT), 512)
            next_fold()
            for i in (1, 2):
                wait_weights(pe, ("ev", i))
                rows(("ev", i), ("ev", i), HT, r3(weights(("ev", i)), KT), 512)
                next_fold()
            next_fold()
            spread("b_s", diag_2, 4)
            pe.wait_ge(sem("stored"), STORED["ev"])
            wait_weights(pe, ("evs",))
            w = weights(("evs",))
            pe.wait_ge(sem("pool_mat"), 32)
            for g in range(0, 4, 2):
                t = claim(("pool", g))
                for j in range(2):
                    for s in range(NB):
                        mm = pe.matmul(t[:, j * T:(j + 1) * T], pl[:, s, (g + j) * P:(g + j + 1) * P], pool_mat[:, s, g + j, :],
                                       start=(s == 0), stop=(s == NB - 1))
                publish(mm, ("pool", g))
            pe.wait_ge(sem("pooled"), 2)
            for g in range(0, 4, 2):
                t = claim(("mixed", g))
                for j in range(2):
                    mm = pe.matmul(t[:, j * T:(j + 1) * T], w[:, 512 + (g + j) * P:512 + (g + j + 1) * P], pl_t[:, g + j, :],
                                   start=True, stop=True)
                publish(mm, ("mixed", g))
            pe.wait_ge(sem("spatial_in"), 1)
            for b in range(NB):
                t = claim(("spatial", b))
                for g in range(4):
                    mm = pe.matmul(t[:, g * P:(g + 1) * P], vn[:, b, g * P:(g + 1) * P], ws_m[:, g, :], start=True, stop=True)
                released[("evs",)] = publish(mm, ("spatial", b))
            pe.wait_ge(sem("h_ready"), H_READY["even_y"])
            spread("g1_0", hn_flat)
            for i in range(2):
                wait_weights(pe, ("evo", i))
                rows(("evo", i), ("evo", i), HT, r3(weights(("evo", i)), KT), 512)
            experts(0)

            turn("mix_1")
            pe.wait_ge(sem("h_ready"), H_READY["mix_1"])
            for i in range(6):
                wait_weights(pe, ("od", i))
                rows(("od", i), ("od", i), HT, r3(weights(("od", i)), KT), 512)
            for a in range(2):
                pe.wait_ge(sem("roped"), 2 + a)
                turn_heads(("dq_t", "dk_t")[a], dqk[:, a], P, 8)
            pe.wait_ge(sem("heads_turned"), 14)
            pe.wait_ge(sem("stored"), STORED["od"])
            attention(ATT["diff"])
            turn("sub")
            pe.wait_ge(sem("h_ready"), H_READY["sub"])
            spread("g1_1", diag_3)
            for i in range(2):
                wait_weights(pe, ("odo", i))
                rows(("odo", i), ("odo", i), HT, r3(weights(("odo", i)), KT), 512)
            experts(1)
            spread("end2", diag_3)

        @block.scalar
        def _(act):
            own = [0]

            def step(ins):
                own[0] += 1
                ins.then_inc(sem("act_steps"), 1)

            def settle():
                act.wait_ge(sem("act_steps"), own[0])

            def root(name):
                n = NORMS[name]
                for b in range(NB):
                    for i, (lo, hi) in enumerate(n["segs"]):
                        c = n["col"] + b * len(n["segs"]) + i
                        step(act.activation(n["junk"](b)[:, lo:hi], n["src"](b)[:, lo:hi], ACT.Square, accum_out=ss[:, c:c + 1]))
                settle()
                ns = len(n["segs"])
                groups = widths(n["segs"])
                for b in range(NB):
                    for g, (i, j, width) in enumerate(groups):
                        c = n["col"] + b * ns
                        ins = act.activation(rms[:, c + i:c + j], ss[:, c + i:c + j], ACT.Sqrt, bias=vec[:, 58:59] if name == "sub" else eps,
                                             scale=1.0 / width)
                        if b == NB - 1 and g == len(groups) - 1:
                            ins.then_inc(sem("rooted"), 1)

            def store(dst, name, func=ACT.Copy, src=None):
                t = wait_tile(act, name)
                ins = act.activation(dst, t if src is None else src(t), func)
                drained(ins, name)

            def stored(name):
                last = name_of_last[0]
                i = tile_no[last]
                act.wait_ge(sem(f"drained{i % 8}"), i // 8 + 1)
                act.sem_inc(sem("stored"), 1)

            name_of_last = [None]

            def put(dst, name, func=ACT.Copy, src=None):
                store(dst, name, func, src)
                name_of_last[0] = name

            def soft(u):
                k = u["no"] % 2
                act.wait_ge(sem("maxima"), u["no"] + 1)
                for m in range(4):
                    ins = act.activation(u["p"][:, m, :], u["s"][:, m, :], ACT.Exp, bias=mx[:, k, m:m + 1], accum_out=sums[:, k, m:m + 1])
                ins.then_inc(sem("probs"), 1)

            def put_probs(u):
                for half in range(2):
                    put(u["pt"][:, 2 * half:2 * half + 2].rearrange("p m a q -> p (m a q)"), ("pt", u["no"], half))
                i = tile_no[("pt", u["no"], 1)]
                act.wait_ge(sem(f"drained{i % 8}"), i // 8 + 1)
                act.sem_inc(sem("probs_turned"), 1)

            def attention(units):
                for u in units:
                    soft(u)
                    put_probs(u)

            act.wait_ge(sem("made"), 3)
            act.wait_ge(sem("x_loaded"), 16)
            root("mix")
            act.wait_ge(sem("mem_loaded"), 16)
            root("mem")
            act.wait_ge(sem("consts"), 48)
            act.activation(cact[:, :], col("c"), ACT.Silu).then_inc(sem("cact"), 1)
            for b in range(NB):
                put(pa[:, b, :], (("win", 0), b), src=lambda t: t[:, 0:416])
            i = tile_no[(("win", 0), 1)]
            act.wait_ge(sem(f"drained{i % 8}"), i // 8 + 1)
            root("lat")
            for i in range(2):
                put(fqk[:, 2 * i:2 * i + 2].rearrange("p a t -> p (a t)"), (("win", 1), i))
            for b in range(NB):
                put(pc[:, b, :], (("win", 2), b), src=lambda t: t[:, 0:260])
            stored("pc")
            for i in range(2):
                put(cqk[:, 2 * i:2 * i + 2].rearrange("p a t -> p (a t)"), (("win", 3), i))
            for b in range(NB):
                put(pe_[:, b, :], (("win", 4), b), src=lambda t: t[:, 0:256])
            stored("win")
            for b in range(NB):
                put(mq[:, b, :], ("mq", b), src=lambda t: t[:, 0:384])
            for half in range(2):
                for b in range(NB):
                    put(mkv[:, b, half * 384:(half + 1) * 384], ("mkv", half, b), src=lambda t: t[:, 0:384])
            stored("mla")
            for i in range(2):
                put(cross_k[:, 2 * i:2 * i + 2].rearrange("p a t -> p (a t)"), ("ck", i))
            act.wait_ge(sem("forget_in"), 1)
            step(act.activation(fz[:, 2], fz[:, 1], ACT.Exp))
            settle()
            act.activation(fz[:, 3], fz[:, 2], ACT.Ln, bias=unit).then_inc(sem("forget_ln"), 1)
            for name, dst in (("mq_t", mq_t), ("mk_t", mk_t)):
                for b in range(NB):
                    put(dst[0:QK, :, b * P:(b + 1) * P], (name, b, 0), src=lambda t: r3(t[0:QK, :], 4))
                    i = tile_no[(name, b, 0)]
                    act.wait_ge(sem(f"drained{i % 8}"), i // 8 + 1)
                    act.sem_inc(sem("heads_turned"), 1)
            for b in range(NB):
                put(cross_v[:, b, :], ("cv", b))
            stored("cv")
            attention(ATT["self"])
            act.wait_ge(sem("y_ready"), 1)
            root("y")
            act.wait_ge(sem("x_ready"), X_READY["wo"])
            root("cross")
            for i in range(2):
                put(cross_q[:, 2 * i:2 * i + 2].rearrange("p a t -> p (a t)"), ("wcq", i))
            stored("wcq")
            attention(ATT["cross"])
            for b in range(NB):
                put(cross_t[:, :, b * P:(b + 1) * P], ("cross_t", b, 0), src=lambda t: r3(t, 4))
                i = tile_no[("cross_t", b, 0)]
                act.wait_ge(sem(f"drained{i % 8}"), i // 8 + 1)
                act.sem_inc(sem("heads_turned"), 1)
            act.wait_ge(sem("x_ready"), X_READY["wco"])
            root("ffn")
            for i in range(FT // 2):
                if i >= 2:
                    act.wait_ge(sem("act_ready"), i - 1)
                put(silu_g[:, i % 2], (("gu", i), 0), ACT.Silu)
                t = tile_no[(("gu", i), 0)]
                act.wait_ge(sem(f"drained{t % 8}"), t // 8 + 1)
                act.sem_inc(sem("silu"), 1)
            act.wait_ge(sem("x_ready"), X_READY["down"])
            root("end1")

            def experts(l):
                act.wait_ge(sem("x_ready"), X_READY[f"mix_{l}"])
                root(f"peer_{l}")
                for i in range(4):
                    for j in range(2):
                        s = 4 * i + 2 * j
                        put(pq_t[:, s:s + 2].rearrange("p a t -> p (a t)"), (("pq", l, i), j))
                stored(f"pq_{l}")
                for b in range(NB):
                    for i in range(0, SETS, 4):
                        put(sc[:, b, i:i + 4].rearrange("p s n -> p (s n)"), (f"sc_{l}", b, i))
                    stored(f"sc_{l}_{b}")
                for b in range(NB):
                    act.wait_ge(sem("gate_in"), 2 * l + b + 1)
                    act.activation(chosen[:, b, 2], fin_v[:, b], ACT.Exp).then_inc(sem("gate_exp"), 1)
                act.wait_ge(sem("slots"), 2 * l + 2)

                def keep_gates(u, made, at_):
                    act.wait_ge(sem("gates_made"), made)
                    act.activation(arena[:, bass.ds(at_, GROUP * P)], ps[:, 6 + u, :], ACT.Copy).then_inc(sem("gates_stored"), 1)

                with act.Fori(0, NG // 2) as i:
                    for u in range(2):
                        keep_gates(u, i * 2 + (l * NG + u + 1), i * (2 * GROUP * P) + u * GROUP * P)
                for i in range(0, 8, 4):
                    put(g2_row[:, i * P:(i + 4) * P], ("spread", f"g2_{l}", i))
                i = tile_no[("spread", f"g2_{l}", 4)]
                act.wait_ge(sem(f"drained{i % 8}"), i // 8 + 1)
                act.sem_inc(sem("g2_row"), 1)
                with act.Fori(0, TILES // 2) as i:
                    for a in range(2):
                        act.wait_ge(sem("expert_scored"), i * 2 + (l * TILES + a + 1))
                        act.activation(act_e[:, a, :], ps[:, 4 + a, 0:T], ACT.Gelu).then_inc(sem("expert_act"), 1)

            act.wait_ge(sem("x_ready"), X_READY["end1"])
            root("mix_0")
            for i in range(2):
                put(ug_t[:, 2 * i:2 * i + 2].rearrange("p a t -> p (a t)"), (("ev", 0), i), ACT.Gelu)
            for b in range(NB):
                put(vg[:, b, :], (("ev", 1), b), ACT.Gelu)
            stored("vg")
            for b in range(NB):
                put(pl[:, b, :], (("ev", 2), b))
            put(bs_row.rearrange("p a b -> p (a b)"), ("spread", "b_s", 0))
            stored("ev")
            for g in range(0, 4, 2):
                put(pl_t[:, g:g + 2].rearrange("p a t -> p (a t)"), ("pool", g))
                i = tile_no[("pool", g)]
                act.wait_ge(sem(f"drained{i % 8}"), i // 8 + 1)
                act.sem_inc(sem("pooled"), 1)
            act.wait_ge(sem("v_var"), 1)
            act.activation(bn.rearrange("p (b n) -> p b n", b=2)[:, :, 2:3], bn.rearrange("p (b n) -> p b n", b=2)[:, :, 1:2],
                           ACT.Sqrt, bias=eps).then_inc(sem("v_root"), 1)
            for i in range(0, 8, 4):
                put(diag_2[:, i * P:(i + 4) * P], ("spread", "g1_0", i))
            stored("g1_0")
            experts(0)

            act.wait_ge(sem("x_ready"), X_READY["peer_0"])
            root("mix_1")
            for i in range(6):
                for b in range(NB):
                    put(proj[:, b, i * 512:(i + 1) * 512], (("od", i), b))
                if i in (1, 3):
                    stored(f"od{i}")
            stored("od")
            act.wait_ge(sem("angles"), 1)
            act.activation(ang[:, 4], ang[:, 2], ACT.Sin).then_inc(sem("rotation"), 1)
            act.activation(ang[:, 5], ang[:, 3], ACT.Sin).then_inc(sem("rotation"), 1)
            act.wait_ge(sem("lam_in"), 1)
            act.activation(lam2, lam2, ACT.Exp).then_inc(sem("lam_exp"), 1)
            for a, (name, dst) in enumerate((("dq_t", dq_t), ("dk_t", dk_t))):
                for b in range(NB):
                    for h in (0, 4):
                        put(dst[:, h:h + 4, b * P:(b + 1) * P], (name, b, h), src=lambda t: r3(t, 4))
                        i = tile_no[(name, b, h)]
                        act.wait_ge(sem(f"drained{i % 8}"), i // 8 + 1)
                        act.sem_inc(sem("heads_turned"), 1)
            attention(ATT["diff"])
            act.wait_ge(sem("y_ready"), 2)
            root("sub")
            for i in range(0, 8, 4):
                put(rt3.rearrange("p a n -> p (a n)")[:, i * P:(i + 4) * P], ("spread", "g1_1", i))
            stored("g1_1")
            experts(1)
            act.wait_ge(sem("x_ready"), X_READY["peer_1"])
            root("end2")

        @block.vector
        def _(dve):
            own = [0]

            def step(ins):
                own[0] += 1
                ins.then_inc(sem("dve_steps"), 1)

            def settle(but=0):
                if own[0] > but:
                    dve.wait_ge(sem("dve_steps"), own[0] - but)

            def bc(a, n):
                return a.unsqueeze(2).to_broadcast([a.shape[0], a.shape[1], n])

            def scale(name):
                n = NORMS[name]
                dve.wait_ge(sem("rooted"), n["no"] + 1)
                a, b_ = n["col"], n["col"] + 2 * len(n["segs"])
                r = rstd[:, a:b_]
                step(dve.reciprocal(r, rms[:, a:b_]))
                mean, sq = newton[:, 0:b_ - a], newton[:, 16:16 + b_ - a]
                e = EPS * SUB * SUB if name == "sub" else EPS
                ns = len(n["segs"])
                for b in range(NB):
                    for i, j, width in widths(n["segs"]):
                        step(dve.tensor_scalar(mean[:, b * ns + i:b * ns + j], ss[:, a + b * ns + i:a + b * ns + j], 1.0 / width, e, ALU.mult, ALU.add))
                settle()
                step(dve.tensor_tensor(sq, r, r, ALU.mult))
                settle()
                step(dve.tensor_tensor(sq, sq, mean, ALU.mult))
                settle()
                step(dve.tensor_scalar(sq, sq, -0.5, 1.5, ALU.mult, ALU.add))
                settle()
                step(dve.tensor_tensor(r, r, sq, ALU.mult))
                settle()
                if name == "sub":
                    step(dve.scalar_tensor_tensor(out=rstd[:, a:b_], in0=ss[:, a:b_], scalar=SUM_MAX, in1=rstd[:, a:b_], op0=ALU.is_le, op1=ALU.mult))
                    settle()
                for b in range(NB):
                    for i, (lo, hi) in enumerate(n["segs"]):
                        c = n["col"] + b * len(n["segs"]) + i
                        ins = dve.tensor_scalar(n["dst"](b)[:, lo:hi], n["src"](b)[:, lo:hi], rstd[:, c:c + 1], None, ALU.mult)
                        if b == NB - 1 and i == len(n["segs"]) - 1:
                            ins.then_inc(sem("normed"), 1)
                        else:
                            step(ins)

            def gain(name, dst, g, shift=None, nk=KT):
                ins = None
                for b in range(NB):
                    for i in range(0, nk, 4):
                        j = min(i + 4, nk)
                        t = wait_tile(dve, (name, b, i))
                        part = dst[:, i:j, b * P:(b + 1) * P]
                        ins = dve.tensor_tensor(part, r3(t[:, 0:(j - i) * P], j - i), bc(g[:, i:j], P), ALU.mult)
                        drained(ins, (name, b, i))
                wait_own_tile((name, b, i))
                if shift is not None:
                    for b in range(NB):
                        part = dst[:, :, b * P:(b + 1) * P]
                        step(dve.tensor_tensor(part, part, bc(shift, P), ALU.add))
                    settle()
                dve.sem_inc(sem("h_ready"), 1)

            def wait_own_tile(name):
                i = tile_no[name]
                dve.wait_ge(sem(f"drained{i % 8}"), i // 8 + 1)

            def add_to_x(tiles, row=None):
                for (b, half), name in tiles:
                    t = wait_tile(dve, name)
                    part = X[:, b, half * 512:(half + 1) * 512]
                    if row is None:
                        drained(dve.tensor_tensor(part, part, t, ALU.add), name)
                    else:
                        tmp = hn_flat[:, (2 * b + half) * 512:(2 * b + half + 1) * 512]
                        drained(dve.tensor_tensor(tmp, t, row[:, half * 512:(half + 1) * 512], ALU.mult), name)
                        wait_own_tile(name)
                        step(dve.tensor_tensor(part, part, tmp, ALU.add))
                wait_own_tile(name)
                settle()
                dve.sem_inc(sem("x_ready"), 1)

            def soft(u):
                k = u["no"] % 2
                for half in range(2):
                    t = wait_tile(dve, ("s", u["no"], half))
                    dst = u["s"][:, 2 * half:2 * half + 2, :]
                    if u["mask"] is None:
                        ins = dve.tensor_scalar(dst, r3(t, 2), u["scale"], None, ALU.mult)
                    else:
                        if isinstance(u["mask"], str):
                            mask = relb[:, u["b"], half::2, :]
                        else:
                            mask = u["mask"][:, u["b"], :].unsqueeze(1).to_broadcast([P, 2, T])
                        ins = dve.scalar_tensor_tensor(out=dst, in0=r3(t, 2), scalar=u["scale"], in1=mask, op0=ALU.mult, op1=ALU.add)
                    drained(ins, ("s", u["no"], half))
                wait_own_tile(("s", u["no"], 1))
                dve.tensor_reduce(mx[:, k, :], u["s"], AX, ALU.max, negate=True).then_inc(sem("maxima"), 1)

            def weigh(u):
                k = u["no"] % 2
                dve.wait_ge(sem("probs"), u["no"] + 1)
                step(dve.reciprocal(rinv[:, k, :], sums[:, k, :]))
                settle()
                w = rinv[:, k, :]
                if u["kind"] == "diff":
                    step(dve.tensor_tensor(wcoef[:, k, :], w, coef, ALU.mult))
                    settle()
                    w = wcoef[:, k, :]
                t = wait_tile(dve, ("o", u["no"]))
                n = 4 * u["dv"]
                if u["kind"] in ("fox", "chk"):
                    dst = u["out"].rearrange("p (a b n) -> p b a n", a=2, b=2)
                    src = t[:, 0:n].rearrange("p (b a n) -> p b a n", a=2, b=2)
                    w = w.rearrange("p (b a) -> p b a", b=2).unsqueeze(3).to_broadcast([P, 2, 2, u["dv"]])
                else:
                    dst = r3(u["out"] if u["kind"] != "diff" else dtmp[:, k, :], 4)
                    src, w = r3(t[:, 0:n], 4), bc(w, u["dv"])
                drained(dve.tensor_tensor(dst, src, w, ALU.mult), ("o", u["no"]))
                if u["kind"] == "diff":
                    wait_own_tile(("o", u["no"]))
                    pair = dtmp[:, k, :].rearrange("p (m h n) -> p h m n", h=2, m=2)
                    step(dve.tensor_tensor(r3(u["out"], 2), pair[:, :, 0, :], pair[:, :, 1, :], ALU.add))

            def attention(units):
                soft(units[0])
                for i, u in enumerate(units):
                    if i + 1 < len(units):
                        soft(units[i + 1])
                    weigh(u)
                wait_own_tile(("o", units[-1]["no"]))
                settle()

            ada_sum = [(l, j) for l in range(2) for j in range(12)]
            ada_put = list(ada_sum)

            def modulation_sum():
                l, j = ada_sum.pop(0)
                i = 12 * l + j
                name = ("ada", l, j)
                if i == 0:
                    dve.wait_ge(sem("cact"), 1)
                wait_weights(dve, name)
                w = r3(weights(name), KT)
                acc = acc_ada[:, i % 4]
                for k in range(KT):
                    for h in range(2):
                        part, wk = acc[:, h * 256:(h + 1) * 256], w[:, k, h * 256:(h + 1) * 256]
                        if k == 0:
                            ins = dve.tensor_scalar(part, wk, cact[:, 0:1], None, ALU.mult)
                        else:
                            settle(1)
                            ins = dve.scalar_tensor_tensor(out=part, in0=wk, scalar=cact[:, k:k + 1], in1=part, op0=ALU.mult, op1=ALU.add)
                        step(ins)
                settle()
                dve.sem_inc(sem("ada_summed"), 1)
                released[name] = (sem("ada_summed"), i + 1)

            def modulation_put():
                l, j = ada_put.pop(0)
                name = ("ada", l, j)
                t = wait_tile(dve, name)
                at_ = 48 * l + 4 * j
                drained(dve.tensor_tensor(MOD[:, at_:at_ + 4], t[:, 0:4], col("ada_b", at_, 4), ALU.add), name)
                return name

            def mod(l, i):
                return MOD[:, 48 * l + 8 * i:48 * l + 8 * i + 8]

            def mod_gain(g, l, i):
                step(dve.scalar_tensor_tensor(out=vec[:, 16 * l + 8 * (i > 1):16 * l + 8 * (i > 1) + 8], in0=mod(l, i), scalar=1.0,
                                              in1=g, op0=ALU.add, op1=ALU.mult))
                settle()
                return vec[:, 16 * l + 8 * (i > 1):16 * l + 8 * (i > 1) + 8]

            def diagonal(name, dst, v, n=8):
                settle()
                dve.tensor_tensor(r3(dst[:, 0:n * P], n), ident.unsqueeze(1).to_broadcast([P, n, P]), bc(v, P), ALU.mult)\
                   .then_inc(sem("diag"), 1)

            def rotate(dst1, dst2, x1, x2, c, s, tmp):
                settle()
                for i, (x, y) in enumerate(((x1, c), (x2, s), (x1, s), (x2, c))):
                    step(dve.tensor_tensor(tmp[i], x, y, ALU.mult))
                settle()
                step(dve.tensor_tensor(dst1, tmp[0], tmp[1], ALU.subtract))
                step(dve.tensor_tensor(dst2, tmp[2], tmp[3], ALU.add))

            dve.memset(ones, 1.0).then_inc(sem("made"), 1)
            dve.memset(eps, EPS).then_inc(sem("made"), 1)
            dve.memset(unit, 1.0).then_inc(sem("made"), 1)
            dve.wait_ge(sem("consts"), 48)
            scale("mix")
            gain("mix", HT, col("norm_mix"))
            dve.wait_ge(sem("masks"), 64)
            for h in range(4):
                step(dve.tensor_tensor(relb[:, :, h, :], relb[:, :, h, :], chunked, ALU.add))
            scale("mem")
            scale("lat")
            lat_g = cols[:, COLS["q_norm"][0]:COLS["q_norm"][0] + 3]
            gain("lat", lat_t, lat_g, nk=3)
            gain("mem", mem_t, col("norm_mem"))
            dve.wait_ge(sem("stored"), STORED["pc"])
            step(dve.tensor_tensor(fz[:, 0], pc[:, :, 256:260], col("f_bias").unsqueeze(1).to_broadcast([P, NB, 4]), ALU.add))
            settle()
            step(dve.tensor_scalar(fz[:, 2], fz[:, 0], -1.0, None, ALU.mult))
            settle()
            step(dve.tensor_tensor(fz[:, 1], fz[:, 0], fz[:, 2], ALU.min))
            settle()
            dve.sem_inc(sem("forget_in"), 1)
            dve.wait_ge(sem("stored"), STORED["mla"])
            for b in range(NB):
                q = mq[:, b, :].rearrange("p (h n) -> p h n", h=4)
                c = rot[:, b, 0:16].unsqueeze(1).to_broadcast([P, 4, 16])
                s = rot[:, b, 16:32].unsqueeze(1).to_broadcast([P, 4, 16])
                tmp = [r3(rtmp[:, i, :], 4) for i in range(4)]
                rotate(q[:, :, 64:80], q[:, :, 80:96], q[:, :, 64:80], q[:, :, 80:96], c, s, tmp)
                k = mk[:, b, :].rearrange("p (h n) -> p h n", h=4)
                kv = mkv[:, b, :].rearrange("p (h n) -> p h n", h=4)
                step(dve.tensor_copy(k[:, :, 0:64], kv[:, :, 0:64]))
                tmp = [rtmp[:, i, 0:16] for i in range(4)]
                rotate(k[:, 0, 64:80], k[:, 0, 80:96], pa[:, b, 384:400], pa[:, b, 400:416], rot[:, b, 0:16], rot[:, b, 16:32], tmp)
                settle()
                for h in range(1, 4):
                    step(dve.tensor_copy(k[:, h, 64:96], k[:, 0, 64:96]))
            settle()
            dve.sem_inc(sem("roped"), 1)
            dve.wait_ge(sem("forget_ln"), 1)
            step(dve.scalar_tensor_tensor(out=fz[:, 1], in0=fz[:, 0], scalar=0.0, in1=fz[:, 3], op0=ALU.min, op1=ALU.subtract))
            settle()
            for b in range(NB):
                step(dve.tensor_scalar(flb[:, b], bc(fz[:, 1, b, :], T), 8.0, None, ALU.mult))
                step(dve.tensor_scalar(nfl[:, b], bc(fz[:, 1, b, :], P), -8.0, None, ALU.mult))
            settle()
            dve.sem_inc(sem("forget"), 1)
            modulation_sum()
            attention(ATT["self"])
            dve.sem_inc(sem("y_ready"), 1)
            scale("y")
            gain("y", HT, col("out_norm"))
            add_to_x([((b, i), (("wo", i), b)) for i in range(2) for b in range(NB)])
            modulation_put()
            scale("cross")
            modulation_sum()
            gain("cross", HT, col("norm_cross"))
            modulation_sum()
            modulation_put()
            attention(ATT["cross"])
            dve.sem_inc(sem("cross_out"), 1)
            modulation_sum()
            modulation_put()
            add_to_x([((b, half), ("wco", b, half)) for b in range(NB) for half in range(2)])
            scale("ffn")
            gain("ffn", HT, col("norm_ffn"))
            for i in range(FT // 2):
                dve.wait_ge(sem("silu"), i + 1)
                t = wait_tile(dve, (("gu", i), 1))
                ins = dve.tensor_tensor(act_t[:, 2 * i:2 * i + 2, :], r3(silu_g[:, i % 2], 2), r3(t, 2), ALU.mult)
                drained(ins, (("gu", i), 1))
                wait_own_tile((("gu", i), 1))
                dve.sem_inc(sem("act_ready"), 1)
                modulation_sum()
                modulation_put()
            for c in range(6):
                modulation_sum()
                if c < 4:
                    modulation_put()
            add_to_x([((b, half), ("down", b, half)) for b in range(NB) for half in range(2)])
            for _ in range(2):
                modulation_put()
            diagonal("end1", diag_f, col("final_norm"))
            scale("end1")

            def end_rows(name, dst):
                dve.wait_ge(sem("normed"), NORMS[name]["no"] + 1)
                for half in range(2):
                    t = wait_tile(dve, ("spread", name, 4 * half))
                    for b in range(NB):
                        ins = dve.tensor_tensor(dst[:, b, half * 512:(half + 1) * 512], HN[:, b, half * 512:(half + 1) * 512], t, ALU.mult)
                        if b == NB - 1:
                            drained(ins, ("spread", name, 4 * half))
                        else:
                            step(ins)
                settle()
                wait_own_tile(("spread", name, 4))
                dve.sem_inc(sem("x_ready"), 1)

            end_rows("end1", X)

            def experts(l):
                scale(f"peer_{l}")
                g = mod_gain(col("norm_ffn_2", 8 * l, 8), l, 4)
                gain(f"peer_{l}", HT, g, mod(l, 3))
                for s in range(SETS):
                    if s == 0:
                        dve.wait_ge(sem("stored"), STORED[f"sc_{l}_1"])
                    lo, hi = slice(0, 8), slice(8, 16)
                    for b in range(NB):
                        settle(1)
                        step(dve.max(top_v[:, b, s, lo], sc[:, b, s, :]))
                    for b in range(NB):
                        settle(1)
                        step(dve.max_index(top_i[:, b, s, lo], top_v[:, b, s, lo], sc[:, b, s, :]))
                    for b in range(NB):
                        settle(1)
                        step(dve.match_replace(sw[:, b, s, :], top_v[:, b, s, lo], sc[:, b, s, :], 4 * NEG))
                    for b in range(NB):
                        settle(1)
                        step(dve.max(top_v[:, b, s, hi], sw[:, b, s, :]))
                    for b in range(NB):
                        settle(1)
                        step(dve.max_index(top_i[:, b, s, hi], top_v[:, b, s, hi], sw[:, b, s, :]))
                settle()
                for b in range(NB):
                    pair = top_v[:, b].rearrange("p (h a) k -> p h a k", a=2)
                    step(dve.tensor_copy(top_f[:, b], top_i[:, b]))
                    step(dve.tensor_tensor(cand[:, b].rearrange("p h (i j) -> p h i j", i=TOPK),
                                           pair[:, :, 0, :].unsqueeze(3).to_broadcast([P, 8, TOPK, TOPK]),
                                           pair[:, :, 1, :].unsqueeze(2).to_broadcast([P, 8, TOPK, TOPK]), ALU.add))
                for h in range(HEADS8):
                    lo, hi = slice(0, 8), slice(8, 16)
                    for b in range(NB):
                        settle(1)
                        step(dve.max(fin_v[:, b, h, lo], cand[:, b, h, :]))
                    for b in range(NB):
                        settle(1)
                        step(dve.max_index(fin_p[:, b, h, lo], fin_v[:, b, h, lo], cand[:, b, h, :]))
                    for b in range(NB):
                        settle(1)
                        step(dve.match_replace(cw[:, b, h, :], fin_v[:, b, h, lo], cand[:, b, h, :], 4 * NEG))
                    for b in range(NB):
                        settle(1)
                        step(dve.max(fin_v[:, b, h, hi], cw[:, b, h, :]))
                    for b in range(NB):
                        settle(1)
                        step(dve.max_index(fin_p[:, b, h, hi], fin_v[:, b, h, hi], cw[:, b, h, :]))
                settle()
                step(dve.tensor_scalar(fin_ij[:, 0], fin_p, 4, None, ALU.logical_shift_right))
                step(dve.tensor_scalar(fin_ij[:, 1], fin_p, 15, None, ALU.bitwise_and))
                settle()
                step(dve.tensor_copy(fin_f, fin_ij))
                settle()
                for b in range(NB):
                    keys = top_f[:, b].rearrange("p (h a) k -> p h a k", a=2)
                    for a in range(2):
                        e = eq[:, a].rearrange("p (s n) -> p s n", n=TOPK)
                        step(dve.tensor_tensor(e, iota[:, 0:TOPK].unsqueeze(1).to_broadcast([P, P, TOPK]),
                                               bc(fin_f[:, a, b].rearrange("p h k -> p (h k)"), TOPK), ALU.is_equal))
                    for a in range(2):
                        e = eq[:, a].rearrange("p (h k n) -> p h k n", h=8, k=TOPK)
                        settle(1)
                        step(dve.tensor_tensor(e, e, keys[:, :, a, :].unsqueeze(2).to_broadcast([P, 8, TOPK, TOPK]), ALU.mult))
                    for a in range(2):
                        settle(1)
                        step(dve.tensor_reduce(chosen[:, b, a].rearrange("p h k -> p (h k)"),
                                               eq[:, a].rearrange("p (s n) -> p s n", n=TOPK), AX, ALU.add))
                    step(dve.tensor_copy(gsum[:, b, 0], fin_v[:, b, :, 0]))
                    settle()
                    step(dve.tensor_tensor(fin_v[:, b], fin_v[:, b], bc(gsum[:, b, 0], TOPK), ALU.subtract))
                    settle()
                    dve.sem_inc(sem("gate_in"), 1)
                for b in range(NB):
                    dve.wait_ge(sem("gate_exp"), 2 * l + b + 1)
                    step(dve.tensor_reduce(gsum[:, b, 1], chosen[:, b, 2], AX, ALU.add))
                    settle()
                    step(dve.reciprocal(gsum[:, b, 0], gsum[:, b, 1]))
                    settle()
                    step(dve.tensor_tensor(chosen[:, b, 2], chosen[:, b, 2], bc(gsum[:, b, 0], TOPK), ALU.mult))
                    settle()
                    dve.sem_inc(sem("chosen"), 1)
                for b in range(NB):
                    t = wait_tile(dve, (f"slots_{l}", b))
                    drained(dve.tensor_copy(slots_t[:, :, b * P:(b + 1) * P], r3(t[:, 0:3 * P], 3)), (f"slots_{l}", b))
                    wait_own_tile((f"slots_{l}", b))
                    dve.sem_inc(sem("slots"), 1)

                def one_hots(u, at_):
                    for t in range(GROUP):
                        dve.tensor_scalar(hot[:, u, 0, t, :], iota, slots_t[:, 0, bass.ds(at_ + t, 1)], None, ALU.is_equal)
                        ins = dve.tensor_scalar(hot[:, u, 1, t, :], iota, slots_t[:, 1, bass.ds(at_ + t, 1)],
                                                slots_t[:, 2, bass.ds(at_ + t, 1)], ALU.is_equal, ALU.mult)
                    ins.then_inc(sem("hot"), 1)

                for u in range(2):
                    one_hots(u, u * GROUP)
                with dve.Fori(1, NG // 2) as i:
                    for u in range(2):
                        dve.wait_ge(sem("gates_made"), i * 2 + (l * NG + u - 1))
                        one_hots(u, i * (2 * GROUP) + u * GROUP)
                dve.wait_ge(sem("gates_stored"), (l + 1) * NG)
                diagonal(f"g2_{l}", hn_flat, mod(l, 5))
                def high(dst, src):
                    return dve.tensor_copy(dst, src)

                def low(dst, src, h):
                    return dve.tensor_tensor(dst, src, h.bitcast(F32), ALU.subtract)

                def arrived(kind, n, turn=None):
                    s = n % E_SLOTS
                    count = 16 * (l * len(range(s, TILES, E_SLOTS)) + n // E_SLOTS + 1)
                    dve.wait_ge(sem(f"expert_{kind}{s}_arrived"), count if turn is None else turn * (16 * STEP // E_SLOTS) + count)

                settle()
                step(high(ht_high, HT))
                settle()
                low(ht_low, HT, ht_high).then_inc(sem("ht_split"), 1)
                for n in range(2):
                    arrived("u", n)
                    step(high(exp_uh[:, n], exp_u[:, n]))
                    settle()
                    low(exp_ul[:, n], exp_u[:, n], exp_uh[:, n]).then_inc(sem("expert_u"), 1)
                arrived("v", 0)
                step(high(exp_vh[:, 0], exp_v[:, 0]))
                settle()
                low(exp_vl[:, 0], exp_v[:, 0], exp_vh[:, 0]).then_inc(sem("expert_v"), 1)

                def expert(j, turn=None, more_u=True, more_v=True):
                    def at_(n, each=1):
                        return n if turn is None else turn * (STEP * each) + n

                    n = at_(j)
                    done = split_base + 4 * j
                    dve.wait_ge(sem("expert_act"), at_(l * TILES + j + 1))
                    g = gates[:, :, bass.ds(n, 1)].rearrange("p t o -> p (t o)") if turn is not None else gates[:, :, j]
                    dve.tensor_tensor(act_e[:, j % 2], act_e[:, j % 2], g, ALU.mult).then_inc(sem("split_steps"), 1)
                    if more_u:
                        u, ul, uh = exp_u[:, (j + 2) % E_SLOTS], exp_ul[:, (j + 2) % E_SLOTS], exp_uh[:, j % 2]
                        arrived("u", j + 2, turn)
                        high(uh, u).then_inc(sem("split_steps"), 1)
                    dve.wait_ge(sem("split_steps"), at_(done + 1, 4))
                    high(act_h[:, j % 2], act_e[:, j % 2]).then_inc(sem("split_steps"), 1)
                    if more_u:
                        dve.wait_ge(sem("split_steps"), at_(done + 2, 4))
                        low(ul, u, uh).then_inc(sem("expert_u"), 1)
                    dve.wait_ge(sem("split_steps"), at_(done + 2 + more_u, 4))
                    low(act_l[:, j % 2], act_e[:, j % 2], act_h[:, j % 2]).then_inc(sem("expert_gated"), 1)
                    if more_v:
                        v, vl, vh = exp_v[:, (j + 1) % E_SLOTS], exp_vl[:, (j + 1) % E_SLOTS], exp_vh[:, (j + 1) % 2]
                        arrived("v", j + 1, turn)
                        dve.wait_ge(sem("expert_used"), at_(l * (TILES + 1) + j + 1))
                        high(vh, v).then_inc(sem("split_steps"), 1)
                        dve.wait_ge(sem("split_steps"), at_(done + 3 + more_u, 4))
                        low(vl, v, vh).then_inc(sem("expert_v"), 1)

                split_base = l * (4 * TILES - 3)
                with dve.Fori(0, (TILES - 2) // STEP) as i:
                    for j in range(STEP):
                        expert(j, i)
                expert(TILES - 2, more_u=False)
                split_base -= 1
                expert(TILES - 1, more_u=False, more_v=False)
                dve.wait_ge(sem("expert_used"), (l + 1) * (TILES + 1))
                for b in range(NB):
                    for half in range(2):
                        tmp = hn_flat[:, half * 512:(half + 1) * 512]
                        settle()
                        step(dve.tensor_tensor(tmp, ps[:, 2 * b + half, :], g2_row[:, half * 512:(half + 1) * 512], ALU.mult))
                        settle()
                        part = X[:, b, half * 512:(half + 1) * 512]
                        step(dve.tensor_tensor(part, part, tmp, ALU.add))
                settle()
                dve.sem_inc(sem("x_ready"), 1)

            scale("mix_0")
            g = mod_gain(col("norm_mix_2", 0, 8), 0, 1)
            gain("mix_0", HT, g, mod(0, 0))
            for i in range(3):
                modulation_sum()
                modulation_put()
            modulation_put()
            diagonal("b_s", diag_2, col("b_s"), 4)
            dve.wait_ge(sem("pool_mat"), 32)
            wait_weights(dve, ("evs",))
            w = weights(("evs",))
            step(dve.tensor_tensor(ws_m, r3(w[:, 0:512], 4), tri_2.unsqueeze(1).to_broadcast([P, 4, P]), ALU.mult))
            dve.wait_ge(sem("stored"), STORED["vg"])
            bnv = bn.rearrange("p (b n) -> p b n", b=2)
            for b in range(NB):
                settle()
                step(dve.bn_stats(vec[:, 48:54], vg[:, b, :]))
                settle()
                step(dve.bn_aggr(bnv[:, b, 0:2], vec[:, 48:54]))
            settle()
            dve.sem_inc(sem("v_var"), 1)
            dve.wait_ge(sem("v_root"), 1)
            step(dve.reciprocal(bnv[:, :, 3:4], bnv[:, :, 2:3]))
            settle()
            for b in range(NB):
                step(dve.tensor_scalar(vn[:, b, :], vg[:, b, :], bnv[:, b, 0:1], bnv[:, b, 3:4], ALU.subtract, ALU.mult))
            settle()
            dve.sem_inc(sem("spatial_in"), 1)
            for g in range(0, 4, 2):
                t = wait_tile(dve, ("mixed", g))
                drained(dve.tensor_tensor(HT[:, 4 + g:6 + g, :], r3(t, 2), bc(col("pool_scale", g, 2), T), ALU.mult), ("mixed", g))
            dve.wait_ge(sem("stored"), STORED["ev"])
            for b in range(NB):
                part = HT[:, 0:4, b * P:(b + 1) * P]
                t = wait_tile(dve, ("spatial", b))
                drained(dve.tensor_tensor(part, r3(t, 4), bc(col("g_v"), P), ALU.mult), ("spatial", b))
                wait_own_tile(("spatial", b))
                step(dve.tensor_tensor(part, part, bs_row, ALU.add))
                settle()
                step(dve.tensor_tensor(part, part, ug_t[:, :, b * P:(b + 1) * P], ALU.mult))
            settle()
            dve.sem_inc(sem("h_ready"), 1)
            diagonal("g1_0", hn_flat, mod(0, 2))
            dve.wait_ge(sem("stored"), STORED["g1_0"])
            add_to_x([((b, i), (("evo", i), b)) for i in range(2) for b in range(NB)], diag_2)
            experts(0)

            dve.wait_ge(sem("consts3"), 48)
            step(dve.tensor_copy(posf, pos_i[:, :]))
            settle()
            for b in range(NB):
                step(dve.tensor_scalar(ang[:, 0, b, :], inv_f, posf[:, b:b + 1], None, ALU.mult))
            settle()
            magic, two_pi = 12582912.0, 2 * np.pi
            p1 = 6.28125
            p2 = 0.001934051513671875
            p3 = two_pi - p1 - p2
            step(dve.tensor_scalar(ang[:, 1], ang[:, 0], float(1 / two_pi), magic, ALU.mult, ALU.add))
            settle()
            step(dve.tensor_scalar(ang[:, 1], ang[:, 1], magic, None, ALU.subtract))
            settle()
            for p in (p1, p2, p3):
                step(dve.scalar_tensor_tensor(out=ang[:, 0], in0=ang[:, 1], scalar=-float(p), in1=ang[:, 0], op0=ALU.mult, op1=ALU.add))
                settle()
            lim = 3.1415925
            step(dve.tensor_scalar(ang[:, 2], ang[:, 0], lim, -lim, ALU.min, ALU.max))
            step(dve.tensor_scalar(ang[:, 3], ang[:, 0], float(np.pi / 2), None, ALU.add))
            settle()
            step(dve.tensor_scalar(ang[:, 1], ang[:, 3], float(np.pi), -float(two_pi), ALU.is_gt, ALU.mult))
            settle()
            step(dve.tensor_tensor(ang[:, 3], ang[:, 3], ang[:, 1], ALU.add))
            settle()
            step(dve.tensor_scalar(ang[:, 3], ang[:, 3], lim, -lim, ALU.min, ALU.max))
            settle()
            dve.sem_inc(sem("angles"), 1)
            for i in range(2):
                step(dve.tensor_tensor(lam_p[:, i, :], lam_in[:, 2 * i, :], lam_in[:, 2 * i + 1, :], ALU.mult))
            settle()
            step(dve.tensor_reduce(lam2, lam_p, AX, ALU.add))
            settle()
            dve.sem_inc(sem("lam_in"), 1)
            step(dve.memset(coef, 1.0))
            step(dve.memset(vec[:, 58:59], EPS * SUB * SUB))
            step(dve.tensor_scalar(vec[:, 56:57], col("g_sub"), 1.0 - LAM_INIT, None, ALU.mult))
            scale("mix_1")
            g = mod_gain(col("norm_mix_2", 8, 8), 1, 1)
            gain("mix_1", HT, g, mod(1, 0))
            dve.wait_ge(sem("lam_exp"), 1)
            step(dve.tensor_tensor(vec[:, 57:58], lam2[:, 1:2], lam2[:, 0:1], ALU.subtract))
            settle()
            for i in (2, 3):
                step(dve.tensor_scalar(coef[:, i:i + 1], vec[:, 57:58], LAM_INIT, None, ALU.subtract))
            dve.wait_ge(sem("rotation"), 2)
            for a in range(2):
                dve.wait_ge(sem("stored"), STORED[f"od{2 * a + 1}"])
                for b in range(NB):
                    x = proj[:, b, a * D:(a + 1) * D].rearrange("p (m n) -> p m n", m=16)
                    y = dqk[:, a, b, :].rearrange("p (m n) -> p m n", m=16)
                    c = ang[:, 5, b, :].unsqueeze(1).to_broadcast([P, 16, 32])
                    s = ang[:, 4, b, :].unsqueeze(1).to_broadcast([P, 16, 32])
                    rotate(y[:, :, 0:32], y[:, :, 32:64], x[:, :, 0:32], x[:, :, 32:64], c, s, [r3(rt3[:, i, :], 16) for i in range(4)])
                settle()
                dve.sem_inc(sem("roped"), 1)
            attention(ATT["diff"])
            step(dve.tensor_scalar(do, do, SUB, SUB_MAX, ALU.mult, ALU.min))
            settle()
            step(dve.tensor_scalar(do, do, -SUB_MAX, None, ALU.max))
            settle()
            dve.sem_inc(sem("y_ready"), 1)
            scale("sub")
            gain("sub", HT, vec[:, 56:57].to_broadcast([P, 8]))
            diagonal("g1_1", diag_3, mod(1, 2))
            dve.wait_ge(sem("stored"), STORED["g1_1"])
            add_to_x([((b, i), (("odo", i), b)) for i in range(2) for b in range(NB)], rt3.rearrange("p a n -> p (a n)"))
            experts(1)
            diagonal("end2", diag_3, col("final_norm_2"))
            scale("end2")
            end_rows("end2", HN)

        @block.sync
        def _(sp):
            sp.dma_start(X.rearrange("p b n -> p (b n)"), d["x"]).then_inc(sem("x_loaded"), 16)
            sp.dma_start(cols[:, :], d["cols"]).then_inc(sem("consts"), 16)
            sp.dma_start(ident, d["perm"][:, 0:P]).then_inc(sem("consts"), 16)
            sp.dma_start(iota, d["perm"][:, P:2 * P]).then_inc(sem("consts"), 16)

            def load(i):
                name = STREAM[i]
                if i >= SLOTS:
                    s, v = released[STREAM[i - SLOTS]]
                    sp.wait_ge(s, v)
                sp.dma_start(weights(name), d["stream"][i, :, 0:SIZE.get(name, SLOT)]).then_inc(sem(f"arrived{i % SLOTS}"), 16)

            def load_experts(l):
                for j in range(SLOTS):
                    i = chunk_no[("keys", l)] - j
                    s, v = released[STREAM[i]]
                    sp.wait_ge(s, v)
                base = l * TILES

                def fetch(s, src_u, src_v, scored=None, used=None):
                    if scored is not None:
                        sp.wait_ge(sem("expert_scored"), scored)
                    sp.dma_start(exp_u[:, s, :], src_u).then_inc(sem(f"expert_u{s}_arrived"), 16)
                    if used is not None:
                        sp.wait_ge(sem("expert_used"), used)
                    sp.dma_start(exp_v[:, s, :], src_v).then_inc(sem(f"expert_v{s}_arrived"), 16)

                u, v = d["experts_u"][l], d["experts_v"][l]
                for n in range(E_SLOTS):
                    fetch(n, u[n], v[n])
                turns = (TILES - E_SLOTS) // E_SLOTS
                with sp.Fori(0, turns) as i:
                    for s in range(E_SLOTS):
                        at_ = bass.ds(i * E_SLOTS + (E_SLOTS + s), 1)
                        fetch(s, u[at_].rearrange("o p n -> (o p) n"), v[at_].rearrange("o p n -> (o p) n"),
                              i * E_SLOTS + (base + s + 1), i * E_SLOTS + (base + l + s + 2))
                for n in range((turns + 1) * E_SLOTS, TILES):
                    fetch(n % E_SLOTS, u[n], v[n], base + n - 2, base + l + n - 1)
                sp.wait_ge(sem("expert_used"), (l + 1) * (TILES + 1))

            load(0)
            sp.dma_start(mem.rearrange("p b n -> p (b n)"), d["mem"]).then_inc(sem("mem_loaded"), 16)
            load(1)
            sp.dma_start(arena[:, 0:3 * 2 * T], d["masks"]).then_inc(sem("masks"), 16)
            sp.dma_start(rot.rearrange("p b n -> p (b n)"), d["rot"]).then_inc(sem("masks"), 16)
            sp.dma_start(relb.rearrange("p b h k -> p (b h k)"), d["rel"]).then_inc(sem("masks"), 16)
            sp.dma_start(pos_i[:, :], d["pos"]).then_inc(sem("masks"), 16)
            for i in range(2, len(STREAM)):
                name = STREAM[i]
                if name == ("evs",):
                    sp.wait_ge(sem("x_ready"), X_READY["end1"])
                    sp.dma_start(pool_mat.rearrange("p s g t -> p (s g t)"), d["pool"]).then_inc(sem("pool_mat"), 16)
                    sp.dma_start(tri_2, d["masks"][:, 4 * T:4 * T + P]).then_inc(sem("pool_mat"), 16)
                load(i)
                if name[0] == "keys":
                    load_experts(name[1])
                if name == ("keys", 0):
                    sp.dma_start(causal_3.rearrange("p b k -> p (b k)"), d["masks"][:, 0:2 * T]).then_inc(sem("consts3"), 16)
                    sp.dma_start(inv_f, d["inv_f"]).then_inc(sem("consts3"), 16)
                    sp.dma_start(lam_in.rearrange("p a n -> p (a n)"), d["lam"]).then_inc(sem("consts3"), 16)
            sp.wait_ge(sem("x_ready"), X_READY["end2"])
            for b in range(NB):
                sp.dma_start(out[0, b * P:(b + 1) * P, :], HN[:, b, :]).then_inc(sem("written"), 16)
            sp.wait_ge(sem("written"), 16 * NB)


H_READY = {n: i + 1 for i, n in enumerate(("mix", "lat", "mem", "y", "cross", "ffn", "mix_0", "even_y", "peer_0", "mix_1", "sub", "peer_1"))}
X_READY = {n: i + 1 for i, n in enumerate(("wo", "wco", "down", "end1", "mix_0", "peer_0", "mix_1", "peer_1", "end2"))}
STORED = {n: i + 1 for i, n in enumerate(("pc", "win", "mla", "cv", "wcq", "vg", "ev", "g1_0", "pq_0", "sc_0_0", "sc_0_1",
                                          "od1", "od3", "od", "g1_1", "pq_1", "sc_1_0", "sc_1_1"))}
SPREADS = {n: i for i, n in enumerate(("end1", "b_s", "g1_0", "g2_0", "g1_1", "g2_1", "end2"))}


def _tiles(w):
    k, n = w.shape
    return w.reshape(k // P, P, n).transpose(1, 0, 2).reshape(P, -1)


def _layout(a):
    f = np.float32
    m = {k: np.asarray(v) for k, v in a.items()}
    stream = np.zeros((len(STREAM), P, SLOT), f)
    w_in, ckv, gu, down = m["w_in"][0], m["w_ckv"][0], m["w_gu"][0], m["w_down"][0]
    ev, od = m["ev_w_in_2"][0], m["od_w_in_2"][0]
    for i, name in enumerate(STREAM):
        kind, j = name[0], name[1] if len(name) > 1 else 0
        c = slice(512 * j, 512 * j + 512)
        if kind == "win":
            t = _tiles(w_in[:, WIN[j]:WIN[j + 1]])
        elif kind == "mla":
            t = np.concatenate([_tiles(m["w_uq"][0]), _tiles(m["w_ukv"][0])], 1)
        elif kind == "ck":
            t = _tiles(ckv[:, 0:512])
        elif kind == "cv":
            t = _tiles(ckv[:, 512:])
        elif kind == "wo":
            t = _tiles(m["w_o"][0][:, c])
        elif kind == "wcq":
            t = _tiles(m["w_cq"][0])
        elif kind == "wco":
            t = _tiles(m["w_co"][0])
        elif kind == "gu":
            t = _tiles(np.concatenate([gu[:, 256 * j:256 * j + 256], gu[:, FFN + 256 * j:FFN + 256 * j + 256]], 1))
        elif kind == "down":
            t = _tiles(down[512 * j:min(512 * j + 512, FFN)])
        elif kind == "ada":
            t = _tiles(m["ada_w_2"][name[1]][:, 512 * name[2]:512 * name[2] + 512])
        elif kind == "ev":
            t = _tiles(ev[:, c])
        elif kind == "evs":
            t = np.concatenate([m["ev_w_s_2"][0].transpose(2, 0, 1).reshape(P, -1), m["ev_w_pool_2"][0].transpose(1, 0, 2).reshape(P, -1)], 1)
        elif kind == "evo":
            t = _tiles(m["ev_w_out_2"][0][:, c])
        elif kind == "pq":
            t = _tiles(m["peer_w_q_2"][name[1]].reshape(D, -1)[:, 512 * name[2]:512 * name[2] + 512])
        elif kind == "keys":
            t = m["peer_sub_keys_2"][j].reshape(SETS, NKEYS, P).transpose(2, 0, 1).reshape(P, -1)
        elif kind == "od":
            t = _tiles(od[:, c])
        else:
            t = _tiles(m["od_w_out_2"][0][:, c])
        stream[i, :, 0:t.shape[1]] = t
        assert t.shape[1] == SIZE.get(name, SLOT), name

    def cv(x):
        return np.asarray(x).reshape(-1, P).T

    parts = {"norm_mix": cv(m["norm_mix"]), "q_norm": cv(m["q_norm"]), "kv_norm": cv(m["kv_norm"]), "out_norm": cv(m["out_norm"]),
             "norm_cross": cv(m["norm_cross"]), "norm_mem": cv(m["norm_mem"]), "norm_ffn": cv(m["norm_ffn"]),
             "final_norm": cv(m["final_norm"]), "c": cv(m["c_2"]), "ada_b": cv(m["ada_b_2"]), "norm_mix_2": cv(m["norm_mix_2"]),
             "norm_ffn_2": cv(m["norm_ffn_2"]), "g_v": cv(m["ev_g_v_2"]), "pool_scale": cv(m["ev_pool_scale_2"]),
             "b_s": cv(m["ev_b_s_2"]), "g_sub": cv(m["od_g_sub_2"]), "final_norm_2": cv(m["final_norm_2"]),
             "f_bias": np.repeat(m["f_bias"].reshape(1, 4), P, 0)}
    cols = np.zeros((P, NCOLS), f)
    for name, (a_, n) in COLS.items():
        cols[:, a_:a_ + n] = parts[name]

    q = np.arange(T)
    causal = np.where(q[None, :] <= q[:, None], 0.0, NEG).astype(f)
    chunked = np.where(q[None, :] // 64 <= q[:, None] // 64, 0.0, NEG).astype(f)
    tri = (q[:, None] <= q[None, :]).astype(f)
    masks = np.concatenate([_tiles(causal), _tiles(chunked), _tiles(tri)], 1)
    inv = (np.float32(10000.0) ** (-np.arange(0, ROPE, 2, dtype=f) / f(ROPE))).astype(f)
    turns = (q.astype(f)[:, None] * inv[None, :]).astype(f)
    rot = _tiles(np.concatenate([np.cos(turns), np.sin(turns)], 1).astype(f))
    pool = np.zeros((4, T, T), f)
    for g, w in enumerate(WINDOWS):
        for t in range(T):
            lo = max(0, t + 1 - w)
            pool[g, lo:t + 1, t] = f(1.0) / f(min(t + 1, w))
            pool[g, t, t] -= f(1.0)
    pool = pool.reshape(4, NB, P, T).transpose(2, 1, 0, 3).reshape(P, -1)
    table = m["rel_bias"][0]
    band = np.concatenate([np.repeat(table[:, -1:], T - 1 - 128, 1), table[:, ::-1], np.repeat(table[:, 0:1], T - 1 - 63, 1)], 1)
    rel = np.stack([band[:, T - 1 - i:2 * T - 1 - i] for i in range(T)])
    rel = rel.reshape(NB, P, 4, T).transpose(1, 0, 2, 3).reshape(P, -1)
    lam = np.concatenate([m[f"od_lam_{n}_2"].reshape(1, -1) for n in ("q1", "k1", "q2", "k2")], 1)
    experts_u = m["peer_u_2"].reshape(2, TILES, P, KT, P).transpose(0, 1, 4, 3, 2).reshape(2, TILES, P, D)
    inv3 = (f(1.0) / (f(10000.0) ** (np.arange(0, 64, 2, dtype=f) / f(64)))).astype(f)
    return {
        "x": _tiles(m["x"][0]), "mem": _tiles(m["mem"][0]), "cols": cols, "stream": stream,
        "perm": np.concatenate([np.eye(P, dtype=f), np.repeat(np.arange(P, dtype=f)[None], P, 0)], 1),
        "masks": masks, "rot": rot, "rel": rel, "pos": m["positions_2"].reshape(NB, P).T.astype(np.int32),
        "pool": pool, "inv_f": np.repeat(inv3[None], P, 0), "lam": np.repeat(lam, P, 0),
        "experts_u": experts_u, "experts_v": m["peer_v_2"].reshape(2, TILES, P, D),
    }


def kernel(**inputs):
    import concourse.bacc as bacc
    from concourse.bass_utils import run_bass_kernel_spmd

    arrays = {k: np.ascontiguousarray(v) for k, v in _layout(inputs).items()}
    nc = bacc.Bacc("TRN2", target_bir_lowering=False, num_devices=1)
    d = {k: nc.dram_tensor(f"in_{k}", v.shape, mybir.dt.from_np(v.dtype), kind="ExternalInput").ap() for k, v in arrays.items()}
    out = nc.dram_tensor("out_0", (1, T, D), F32, kind="ExternalOutput").ap()
    program(nc, d, out)
    r = run_bass_kernel_spmd(nc, [{f"in_{k}": v for k, v in arrays.items()}], core_ids=[0])
    return r.results[0]["out_0"]
```

```python
from contextlib import ExitStack

import numpy as np

import concourse.bass as bass
from concourse import mybir

P = 128
D = 1024
KT = D // P
T = 256
NB = T // P
EPS = 1e-6
NEG = -1e30

MLA_H, NOPE, ROPE, MLA_V = 4, 64, 32, 128
QK = NOPE + ROPE
FFN = 2816
FT = FFN // P
HEADS8, TOPK, NKEYS = 8, 16, 128
SETS = 2 * HEADS8
TILES = NKEYS
SUB = 2.0 ** -40
SUB_MAX = 2.0 ** 26
SUM_MAX = 3.4028234663852886e38 * SUB * SUB
LAM_INIT = 0.8 - 0.6 * float(np.exp(-0.3))
WINDOWS = (2, 4, 8, 16)

F32 = mybir.dt.float32
I32 = mybir.dt.int32
U32 = mybir.dt.uint32
F32R = mybir.dt.float32r
ALU = mybir.AluOpType
ACT = mybir.ActivationFunctionType
AX = mybir.AxisListType.X

SLOTS = 3
SLOT = 4096
E_SLOTS = 3
STEP = 6
CANDS = 16 + 7 * 8 + 8
GROUP = 4

COLS = {}
_at = 0
for _name, _n in (("norm_mix", 8), ("q_norm", 2), ("kv_norm", 1), ("out_norm", 8), ("norm_cross", 8),
                  ("norm_mem", 8), ("norm_ffn", 8), ("final_norm", 8), ("c", 8), ("ada_b", 96),
                  ("norm_mix_2", 16), ("norm_ffn_2", 16), ("g_v", 4), ("pool_scale", 4), ("b_s", 4),
                  ("g_sub", 1), ("final_norm_2", 8), ("f_bias", 4)):
    COLS[_name] = (_at, _n)
    _at += _n
NCOLS = _at

def _plan():
    ada = [("ada", l, j) for l in range(2) for j in range(12)]
    order = [("win", i) for i in range(5)] + [("mla",), ("ck",), ("cv",)]
    for name in [("wo", 0), ("wo", 1), ("wcq",), ("wco",)] + [("gu", i) for i in range(FT // 2)] + [("down", i) for i in range(6)]:
        order += [name, ada.pop(0)]
    for name in [("ev", 0), ("ev", 1), ("ev", 2)]:
        order += [name, ada.pop(0)]
    order += [("evs",), ("evo", 0), ("evo", 1)] + [("pq", 0, i) for i in range(4)]
    order += [("od", i) for i in range(6)] + [("odo", 0), ("odo", 1)] + [("pq", 1, i) for i in range(4)]
    return order


STREAM = _plan()
WIN = (0, 416, 928, 1188, 1700, 1956)
IN_PARTS = [("od", i) for i in range(1, 6)]
SIZE = {("mla",): 2 * 384 + 768, ("evs",): 1024, ("down", 5): 2048}
SIZE |= {("win", i): KT * (WIN[i + 1] - WIN[i]) for i in range(5)}


def program(nc, d, out):
    ctx = ExitStack()
    with ctx:
        def sb(name, n, dt=F32):
            return ctx.enter_context(nc.sbuf_tensor(name, [P, n], dt))

        sems = {}

        def sem(name):
            if name not in sems:
                sems[name] = ctx.enter_context(nc.semaphore(name))
            return sems[name]

        shared = (("HN", NB * D), ("HT", KT * T), ("ring", SLOTS * SLOT),
                  ("arena", T * NKEYS))
        with ExitStack() as whole_floats:
            hn_flat, ht_flat, ring, arena = [whole_floats.enter_context(nc.sbuf_tensor(name, [P, n], F32))[:, :] for name, n in shared]
        hn_r, ht_r, ring_r = [sb(f"{name}_rounded", n, F32R)[:, :] for name, n in shared[:3]]
        parts_at = 13600
        sb("arena_before", parts_at)
        parts_r = sb("parts", 3 * SLOT, F32R)[:, :]
        sb("arena_behind", T * NKEYS - parts_at - 3 * SLOT)
        HN = hn_flat.rearrange("p (b n) -> p b n", b=NB)
        HT = ht_flat.rearrange("p (k t) -> p k t", k=KT)
        X = sb("X", NB * D)[:, :].rearrange("p (b n) -> p b n", b=NB)
        cols = sb("cols", NCOLS)
        ident = sb("ident", P)[:, :]
        iota = sb("iota", P)[:, :]
        MOD = sb("MOD", 96)
        vec = sb("vec", 64)
        stat = sb("stat", 3 * 80)
        small = sb("small", 64)
        slots_t = sb("slots_t", 3 * T)[:, :].rearrange("p (a t) -> p a t", a=3)
        pos_i = sb("pos_i", NB, I32)
        ps = ctx.enter_context(nc.psum_tensor("ps", [P, 8, 512], F32))

        def col(name, i=0, n=None):
            a, w = COLS[name]
            return cols[:, a + i:a + i + (w if n is None else n)]

        class Region:
            def __init__(self, at=0):
                self.at = at

            def take(self, n, dt=None):
                a = arena[:, self.at:self.at + n]
                self.at += n
                assert self.at <= T * NKEYS, self.at
                return a if dt is None else a.bitcast(dt)

        def r3(a, n):
            return a.rearrange("p (a b) -> p a b", a=n)

        w_high = r3(parts_r[:, 0:2 * SLOT], 2)
        ht_parts = [r3(parts_r[:, i * KT * T:(i + 1) * KT * T], KT) for i in (4, 5)]
        split_no = {name: i for i, name in enumerate(IN_PARTS)}

        one = Region()
        causal = r3(one.take(2 * T), NB)
        chunked = r3(one.take(2 * T), NB)
        tri = r3(one.take(2 * T), NB)
        rot = r3(one.take(2 * ROPE), NB)
        relb = one.take(2 * 4 * T).rearrange("p (b h k) -> p b h k", b=2, h=4)
        start_reuse = one.at
        pa = r3(one.take(2 * 416), NB)
        fqk = r3(one.take(4 * T), 4)
        pc = r3(one.take(2 * 260), NB)
        cqk = r3(one.take(4 * T), 4)
        pe_ = r3(one.take(2 * 256), NB)
        lat_n = r3(one.take(2 * 384), NB)
        lat_t = r3(one.take(3 * T), 3)
        mq = r3(one.take(2 * 384), NB)
        mq_t = r3(one.take(4 * T), 4)
        mkv = r3(one.take(2 * 768), NB)
        mk = r3(one.take(2 * 384), NB)
        mk_t = r3(one.take(4 * T), 4)
        rtmp = r3(one.take(4 * 64), 4)
        flb = one.take(2 * 4 * T).rearrange("p (b h k) -> p b h k", b=2, h=4)
        nfl = one.take(2 * 4 * P).rearrange("p (b h k) -> p b h k", b=2, h=4)
        ymix = r3(one.take(2 * D), NB)
        s_buf = one.take(2 * D).rearrange("p (u m k) -> p u m k", u=2, m=4)
        p_buf = one.take(2 * D).rearrange("p (u m k) -> p u m k", u=2, m=4)
        pt_buf = one.take(2 * D).rearrange("p (u m a q) -> p u m a q", u=2, m=4, a=2)
        mem_t = r3(one.take(KT * T), KT)
        mem = r3(one.take(2 * D), NB)
        acc_ada = r3(mem.rearrange("p b n -> p (b n)"), 4)
        cross_k = r3(one.take(4 * T), 4)
        cross_v = r3(one.take(2 * 512), NB)
        cross_q, cross_t = fqk, mq_t
        cross_o = r3(cqk.rearrange("p a b -> p (a b)"), NB)
        ffn = Region(start_reuse)
        act_t = r3(ffn.take(FT * T), FT)
        silu_g = r3(ffn.take(2 * 512), 2)
        diag_f = ffn.take(D)

        two = Region()
        ug_t = r3(two.take(4 * T), 4)
        vg = r3(two.take(2 * 512), NB)
        vn = r3(two.take(2 * 512), NB)
        pl = r3(two.take(2 * 512), NB)
        bs_row = r3(two.take(4 * P), 4)
        pl_t = r3(two.take(4 * T), 4)
        ws_m = r3(two.take(4 * P), 4)
        diag_2 = two.take(D)
        bn = two.take(2 * 8)
        two.at = parts_at + 3 * SLOT
        pool_mat = two.take(2 * 4 * T).rearrange("p (s g t) -> p s g t", s=2, g=4)
        tri_2 = two.take(P)

        three = Region()
        causal_3 = r3(three.take(2 * T), NB)
        inv_f = three.take(32)
        lam_in = r3(three.take(4 * 64), 4)
        lam_p = r3(three.take(2 * 64), 2)
        ang = three.take(6 * 64).rearrange("p (a b f) -> p a b f", a=6, b=2)
        proj = r3(three.take(2 * 3072), NB)
        rt3 = r3(three.take(4 * 512), 4)
        dqk = three.take(2 * 2 * D).rearrange("p (a b n) -> p a b n", a=2, b=2)
        dq_t = r3(three.take(8 * T), 8)
        dk_t = r3(three.take(8 * T), 8)
        do = r3(three.take(2 * D), NB)
        dtmp = r3(three.take(2 * 512), 2)
        s_buf3 = three.take(2 * D).rearrange("p (u m k) -> p u m k", u=2, m=4)
        p_buf3 = three.take(2 * D).rearrange("p (u m k) -> p u m k", u=2, m=4)
        pt_buf3 = three.take(2 * D).rearrange("p (u m a q) -> p u m a q", u=2, m=4, a=2)
        diag_3 = three.take(D)

        ch = Region()
        pq_t = r3(ch.take(SETS * T), SETS)
        sc = ch.take(2 * SETS * P).rearrange("p (s b n) -> p s b n", b=2, s=SETS)
        sw = ch.take(2 * SETS * P).rearrange("p (s b n) -> p s b n", b=2, s=SETS)
        top_v = ch.take(2 * SETS * TOPK).rearrange("p (a m k) -> p a m k", a=2, k=TOPK)
        top_i = ch.take(2 * SETS * TOPK, U32).rearrange("p (a m k) -> p a m k", a=2, k=TOPK)
        top_f = ch.take(2 * SETS * TOPK).rearrange("p (a m k) -> p a m k", a=2, k=TOPK)
        cand = r3(ch.take(SETS * CANDS), SETS)
        cw = r3(ch.take(SETS * CANDS), SETS)
        fin_v = r3(ch.take(2 * P), SETS)
        fin_p = ch.take(2 * P, U32)
        fin_ij = r3(ch.take(4 * P, U32), 2)
        fin_f = r3(ch.take(6 * P), 3)
        eq = ch.take(2 * 1024).rearrange("p (a n) -> p a n", a=2)
        chosen = ch.take(6 * P).rearrange("p (a b m) -> p a b m", a=3, b=2)
        chosen_h = chosen.rearrange("p a b (h k) -> p a h b k", h=8)
        gsum = ch.take(2 * 16).rearrange("p (a m) -> p a m", a=2)
        keys_at = T * NKEYS - SETS * NKEYS
        keys_t = r3(arena[:, keys_at:], SETS)
        assert max(two.at, three.at, ch.at) <= keys_at
        gates = arena[:, :].rearrange("p (t i) -> p t i", i=NKEYS)

        ones = sb("ones", P)[:, :]
        eps = small[:, 0:1]
        unit = small[:, 1:2]
        fz = r3(small[:, 2:34], 4).rearrange("p a (b h) -> p a b h", b=2)
        mx = r3(sb("mx", 12)[:, :], 3)
        sums = r3(sb("sums", 12)[:, :], 3)
        rinv = r3(small[:, 50:58], 2)
        coef = small[:, 58:62]
        lam2 = small[:, 62:64]
        wcoef = r3(stat[:, 228:236], 2)
        posf = stat[:, 236:238]
        cact = sb("cact", 8)
        newton = sb("newton", 32)
        def norm(src, dst, segs, junk=None):
            return dict(src=src, dst=dst, segs=segs, junk=junk or dst)

        whole = [(0, D)]
        NORMS = {
            "mix": norm(lambda b: X[:, b, :], lambda b: HN[:, b, :], whole),
            "mem": norm(lambda b: mem[:, b, :], lambda b: mem[:, b, :], whole,
                        lambda b: mem_t.rearrange("p k t -> p (k t)")[:, b * D:(b + 1) * D]),
            "lat": norm(lambda b: pa[:, b, 0:384], lambda b: lat_n[:, b, :], [(0, 256), (256, 384)]),
            "y": norm(lambda b: ymix[:, b, :], lambda b: HN[:, b, :], [(0, 512), (512, 768), (768, 1024)]),
            "cross": norm(lambda b: X[:, b, :], lambda b: HN[:, b, :], whole),
            "ffn": norm(lambda b: X[:, b, :], lambda b: HN[:, b, :], whole),
            "end1": norm(lambda b: X[:, b, :], lambda b: HN[:, b, :], whole),
            "mix_0": norm(lambda b: X[:, b, :], lambda b: HN[:, b, :], whole),
            "peer_0": norm(lambda b: X[:, b, :], lambda b: HN[:, b, :], whole),
            "mix_1": norm(lambda b: X[:, b, :], lambda b: HN[:, b, :], whole),
            "sub": norm(lambda b: do[:, b, :], lambda b: HN[:, b, :], [(128 * h, 128 * h + 128) for h in range(8)]),
            "peer_1": norm(lambda b: X[:, b, :], lambda b: HN[:, b, :], whole),
            "end2": norm(lambda b: X[:, b, :], lambda b: HN[:, b, :], whole),
        }
        at = 0
        for k, (name, n) in enumerate(NORMS.items()):
            n["no"], n["col"] = k, at
            at += 2 * len(n["segs"])
        assert at <= 76, at
        ss, rms, rstd = stat[:, 0:76], stat[:, 76:152], stat[:, 152:228]

        def widths(segs):
            groups = []
            for i, (lo, hi) in enumerate(segs):
                if groups and groups[-1][2] == hi - lo:
                    groups[-1][1] += 1
                else:
                    groups.append([i, i + 1, hi - lo])
            return groups

        PAIRED = (0, 2, 1, 3)

        def unit_of(kind, b, g=0):
            u = dict(kind=kind, b=b)
            if kind == "mla":
                u["qk"] = [[(mq_t[0:QK, h, b * P:(b + 1) * P], mk_t[0:QK, h, :])] for h in range(4)]
                u["v"] = lambda kb, h: mkv[:, kb, h * 192 + 64:(h + 1) * 192]
                u["scale"], u["dv"], u["mask"] = float(QK) ** -0.5, 128, chunked
                u["out"] = ymix[:, b, 0:512]
            elif kind == "fox":
                u["qk"] = []
                for h in PAIRED:
                    q = slice(64 * (h % 2), 64 * (h % 2) + 64)
                    pairs = [(fqk[q, h // 2, b * P:(b + 1) * P], fqk[q, 2 + h // 2, :])]
                    for s in range(NB):
                        pairs.append((tri[:, s, b * P:(b + 1) * P], flb[:, s, h, :]))
                        pairs.append((nfl[:, s, h, :], tri[:, s, :]))
                    u["qk"].append(pairs)
                u["v"] = lambda kb, m: pc[:, kb, PAIRED[m] * 64:(PAIRED[m] + 1) * 64]
                u["scale"], u["dv"], u["mask"] = 0.125, 64, causal
                u["out"] = ymix[:, b, 512:768]
            elif kind == "chk":
                u["qk"] = []
                for h in PAIRED:
                    q = slice(64 * (h % 2), 64 * (h % 2) + 64)
                    u["qk"].append([(cqk[q, h // 2, b * P:(b + 1) * P], cqk[q, 2 + h // 2, :])])
                u["v"] = lambda kb, m: pe_[:, kb, PAIRED[m] * 64:(PAIRED[m] + 1) * 64]
                u["scale"], u["dv"], u["mask"] = 0.125, 64, "rel"
                u["out"] = ymix[:, b, 768:1024]
            elif kind == "cross":
                u["qk"] = [[(cross_q[:, h, b * P:(b + 1) * P], cross_k[:, h, :])] for h in range(4)]
                u["v"] = lambda kb, h: cross_v[:, kb, h * P:(h + 1) * P]
                u["scale"], u["dv"], u["mask"] = float(P) ** -0.5, 128, None
                u["out"] = cross_o[:, b, :]
            else:
                u["qk"] = []
                for i in range(4):
                    h, q = 2 * g + i % 2, slice(64 * (i // 2), 64 * (i // 2) + 64)
                    u["qk"].append([(dq_t[q, h, b * P:(b + 1) * P], dk_t[q, h, :])])
                u["v"] = lambda kb, i: proj[:, kb, 2048 + (2 * g + i % 2) * P:2048 + (2 * g + i % 2 + 1) * P]
                u["scale"], u["dv"], u["mask"] = 0.125, 128, causal_3
                u["out"] = do[:, b, 2 * g * P:(2 * g + 2) * P]
            return u

        ATT = {"self": [unit_of(k, b) for k in ("mla", "fox", "chk") for b in range(NB)],
               "cross": [unit_of("cross", b) for b in range(NB)],
               "diff": [unit_of("diff", b, g) for g in range(4) for b in range(NB)]}
        n = 0
        for units in ATT.values():
            for u in units:
                u["no"] = n
                sbuf, pbuf, ptbuf = (s_buf3, p_buf3, pt_buf3) if u["kind"] == "diff" else (s_buf, p_buf, pt_buf)
                u["s"], u["p"], u["pt"] = sbuf[:, n % 2], pbuf[:, n % 2], ptbuf[:, n % 2]
                n += 1

        tile_no = {}
        chunk_no = {name: i for i, name in enumerate(STREAM)}
        released = {}

        def weights(name):
            s = chunk_no[name] % SLOTS
            return ring[:, s * SLOT:s * SLOT + SIZE.get(name, SLOT)]

        def weights_low(name):
            s = chunk_no[name] % SLOTS
            return ring_r[:, s * SLOT:(s + 1) * SLOT]

        def weights_high(name):
            return w_high[:, split_no[name] % 2]

        def wait_weights(eng, name):
            i = chunk_no[name]
            eng.wait_ge(sem(f"arrived{i % SLOTS}"), 16 * (i // SLOTS + 1))

        def tile(name):
            return ps[:, tile_no[name] % 8, :]

        def wait_tile(eng, name):
            i = tile_no[name]
            eng.wait_ge(sem(f"filled{i % 8}"), i // 8 + 1)
            return tile(name)

        def drained(ins, name):
            ins.then_inc(sem(f"drained{tile_no[name] % 8}"), 1)

        exp_u = r3(ring[:, 0:3 * D], E_SLOTS)
        exp_v = r3(ring[:, 3 * D:6 * D], E_SLOTS)
        exp_ul = r3(ring_r[:, 0:3 * D], E_SLOTS)
        exp_vl = r3(ring_r[:, 3 * D:6 * D], E_SLOTS)
        exp_uh = r3(ring_r[:, 6 * D:8 * D], 2)
        exp_vh = r3(ring_r[:, 8 * D:10 * D], 2)
        ht_high = r3(ring_r[:, 10 * D:12 * D], KT)
        ht_low = r3(ht_r, KT)
        act_e = r3(hn_flat[:, 0:512], 2)
        act_l = r3(hn_r[:, 0:512], 2)
        act_h = r3(hn_r[:, 512:1024], 2)
        g2_row = hn_flat[:, 1024:2048]
        hot = hn_flat.rearrange("p (u a t n) -> p u a t n", u=2, a=2, t=GROUP)
        NG = T // GROUP

        block = ctx.enter_context(nc.Block())

        @block.tensor
        def _(pe):
            def claim(name):
                i = len(tile_no)
                tile_no[name] = i
                if i >= 8:
                    pe.wait_ge(sem(f"drained{i % 8}"), i // 8)
                return ps[:, i % 8, :]

            def publish(ins, name):
                ins.then_inc(sem(f"filled{tile_no[name] % 8}"), 1)
                return sem(f"filled{tile_no[name] % 8}"), tile_no[name] // 8 + 1

            def in_parts(out_, w, x, first, last):
                for i, (p, q) in enumerate(((w[0], x[0]), (w[0], x[1]), (w[1], x[0]))):
                    mm = pe.matmul(out_, p, q, start=(first and i == 0), stop=(last and i == 2))
                return mm

            def parts(name):
                pe.wait_ge(sem("ht_parts"), 1)
                pe.wait_ge(sem("weights_low"), split_no[name] + 1)
                return r3(weights_high(name), KT), r3(weights_low(name), KT)

            def rows_in_parts(name):
                w = parts(name)
                for b in range(NB):
                    t = claim((name, b))
                    for k in range(KT):
                        mm = in_parts(t, [h[:, k, b * P:(b + 1) * P] for h in ht_parts], [p[:, k, :] for p in w], k == 0, k == KT - 1)
                    released[name] = publish(mm, (name, b))

            def rows(chunk, name, src, w, n, nk=KT):
                for b in range(NB):
                    t = claim((name, b))
                    for k in range(nk):
                        mm = pe.matmul(t[:, 0:n], src[:, k, b * P:(b + 1) * P], w[:, k, :],
                                       start=(k == 0), stop=(k == nk - 1))
                    released[chunk] = publish(mm, (name, b))

            def turned(chunk, name, src, w, n):
                for i in range(n // 256):
                    t = claim((name, i))
                    for j in range(2):
                        for k in range(KT):
                            mm = pe.matmul(t[:, j * T:(j + 1) * T], w[:, k, i * 256 + j * P:i * 256 + (j + 1) * P],
                                           src[:, k, :], start=(k == 0), stop=(k == KT - 1))
                    released[chunk] = publish(mm, (name, i))

            def turn(norm, nk=KT):
                n = NORMS[norm]
                for b in range(NB):
                    pe.wait_ge(sem("normed"), NB * n["no"] + b + 1)
                    for i in range(0, nk, 4):
                        t = claim((norm, b, i))
                        for k in range(i, min(i + 4, nk)):
                            mm = pe.transpose(t[:, (k - i) * P:(k - i + 1) * P], n["dst"](b)[:, k * P:(k + 1) * P], ident)
                        publish(mm, (norm, b, i))

            def turn_heads(name, src, width, heads):
                for b in range(NB):
                    for i in range(0, heads, 4):
                        t = claim((name, b, i))
                        for h in range(i, i + 4):
                            mm = pe.transpose(t[0:width, (h - i) * P:(h - i + 1) * P],
                                              src[:, b, h * width:(h + 1) * width], ident)
                        publish(mm, (name, b, i))

            def scores(u):
                for half in range(2):
                    t = claim(("s", u["no"], half))
                    for m in range(2):
                        pairs = u["qk"][2 * half + m]
                        for i, (q, k) in enumerate(pairs):
                            mm = pe.matmul(t[:, m * T:(m + 1) * T], q, k, start=(i == 0), stop=(i == len(pairs) - 1))
                    publish(mm, ("s", u["no"], half))

            def turn_probs(u):
                pe.wait_ge(sem("probs"), u["no"] + 1)
                for half in range(2):
                    t = claim(("pt", u["no"], half))
                    for m in range(2):
                        for kb in range(NB):
                            mm = pe.transpose(t[:, (2 * m + kb) * P:(2 * m + kb + 1) * P],
                                              u["p"][:, 2 * half + m, kb * P:(kb + 1) * P], ident)
                    publish(mm, ("pt", u["no"], half))

            def values(u):
                pe.wait_ge(sem("probs_turned"), u["no"] + 1)
                t = claim(("o", u["no"]))
                for m in range(4):
                    for kb in range(NB):
                        mm = pe.matmul(t[:, m * u["dv"]:(m + 1) * u["dv"]], u["pt"][:, m, kb, :], u["v"](kb, m),
                                       start=(kb == 0), stop=(kb == NB - 1))
                publish(mm, ("o", u["no"]))

            def attention(units):
                scores(units[0])
                scores(units[1])
                for i, u in enumerate(units):
                    turn_probs(u)
                    if i + 2 < len(units):
                        scores(units[i + 2])
                    values(u)

            def fold(l, j):
                i = 12 * l + j
                pe.wait_ge(sem("ada_summed"), i + 1)
                t = claim(("ada", l, j))
                for c in range(4):
                    mm = pe.matmul(t[:, c:c + 1], acc_ada[:, i % 4, c * P:(c + 1) * P], ones[:, 0:1], start=True, stop=True)
                publish(mm, ("ada", l, j))

            ada_left = [(l, j) for l in range(2) for j in range(12)]

            def next_fold():
                fold(*ada_left.pop(0))

            def spread(name, diag, n=8):
                pe.wait_ge(sem("diag"), SPREADS[name] + 1)
                for i in range(0, n, 4):
                    t = claim(("spread", name, i))
                    for k in range(i, i + 4):
                        mm = pe.matmul(t[:, (k - i) * P:(k - i + 1) * P], ones, diag[:, k * P:(k + 1) * P], start=True, stop=True)
                    publish(mm, ("spread", name, i))

            pe.wait_ge(sem("consts"), 48)
            pe.wait_ge(sem("made"), 3)
            turn("mix")
            pe.wait_ge(sem("h_ready"), H_READY["mix"])
            for i in range(5):
                wait_weights(pe, ("win", i))
                n = WIN[i + 1] - WIN[i]
                w = r3(weights(("win", i)), KT)
                (turned if i in (1, 3) else rows)(("win", i), ("win", i), HT, w, n)
                if i == 1:
                    turn("lat", 3)
                if i == 2:
                    turn("mem")
            pe.wait_ge(sem("h_ready"), H_READY["lat"])
            wait_weights(pe, ("mla",))
            w = weights(("mla",))
            rows(("mla",), "mq", lat_t, r3(w[:, 0:768], 2), 384, 2)
            for half in range(2):
                for b in range(NB):
                    t = claim(("mkv", half, b))
                    mm = pe.matmul(t[:, 0:384], lat_t[:, 2, b * P:(b + 1) * P], w[:, 768 + half * 384:768 + (half + 1) * 384],
                                   start=True, stop=True)
                    released[("mla",)] = publish(mm, ("mkv", half, b))
            pe.wait_ge(sem("h_ready"), H_READY["mem"])
            wait_weights(pe, ("ck",))
            turned(("ck",), "ck", mem_t, r3(weights(("ck",)), KT), 512)
            pe.wait_ge(sem("roped"), 1)
            turn_heads("mq_t", mq, QK, 4)
            turn_heads("mk_t", mk, QK, 4)
            wait_weights(pe, ("cv",))
            rows(("cv",), "cv", mem_t, r3(weights(("cv",)), KT), 512)
            pe.wait_ge(sem("heads_turned"), 4)
            pe.wait_ge(sem("stored"), STORED["win"])
            pe.wait_ge(sem("forget"), 1)
            pe.wait_ge(sem("masks"), 64)
            attention(ATT["self"])
            turn("y")
            pe.wait_ge(sem("h_ready"), H_READY["y"])
            for i in range(2):
                wait_weights(pe, ("wo", i))
                rows(("wo", i), ("wo", i), HT, r3(weights(("wo", i)), KT), 512)
                if i:
                    next_fold()
            turn("cross")
            pe.wait_ge(sem("h_ready"), H_READY["cross"])
            wait_weights(pe, ("wcq",))
            turned(("wcq",), "wcq", HT, r3(weights(("wcq",)), KT), 512)
            next_fold()
            pe.wait_ge(sem("stored"), STORED["wcq"])
            attention(ATT["cross"])
            pe.wait_ge(sem("cross_out"), 1)
            turn_heads("cross_t", cross_o, P, 4)
            pe.wait_ge(sem("heads_turned"), 6)
            wait_weights(pe, ("wco",))
            w = r3(weights(("wco",)), 4)
            next_fold()
            for b in range(NB):
                for half in range(2):
                    t = claim(("wco", b, half))
                    for k in range(4):
                        mm = pe.matmul(t, cross_t[:, k, b * P:(b + 1) * P], w[:, k, half * 512:(half + 1) * 512],
                                       start=(k == 0), stop=(k == 3))
                    released[("wco",)] = publish(mm, ("wco", b, half))
            turn("ffn")
            pe.wait_ge(sem("h_ready"), H_READY["ffn"])
            for i in range(FT // 2):
                name = ("gu", i)
                wait_weights(pe, name)
                turned(name, name, HT, r3(weights(name), KT), 512)
                next_fold()
            pe.wait_ge(sem("act_ready"), FT // 2)
            down = [claim(("down", b, half)) for b in range(NB) for half in range(2)]
            for c in range(6):
                name = ("down", c)
                wait_weights(pe, name)
                nk = 4 if c < 5 else 2
                w = r3(weights(name), nk)
                for k in range(nk):
                    kt = 4 * c + k
                    for b in range(NB):
                        for half in range(2):
                            mm = pe.matmul(down[2 * b + half], act_t[:, kt, b * P:(b + 1) * P], w[:, k, half * 512:(half + 1) * 512],
                                           start=(kt == 0), stop=(kt == FT - 1))
                            if kt == FT - 1:
                                released[name] = publish(mm, ("down", b, half))
                if c < 5:
                    mm.then_inc(sem("down_read"), 1)
                    released[name] = (sem("down_read"), c + 1)
                if c < 4:
                    next_fold()
            for _ in range(2):
                next_fold()
            spread("end1", diag_f)

            def experts(l):
                turn(f"peer_{l}")
                pe.wait_ge(sem("h_ready"), H_READY[f"peer_{l}"])
                for i in range(4):
                    name = ("pq", l, i)
                    wait_weights(pe, name)
                    for j in range(2):
                        h = 2 * i + j
                        turned(name, (name, j), HT, r3(weights(name), KT)[:, :, j * 256:(j + 1) * 256], 256)
                        pe.wait_ge(sem("keys_loaded"), 16 * (l + 1))
                        pe.wait_ge(sem("stored"), STORED[f"pq_{l}_{h}"])
                        t = claim((f"sc_{l}", h))
                        for s in range(2):
                            for b in range(NB):
                                mm = pe.matmul(t[:, (2 * s + b) * P:(2 * s + b + 1) * P], pq_t[:, 2 * h + s, b * P:(b + 1) * P],
                                               keys_t[:, 2 * h + s, :], start=True, stop=True)
                        publish(mm, (f"sc_{l}", h))
                pe.wait_ge(sem("chosen"), l + 1)
                for b in range(NB):
                    t = claim((f"slots_{l}", b))
                    for a in range(3):
                        mm = pe.transpose(t[:, a * P:(a + 1) * P], chosen[:, a, b, :], ident)
                    publish(mm, (f"slots_{l}", b))
                for bank in range(8):
                    pe.wait_ge(sem(f"drained{bank}"), (len(tile_no) - 1 - bank) // 8 + 1)

                def gate_products(u, ready, stored):
                    pe.wait_ge(sem("hot"), ready)
                    if stored is not None:
                        pe.wait_ge(sem("gates_stored"), stored)
                    for t in range(GROUP):
                        mm = pe.matmul(ps[:, 6 + u, t * P:(t + 1) * P], hot[:, u, 1, t, :], hot[:, u, 0, t, :],
                                       start=True, stop=True)
                    mm.then_inc(sem("gates_made"), 1)

                for u in range(2):
                    gate_products(u, l * NG + u + 1, None)
                with pe.Fori(1, NG // 2) as i:
                    for u in range(2):
                        gate_products(u, i * 2 + (l * NG + u + 1), i * 2 + (l * NG + u - 1))
                spread(f"g2_{l}", hn_flat)
                pe.wait_ge(sem("g2_row"), l + 1)
                for bank in range(8):
                    pe.wait_ge(sem(f"drained{bank}"), (len(tile_no) - 1 - bank) // 8 + 1)

                def expert_scores(j, ready):
                    pe.wait_ge(sem("expert_u"), ready)
                    for k in range(KT):
                        c = slice(k * P, (k + 1) * P)
                        mm = in_parts(ps[:, 4 + j % 2, 0:T], (exp_uh[:, j % 2, c], exp_ul[:, j % E_SLOTS, c]),
                                           (ht_high[:, k, :], ht_low[:, k, :]), k == 0, k == KT - 1)
                    mm.then_inc(sem("expert_scored"), 1)

                def expert_values(j, ready, first=False, last=False):
                    pe.wait_ge(sem("expert_gated"), ready)
                    pe.wait_ge(sem("expert_v"), ready)
                    for b in range(NB):
                        for half in range(2):
                            t, c = slice(b * P, (b + 1) * P), slice(half * 512, (half + 1) * 512)
                            mm = in_parts(ps[:, 2 * b + half, :], (act_h[:, j % 2, t], act_l[:, j % 2, t]),
                                               (exp_vh[:, j % 2, c], exp_vl[:, j % E_SLOTS, c]), first, last)
                    mm.then_inc(sem("expert_used"), 1)

                base = l * TILES
                pe.wait_ge(sem("ht_split"), l + 1)
                pe.sem_inc(sem("expert_used"), 1)
                for n in range(2):
                    expert_scores(n, base + n + 1)
                expert_values(0, base + 1, first=True)
                turns = (TILES - 2) // STEP - 1
                with pe.Fori(0, turns) as i:
                    for j in range(1, STEP + 1):
                        expert_scores(j + 1, i * STEP + (base + j + 2))
                        expert_values(j, i * STEP + (base + j + 1))
                for n in range(turns * STEP + 1, TILES):
                    if n + 1 < TILES:
                        expert_scores(n + 1, base + n + 2)
                    expert_values(n, base + n + 1, last=(n == TILES - 1))

            turn("mix_0")
            pe.wait_ge(sem("h_ready"), H_READY["mix_0"])
            wait_weights(pe, ("ev", 0))
            turned(("ev", 0), ("ev", 0), HT, r3(weights(("ev", 0)), KT), 512)
            next_fold()
            for i in (1, 2):
                wait_weights(pe, ("ev", i))
                rows(("ev", i), ("ev", i), HT, r3(weights(("ev", i)), KT), 512)
                next_fold()
            next_fold()
            spread("b_s", diag_2, 4)
            pe.wait_ge(sem("stored"), STORED["ev"])
            wait_weights(pe, ("evs",))
            w = weights(("evs",))
            pe.wait_ge(sem("pool_mat"), 32)
            for g in range(0, 4, 2):
                t = claim(("pool", g))
                for j in range(2):
                    for s in range(NB):
                        mm = pe.matmul(t[:, j * T:(j + 1) * T], pl[:, s, (g + j) * P:(g + j + 1) * P], pool_mat[:, s, g + j, :],
                                       start=(s == 0), stop=(s == NB - 1))
                publish(mm, ("pool", g))
            pe.wait_ge(sem("pooled"), 2)
            for g in range(0, 4, 2):
                t = claim(("mixed", g))
                for j in range(2):
                    mm = pe.matmul(t[:, j * T:(j + 1) * T], w[:, 512 + (g + j) * P:512 + (g + j + 1) * P], pl_t[:, g + j, :],
                                   start=True, stop=True)
                publish(mm, ("mixed", g))
            pe.wait_ge(sem("spatial_in"), 1)
            for b in range(NB):
                t = claim(("spatial", b))
                for g in range(4):
                    mm = pe.matmul(t[:, g * P:(g + 1) * P], vn[:, b, g * P:(g + 1) * P], ws_m[:, g, :], start=True, stop=True)
                released[("evs",)] = publish(mm, ("spatial", b))
            pe.wait_ge(sem("h_ready"), H_READY["even_y"])
            spread("g1_0", hn_flat)
            for i in range(2):
                wait_weights(pe, ("evo", i))
                rows(("evo", i), ("evo", i), HT, r3(weights(("evo", i)), KT), 512)
            experts(0)

            turn("mix_1")
            pe.wait_ge(sem("h_ready"), H_READY["mix_1"])
            wait_weights(pe, ("od", 0))
            rows(("od", 0), ("od", 0), HT, r3(weights(("od", 0)), KT), 512)
            for i in range(1, 6):
                rows_in_parts(("od", i))
            for a in range(2):
                pe.wait_ge(sem("roped"), 2 + a)
                turn_heads(("dq_t", "dk_t")[a], dqk[:, a], P, 8)
            pe.wait_ge(sem("heads_turned"), 14)
            pe.wait_ge(sem("stored"), STORED["od"])
            attention(ATT["diff"])
            turn("sub")
            pe.wait_ge(sem("h_ready"), H_READY["sub"])
            spread("g1_1", diag_3)
            for i in range(2):
                wait_weights(pe, ("odo", i))
                rows(("odo", i), ("odo", i), HT, r3(weights(("odo", i)), KT), 512)
            experts(1)
            spread("end2", diag_3)

        @block.scalar
        def _(act):
            own = [0]

            def step(ins):
                own[0] += 1
                ins.then_inc(sem("act_steps"), 1)

            def settle():
                act.wait_ge(sem("act_steps"), own[0])

            def root(name, x=None):
                n = NORMS[name]
                ns = len(n["segs"])
                for b in range(NB):
                    if x is not None:
                        act.wait_ge(sem("x_ready"), X_READY[x] - NB + b + 1)
                    c = n["col"] + b * ns
                    for i, (lo, hi) in enumerate(n["segs"]):
                        step(act.activation(n["junk"](b)[:, lo:hi], n["src"](b)[:, lo:hi], ACT.Square, accum_out=ss[:, c + i:c + i + 1]))
                    settle()
                    for i, j, width in widths(n["segs"]):
                        ins = act.activation(rms[:, c + i:c + j], ss[:, c + i:c + j], ACT.Sqrt, bias=vec[:, 58:59] if name == "sub" else eps,
                                             scale=1.0 / width)
                        if j == ns:
                            ins.then_inc(sem("rooted"), 1)
                        else:
                            step(ins)

            def store(dst, name, func=ACT.Copy, src=None):
                t = wait_tile(act, name)
                ins = act.activation(dst, t if src is None else src(t), func)
                drained(ins, name)

            def stored(name):
                last = name_of_last[0]
                i = tile_no[last]
                act.wait_ge(sem(f"drained{i % 8}"), i // 8 + 1)
                act.sem_inc(sem("stored"), 1)

            name_of_last = [None]

            def put(dst, name, func=ACT.Copy, src=None):
                store(dst, name, func, src)
                name_of_last[0] = name

            def high_part(name):
                n = split_no[name]
                wait_weights(act, name)
                if n >= 2:
                    s, v = released[IN_PARTS[n - 2]]
                    act.wait_ge(s, v)
                act.activation(weights_high(name), weights(name), ACT.Copy).then_inc(sem("weights_high"), 1)

            def soft(u):
                k = u["no"] % 3
                act.wait_ge(sem("maxima"), u["no"] + 1)
                for m in range(4):
                    ins = act.activation(u["p"][:, m, :], u["s"][:, m, :], ACT.Exp, bias=mx[:, k, m:m + 1], accum_out=sums[:, k, m:m + 1])
                ins.then_inc(sem("probs"), 1)

            def put_probs(u):
                for half in range(2):
                    put(u["pt"][:, 2 * half:2 * half + 2].rearrange("p m a q -> p (m a q)"), ("pt", u["no"], half))
                i = tile_no[("pt", u["no"], 1)]
                act.wait_ge(sem(f"drained{i % 8}"), i // 8 + 1)
                act.sem_inc(sem("probs_turned"), 1)

            def attention(units):
                soft(units[0])
                for i, u in enumerate(units):
                    if i + 1 < len(units):
                        soft(units[i + 1])
                    put_probs(u)

            act.wait_ge(sem("made"), 3)
            act.wait_ge(sem("x_loaded"), 16)
            root("mix")
            act.wait_ge(sem("mem_loaded"), 16)
            root("mem")
            act.wait_ge(sem("consts"), 48)
            act.activation(cact[:, :], col("c"), ACT.Silu).then_inc(sem("cact"), 1)
            for b in range(NB):
                put(pa[:, b, :], (("win", 0), b), src=lambda t: t[:, 0:416])
            i = tile_no[(("win", 0), 1)]
            act.wait_ge(sem(f"drained{i % 8}"), i // 8 + 1)
            root("lat")
            for i in range(2):
                put(fqk[:, 2 * i:2 * i + 2].rearrange("p a t -> p (a t)"), (("win", 1), i))
            for b in range(NB):
                put(pc[:, b, :], (("win", 2), b), src=lambda t: t[:, 0:260])
            stored("pc")
            for i in range(2):
                put(cqk[:, 2 * i:2 * i + 2].rearrange("p a t -> p (a t)"), (("win", 3), i))
            for b in range(NB):
                put(pe_[:, b, :], (("win", 4), b), src=lambda t: t[:, 0:256])
            stored("win")
            for b in range(NB):
                put(mq[:, b, :], ("mq", b), src=lambda t: t[:, 0:384])
            for half in range(2):
                for b in range(NB):
                    put(mkv[:, b, half * 384:(half + 1) * 384], ("mkv", half, b), src=lambda t: t[:, 0:384])
            stored("mla")
            for i in range(2):
                put(cross_k[:, 2 * i:2 * i + 2].rearrange("p a t -> p (a t)"), ("ck", i))
            act.wait_ge(sem("forget_in"), 1)
            step(act.activation(fz[:, 2], fz[:, 1], ACT.Exp))
            settle()
            act.activation(fz[:, 3], fz[:, 2], ACT.Ln, bias=unit).then_inc(sem("forget_ln"), 1)
            for name, dst in (("mq_t", mq_t), ("mk_t", mk_t)):
                for b in range(NB):
                    put(dst[0:QK, :, b * P:(b + 1) * P], (name, b, 0), src=lambda t: r3(t[0:QK, :], 4))
                    i = tile_no[(name, b, 0)]
                    act.wait_ge(sem(f"drained{i % 8}"), i // 8 + 1)
                    act.sem_inc(sem("heads_turned"), 1)
            for b in range(NB):
                put(cross_v[:, b, :], ("cv", b))
            stored("cv")
            attention(ATT["self"])
            act.wait_ge(sem("y_ready"), 1)
            root("y")
            root("cross", "wo")
            for i in range(2):
                put(cross_q[:, 2 * i:2 * i + 2].rearrange("p a t -> p (a t)"), ("wcq", i))
            stored("wcq")
            attention(ATT["cross"])
            for b in range(NB):
                put(cross_t[:, :, b * P:(b + 1) * P], ("cross_t", b, 0), src=lambda t: r3(t, 4))
                i = tile_no[("cross_t", b, 0)]
                act.wait_ge(sem(f"drained{i % 8}"), i // 8 + 1)
                act.sem_inc(sem("heads_turned"), 1)
            root("ffn", "wco")
            for i in range(FT // 2):
                if i >= 2:
                    act.wait_ge(sem("act_ready"), i - 1)
                put(silu_g[:, i % 2], (("gu", i), 0), ACT.Silu)
                t = tile_no[(("gu", i), 0)]
                act.wait_ge(sem(f"drained{t % 8}"), t // 8 + 1)
                act.sem_inc(sem("silu"), 1)
            root("end1", "down")

            def experts(l):
                def gate_exp(i):
                    act.wait_ge(sem("gate_in"), 4 * l + i + 1)
                    act.activation(chosen_h[:, 2, 2 * i:2 * i + 2], fin_v[:, 4 * i:4 * i + 4].rearrange("p (h b) k -> p h b k", b=NB), ACT.Exp)\
                       .then_inc(sem("gate_exp"), 1)

                root(f"peer_{l}", f"mix_{l}")
                for i in range(4):
                    for j in range(2):
                        h = 2 * i + j
                        put(pq_t[:, 2 * h:2 * h + 2].rearrange("p a t -> p (a t)"), ((("pq", l, i), j), 0))
                        stored(f"pq_{l}_{h}")
                        put(sc[:, 2 * h:2 * h + 2].rearrange("p s b n -> p (s b n)"), (f"sc_{l}", h))
                        stored(f"sc_{l}_{h}")
                    if i:
                        gate_exp(i - 1)
                gate_exp(3)
                act.wait_ge(sem("slots"), 2 * l + 2)

                def keep_gates(u, made, at_):
                    act.wait_ge(sem("gates_made"), made)
                    act.activation(arena[:, bass.ds(at_, GROUP * P)], ps[:, 6 + u, :], ACT.Copy).then_inc(sem("gates_stored"), 1)

                with act.Fori(0, NG // 2) as i:
                    for u in range(2):
                        keep_gates(u, i * 2 + (l * NG + u + 1), i * (2 * GROUP * P) + u * GROUP * P)
                for i in range(0, 8, 4):
                    put(g2_row[:, i * P:(i + 4) * P], ("spread", f"g2_{l}", i))
                i = tile_no[("spread", f"g2_{l}", 4)]
                act.wait_ge(sem(f"drained{i % 8}"), i // 8 + 1)
                act.sem_inc(sem("g2_row"), 1)
                with act.Fori(0, TILES // 2) as i:
                    for a in range(2):
                        act.wait_ge(sem("expert_scored"), i * 2 + (l * TILES + a + 1))
                        act.activation(act_e[:, a, :], ps[:, 4 + a, 0:T], ACT.Gelu).then_inc(sem("expert_act"), 1)

            root("mix_0", "end1")
            for i in range(2):
                put(ug_t[:, 2 * i:2 * i + 2].rearrange("p a t -> p (a t)"), (("ev", 0), i), ACT.Gelu)
            for b in range(NB):
                put(vg[:, b, :], (("ev", 1), b), ACT.Gelu)
            stored("vg")
            for b in range(NB):
                put(pl[:, b, :], (("ev", 2), b))
            put(bs_row.rearrange("p a b -> p (a b)"), ("spread", "b_s", 0))
            stored("ev")
            for g in range(0, 4, 2):
                put(pl_t[:, g:g + 2].rearrange("p a t -> p (a t)"), ("pool", g))
                i = tile_no[("pool", g)]
                act.wait_ge(sem(f"drained{i % 8}"), i // 8 + 1)
                act.sem_inc(sem("pooled"), 1)
            act.wait_ge(sem("v_var"), 1)
            act.activation(bn.rearrange("p (b n) -> p b n", b=2)[:, :, 2:3], bn.rearrange("p (b n) -> p b n", b=2)[:, :, 1:2],
                           ACT.Sqrt, bias=eps).then_inc(sem("v_root"), 1)
            for i in range(0, 8, 4):
                put(diag_2[:, i * P:(i + 4) * P], ("spread", "g1_0", i))
            stored("g1_0")
            experts(0)

            root("mix_1", "peer_0")
            high_part(("od", 1))
            for i in range(6):
                for b in range(NB):
                    put(proj[:, b, i * 512:(i + 1) * 512], (("od", i), b))
                if i + 2 < 6:
                    high_part(("od", i + 2))
                if i in (1, 3):
                    stored(f"od{i}")
            stored("od")
            act.wait_ge(sem("angles"), 1)
            act.activation(ang[:, 4], ang[:, 2], ACT.Sin).then_inc(sem("rotation"), 1)
            act.activation(ang[:, 5], ang[:, 3], ACT.Sin).then_inc(sem("rotation"), 1)
            act.wait_ge(sem("lam_in"), 1)
            act.activation(lam2, lam2, ACT.Exp).then_inc(sem("lam_exp"), 1)
            for a, (name, dst) in enumerate((("dq_t", dq_t), ("dk_t", dk_t))):
                for b in range(NB):
                    for h in (0, 4):
                        put(dst[:, h:h + 4, b * P:(b + 1) * P], (name, b, h), src=lambda t: r3(t, 4))
                        i = tile_no[(name, b, h)]
                        act.wait_ge(sem(f"drained{i % 8}"), i // 8 + 1)
                        act.sem_inc(sem("heads_turned"), 1)
            attention(ATT["diff"])
            act.wait_ge(sem("y_ready"), 2)
            root("sub")
            for i in range(0, 8, 4):
                put(rt3.rearrange("p a n -> p (a n)")[:, i * P:(i + 4) * P], ("spread", "g1_1", i))
            stored("g1_1")
            experts(1)
            root("end2", "peer_1")

        @block.vector
        def _(dve):
            own = [0]

            def step(ins):
                own[0] += 1
                ins.then_inc(sem("dve_steps"), 1)

            def settle(but=0):
                if own[0] > but:
                    dve.wait_ge(sem("dve_steps"), own[0] - but)

            def bc(a, n):
                return a.unsqueeze(2).to_broadcast([a.shape[0], a.shape[1], n])

            def scale_block(name, b):
                n = NORMS[name]
                ns = len(n["segs"])
                dve.wait_ge(sem("rooted"), NB * n["no"] + b + 1)
                c = slice(n["col"] + b * ns, n["col"] + (b + 1) * ns)
                r = rstd[:, c]
                step(dve.reciprocal(r, rms[:, c]))
                mean, sq = newton[:, 16 * b:16 * b + ns], newton[:, 16 * b + 8:16 * b + 8 + ns]
                e = EPS * SUB * SUB if name == "sub" else EPS
                for i, j, width in widths(n["segs"]):
                    step(dve.tensor_scalar(mean[:, i:j], ss[:, c][:, i:j], 1.0 / width, e, ALU.mult, ALU.add))
                settle()
                step(dve.tensor_tensor(sq, r, r, ALU.mult))
                settle()
                step(dve.tensor_tensor(sq, sq, mean, ALU.mult))
                settle()
                step(dve.tensor_scalar(sq, sq, -0.5, 1.5, ALU.mult, ALU.add))
                settle()
                step(dve.tensor_tensor(r, r, sq, ALU.mult))
                settle()
                if name == "sub":
                    step(dve.scalar_tensor_tensor(out=r, in0=ss[:, c], scalar=SUM_MAX, in1=r, op0=ALU.is_le, op1=ALU.mult))
                    settle()
                for i, (lo, hi) in enumerate(n["segs"]):
                    ins = dve.tensor_scalar(n["dst"](b)[:, lo:hi], n["src"](b)[:, lo:hi], r[:, i:i + 1], None, ALU.mult)
                    if i == ns - 1:
                        ins.then_inc(sem("normed"), 1)
                    else:
                        step(ins)

            def scale(name, blocks=range(NB)):
                for b in blocks:
                    scale_block(name, b)

            def gain(name, dst, g, shift=None, nk=KT):
                ins = None
                for b in range(NB):
                    for i in range(0, nk, 4):
                        j = min(i + 4, nk)
                        t = wait_tile(dve, (name, b, i))
                        if shift is None:
                            part = dst[:, i:j, b * P:(b + 1) * P]
                            ins = dve.tensor_tensor(part, r3(t[:, 0:(j - i) * P], j - i), bc(g[:, i:j], P), ALU.mult)
                        else:
                            for k in range(i, j):
                                ins = dve.tensor_scalar(dst[:, k, b * P:(b + 1) * P], t[:, (k - i) * P:(k - i + 1) * P], g[:, k:k + 1],
                                                        shift[:, k:k + 1], ALU.mult, ALU.add)
                                if k < j - 1:
                                    step(ins)
                        drained(ins, (name, b, i))
                wait_own_tile((name, b, i))
                settle()
                dve.sem_inc(sem("h_ready"), 1)

            def split_ht():
                step(dve.tensor_copy(ht_parts[0], HT))
                settle()
                dve.tensor_tensor(ht_parts[1], HT, ht_parts[0].bitcast(F32), ALU.subtract).then_inc(sem("ht_parts"), 1)

            def low_part(name):
                dve.wait_ge(sem("weights_high"), split_no[name] + 1)
                dve.tensor_tensor(weights_low(name), weights(name), weights_high(name).bitcast(F32), ALU.subtract).then_inc(sem("weights_low"), 1)

            def wait_own_tile(name):
                i = tile_no[name]
                dve.wait_ge(sem(f"drained{i % 8}"), i // 8 + 1)

            def add_to_x(tiles, row=None, norm=None):
                for n, ((b, half), name) in enumerate(tiles):
                    t = wait_tile(dve, name)
                    part = X[:, b, half * 512:(half + 1) * 512]
                    if row is None:
                        drained(dve.tensor_tensor(part, part, t, ALU.add), name)
                    else:
                        tmp = hn_flat[:, (2 * b + half) * 512:(2 * b + half + 1) * 512]
                        drained(dve.tensor_tensor(tmp, t, row[:, half * 512:(half + 1) * 512], ALU.mult), name)
                        wait_own_tile(name)
                        step(dve.tensor_tensor(part, part, tmp, ALU.add))
                    if half == 1:
                        for tile_ in range(n + 1):
                            wait_own_tile(tiles[tile_][1])
                        settle()
                        dve.sem_inc(sem("x_ready"), 1)
                        if b == 0:
                            scale_block(norm, 0)

            def soft(u):
                k = u["no"] % 3
                for half in range(2):
                    t = wait_tile(dve, ("s", u["no"], half))
                    dst = u["s"][:, 2 * half:2 * half + 2, :]
                    if u["mask"] is None:
                        ins = dve.tensor_scalar(dst, r3(t, 2), u["scale"], None, ALU.mult)
                    else:
                        if isinstance(u["mask"], str):
                            mask = relb[:, u["b"], half::2, :]
                        else:
                            mask = u["mask"][:, u["b"], :].unsqueeze(1).to_broadcast([P, 2, T])
                        ins = dve.scalar_tensor_tensor(out=dst, in0=r3(t, 2), scalar=u["scale"], in1=mask, op0=ALU.mult, op1=ALU.add)
                    drained(ins, ("s", u["no"], half))
                wait_own_tile(("s", u["no"], 1))
                dve.tensor_reduce(mx[:, k, :], u["s"], AX, ALU.max, negate=True).then_inc(sem("maxima"), 1)

            def weigh(u):
                k = u["no"] % 2
                dve.wait_ge(sem("probs"), u["no"] + 1)
                step(dve.reciprocal(rinv[:, k, :], sums[:, u["no"] % 3, :]))
                settle()
                w = rinv[:, k, :]
                if u["kind"] == "diff":
                    step(dve.tensor_tensor(wcoef[:, k, :], w, coef, ALU.mult))
                    settle()
                    w = wcoef[:, k, :]
                t = wait_tile(dve, ("o", u["no"]))
                n = 4 * u["dv"]
                if u["kind"] in ("fox", "chk"):
                    dst = u["out"].rearrange("p (a b n) -> p b a n", a=2, b=2)
                    src = t[:, 0:n].rearrange("p (b a n) -> p b a n", a=2, b=2)
                    w = w.rearrange("p (b a) -> p b a", b=2).unsqueeze(3).to_broadcast([P, 2, 2, u["dv"]])
                else:
                    dst = r3(u["out"] if u["kind"] != "diff" else dtmp[:, k, :], 4)
                    src, w = r3(t[:, 0:n], 4), bc(w, u["dv"])
                drained(dve.tensor_tensor(dst, src, w, ALU.mult), ("o", u["no"]))
                if u["kind"] == "diff":
                    wait_own_tile(("o", u["no"]))
                    pair = dtmp[:, k, :].rearrange("p (m h n) -> p h m n", h=2, m=2)
                    step(dve.tensor_tensor(r3(u["out"], 2), pair[:, :, 0, :], pair[:, :, 1, :], ALU.add))

            def attention(units):
                soft(units[0])
                soft(units[1])
                for i, u in enumerate(units):
                    if i + 2 < len(units):
                        dve.wait_ge(sem("probs"), u["no"] + 1)
                        soft(units[i + 2])
                    weigh(u)
                wait_own_tile(("o", units[-1]["no"]))
                settle()

            ada_sum = [(l, j) for l in range(2) for j in range(12)]
            ada_put = list(ada_sum)

            def modulation_sum():
                l, j = ada_sum.pop(0)
                i = 12 * l + j
                name = ("ada", l, j)
                if i == 0:
                    dve.wait_ge(sem("cact"), 1)
                wait_weights(dve, name)
                w = r3(weights(name), KT)
                acc = acc_ada[:, i % 4]
                for k in range(KT):
                    for h in range(2):
                        part, wk = acc[:, h * 256:(h + 1) * 256], w[:, k, h * 256:(h + 1) * 256]
                        if k == 0:
                            ins = dve.tensor_scalar(part, wk, cact[:, 0:1], None, ALU.mult)
                        else:
                            settle(1)
                            ins = dve.scalar_tensor_tensor(out=part, in0=wk, scalar=cact[:, k:k + 1], in1=part, op0=ALU.mult, op1=ALU.add)
                        step(ins)
                settle()
                dve.sem_inc(sem("ada_summed"), 1)
                released[name] = (sem("ada_summed"), i + 1)

            def modulation_put():
                l, j = ada_put.pop(0)
                name = ("ada", l, j)
                t = wait_tile(dve, name)
                at_ = 48 * l + 4 * j
                drained(dve.tensor_tensor(MOD[:, at_:at_ + 4], t[:, 0:4], col("ada_b", at_, 4), ALU.add), name)
                return name

            def mod(l, i):
                return MOD[:, 48 * l + 8 * i:48 * l + 8 * i + 8]

            def mod_gain(g, l, i):
                step(dve.scalar_tensor_tensor(out=vec[:, 16 * l + 8 * (i > 1):16 * l + 8 * (i > 1) + 8], in0=mod(l, i), scalar=1.0,
                                              in1=g, op0=ALU.add, op1=ALU.mult))
                settle()
                return vec[:, 16 * l + 8 * (i > 1):16 * l + 8 * (i > 1) + 8]

            def diagonal(name, dst, v, n=8):
                settle()
                dve.tensor_tensor(r3(dst[:, 0:n * P], n), ident.unsqueeze(1).to_broadcast([P, n, P]), bc(v, P), ALU.mult)\
                   .then_inc(sem("diag"), 1)

            def rotate(dst1, dst2, x1, x2, c, s, tmp):
                settle()
                for i, (x, y) in enumerate(((x1, c), (x2, s), (x1, s), (x2, c))):
                    step(dve.tensor_tensor(tmp[i], x, y, ALU.mult))
                settle()
                step(dve.tensor_tensor(dst1, tmp[0], tmp[1], ALU.subtract))
                step(dve.tensor_tensor(dst2, tmp[2], tmp[3], ALU.add))

            dve.memset(ones, 1.0).then_inc(sem("made"), 1)
            dve.memset(eps, EPS).then_inc(sem("made"), 1)
            dve.memset(unit, 1.0).then_inc(sem("made"), 1)
            dve.wait_ge(sem("consts"), 48)
            scale("mix")
            gain("mix", HT, col("norm_mix"))
            dve.wait_ge(sem("masks"), 64)
            for h in range(4):
                step(dve.tensor_tensor(relb[:, :, h, :], relb[:, :, h, :], chunked, ALU.add))
            scale("mem")
            scale("lat")
            lat_g = cols[:, COLS["q_norm"][0]:COLS["q_norm"][0] + 3]
            gain("lat", lat_t, lat_g, nk=3)
            gain("mem", mem_t, col("norm_mem"))
            dve.wait_ge(sem("stored"), STORED["pc"])
            step(dve.tensor_tensor(fz[:, 0], pc[:, :, 256:260], col("f_bias").unsqueeze(1).to_broadcast([P, NB, 4]), ALU.add))
            settle()
            step(dve.tensor_scalar(fz[:, 2], fz[:, 0], -1.0, None, ALU.mult))
            settle()
            step(dve.tensor_tensor(fz[:, 1], fz[:, 0], fz[:, 2], ALU.min))
            settle()
            dve.sem_inc(sem("forget_in"), 1)
            dve.wait_ge(sem("stored"), STORED["mla"])
            for b in range(NB):
                q = mq[:, b, :].rearrange("p (h n) -> p h n", h=4)
                c = rot[:, b, 0:16].unsqueeze(1).to_broadcast([P, 4, 16])
                s = rot[:, b, 16:32].unsqueeze(1).to_broadcast([P, 4, 16])
                tmp = [r3(rtmp[:, i, :], 4) for i in range(4)]
                rotate(q[:, :, 64:80], q[:, :, 80:96], q[:, :, 64:80], q[:, :, 80:96], c, s, tmp)
                k = mk[:, b, :].rearrange("p (h n) -> p h n", h=4)
                kv = mkv[:, b, :].rearrange("p (h n) -> p h n", h=4)
                step(dve.tensor_copy(k[:, :, 0:64], kv[:, :, 0:64]))
                tmp = [rtmp[:, i, 0:16] for i in range(4)]
                rotate(k[:, 0, 64:80], k[:, 0, 80:96], pa[:, b, 384:400], pa[:, b, 400:416], rot[:, b, 0:16], rot[:, b, 16:32], tmp)
                settle()
                for h in range(1, 4):
                    step(dve.tensor_copy(k[:, h, 64:96], k[:, 0, 64:96]))
            settle()
            dve.sem_inc(sem("roped"), 1)
            dve.wait_ge(sem("forget_ln"), 1)
            step(dve.scalar_tensor_tensor(out=fz[:, 1], in0=fz[:, 0], scalar=0.0, in1=fz[:, 3], op0=ALU.min, op1=ALU.subtract))
            settle()
            for b in range(NB):
                step(dve.tensor_scalar(flb[:, b], bc(fz[:, 1, b, :], T), 8.0, None, ALU.mult))
                step(dve.tensor_scalar(nfl[:, b], bc(fz[:, 1, b, :], P), -8.0, None, ALU.mult))
            settle()
            dve.sem_inc(sem("forget"), 1)
            modulation_sum()
            attention(ATT["self"])
            dve.sem_inc(sem("y_ready"), 1)
            scale("y")
            gain("y", HT, col("out_norm"))
            add_to_x([((b, i), (("wo", i), b)) for i in range(2) for b in range(NB)], norm="cross")
            modulation_put()
            scale("cross", [1])
            modulation_sum()
            gain("cross", HT, col("norm_cross"))
            modulation_sum()
            modulation_put()
            attention(ATT["cross"])
            dve.sem_inc(sem("cross_out"), 1)
            modulation_sum()
            modulation_put()
            add_to_x([((b, half), ("wco", b, half)) for b in range(NB) for half in range(2)], norm="ffn")
            scale("ffn", [1])
            gain("ffn", HT, col("norm_ffn"))
            for i in range(FT // 2):
                dve.wait_ge(sem("silu"), i + 1)
                t = wait_tile(dve, (("gu", i), 1))
                ins = dve.tensor_tensor(act_t[:, 2 * i:2 * i + 2, :], r3(silu_g[:, i % 2], 2), r3(t, 2), ALU.mult)
                drained(ins, (("gu", i), 1))
                wait_own_tile((("gu", i), 1))
                dve.sem_inc(sem("act_ready"), 1)
                modulation_sum()
                modulation_put()
            for c in range(6):
                modulation_sum()
                if c < 4:
                    modulation_put()
            add_to_x([((b, half), ("down", b, half)) for b in range(NB) for half in range(2)], norm="end1")
            for _ in range(2):
                modulation_put()
            diagonal("end1", diag_f, col("final_norm"))
            scale("end1", [1])

            def end_rows(name, dst):
                dve.wait_ge(sem("normed"), NB * NORMS[name]["no"] + NB)
                for half in range(2):
                    t = wait_tile(dve, ("spread", name, 4 * half))
                    for b in range(NB):
                        ins = dve.tensor_tensor(dst[:, b, half * 512:(half + 1) * 512], HN[:, b, half * 512:(half + 1) * 512], t, ALU.mult)
                        if b == NB - 1:
                            drained(ins, ("spread", name, 4 * half))
                        else:
                            step(ins)
                settle()
                wait_own_tile(("spread", name, 4))
                dve.sem_inc(sem("x_ready"), NB)

            end_rows("end1", X)

            def experts(l):
                scale(f"peer_{l}", [1])
                g = mod_gain(col("norm_ffn_2", 8 * l, 8), l, 4)
                gain(f"peer_{l}", HT, g, mod(l, 3))
                lo, hi = slice(0, 8), slice(8, 16)

                def best_16(chains):
                    others = len(chains) - 1
                    for op in range(5):
                        for src, rest, v, at_ in chains:
                            settle(others)
                            if op == 0:
                                ins = dve.max(v[:, lo], src)
                            elif op == 1:
                                ins = dve.max_index(at_[:, lo], v[:, lo], src)
                            elif op == 2:
                                ins = dve.match_replace(rest, v[:, lo], src, 4 * NEG)
                            elif op == 3:
                                ins = dve.max(v[:, hi], rest)
                            else:
                                ins = dve.max_index(at_[:, hi], v[:, hi], rest)
                            step(ins)
                    settle()

                for i in range(4):
                    m = slice(4 * i, 4 * i + 4)
                    for h in (2 * i, 2 * i + 1):
                        dve.wait_ge(sem("stored"), STORED[f"sc_{l}_{h}"])
                        best_16([(sc[:, 2 * h + a, b, :], sw[:, 2 * h + a, b, :], top_v[:, a, 2 * h + b], top_i[:, a, 2 * h + b])
                                 for a in range(2) for b in range(NB)])
                    v0, v1 = top_v[:, 0, m], top_v[:, 1, m]
                    step(dve.tensor_tensor(cand[:, m, 0:16], v0[:, :, 0:1].to_broadcast([P, 4, TOPK]), v1, ALU.add))
                    step(dve.tensor_tensor(cand[:, m, 16:72].rearrange("p m (i j) -> p m i j", j=8),
                                           v0[:, :, 1:8].unsqueeze(3).to_broadcast([P, 4, 7, 8]),
                                           v1[:, :, 0:8].unsqueeze(2).to_broadcast([P, 4, 7, 8]), ALU.add))
                    step(dve.tensor_tensor(cand[:, m, 72:80], v0[:, :, 8:16], v1[:, :, 0:1].to_broadcast([P, 4, 8]), ALU.add))
                    step(dve.tensor_copy(top_f[:, :, m], top_i[:, :, m]))
                    settle()
                    best_16([(cand[:, n, :], cw[:, n, :], fin_v[:, n], fin_p[:, TOPK * n:TOPK * (n + 1)]) for n in range(4 * i, 4 * i + 4)])
                    step(dve.tensor_copy(gsum[:, 0, m], fin_v[:, m, 0]))
                    q = slice(64 * i, 64 * i + 64)
                    p_ = fin_p[:, q]
                    row, column, whole_p = fin_f[:, 0, q], fin_f[:, 1, q], fin_f[:, 2, q]
                    step(dve.tensor_scalar(fin_ij[:, 0, q], p_, 3, None, ALU.logical_shift_right))
                    step(dve.tensor_scalar(fin_ij[:, 1, q], p_, 7, None, ALU.bitwise_and))
                    step(dve.tensor_copy(whole_p, p_))
                    settle(3)
                    step(dve.tensor_tensor(fin_v[:, m], fin_v[:, m], bc(gsum[:, 0, m], TOPK), ALU.subtract))
                    settle(1)
                    step(dve.tensor_copy(fin_f[:, 0:2, q], fin_ij[:, :, q]))
                    settle()
                    dve.sem_inc(sem("gate_in"), 1)
                    step(dve.tensor_scalar(row, row, -1.0, 0.0, ALU.add, ALU.max))
                    step(dve.scalar_tensor_tensor(out=column, in0=whole_p, scalar=72.0, in1=column, op0=ALU.is_lt, op1=ALU.mult))
                    settle(1)
                    step(dve.scalar_tensor_tensor(out=row, in0=whole_p, scalar=-64.0, in1=row, op0=ALU.add, op1=ALU.max))
                    settle()
                    step(dve.scalar_tensor_tensor(out=whole_p, in0=whole_p, scalar=16.0, in1=whole_p, op0=ALU.is_lt, op1=ALU.mult))
                    settle()
                    step(dve.tensor_tensor(column, column, whole_p, ALU.max))
                    settle()
                    for a in range(2):
                        step(dve.tensor_tensor(r3(eq[:, a], 64), iota[:, 0:TOPK].unsqueeze(1).to_broadcast([P, 64, TOPK]),
                                               bc(fin_f[:, a, q], TOPK), ALU.is_equal))
                    for a in range(2):
                        e = eq[:, a].rearrange("p (m k n) -> p m k n", m=4, k=TOPK)
                        settle(1)
                        step(dve.tensor_tensor(e, e, top_f[:, a, m].unsqueeze(2).to_broadcast([P, 4, TOPK, TOPK]), ALU.mult))
                    for a in range(2):
                        settle(1 + a)
                        picked = eq[:, a].rearrange("p (h b k n) -> p h b k n", h=2, b=NB, n=TOPK)
                        for b in range(NB):
                            step(dve.tensor_reduce(chosen_h[:, a, 2 * i:2 * i + 2, b], picked[:, :, b], AX, ALU.add))
                    dve.wait_ge(sem("gate_exp"), 4 * l + i + 1)
                    gate = chosen_h[:, 2, 2 * i:2 * i + 2]
                    step(dve.tensor_reduce(gsum[:, 1, m].rearrange("p (h b) -> p h b", b=NB), gate, AX, ALU.add))
                    settle()
                    step(dve.reciprocal(gsum[:, 0, m], gsum[:, 1, m]))
                    settle()
                    step(dve.tensor_tensor(gate, gate, gsum[:, 0, m].rearrange("p (h b) -> p h b", b=NB).unsqueeze(3).to_broadcast([P, 2, NB, TOPK]), ALU.mult))
                    settle()
                dve.sem_inc(sem("chosen"), 1)
                for b in range(NB):
                    t = wait_tile(dve, (f"slots_{l}", b))
                    drained(dve.tensor_copy(slots_t[:, :, b * P:(b + 1) * P], r3(t[:, 0:3 * P], 3)), (f"slots_{l}", b))
                    wait_own_tile((f"slots_{l}", b))
                    dve.sem_inc(sem("slots"), 1)

                def one_hots(u, at_):
                    for t in range(GROUP):
                        dve.tensor_scalar(hot[:, u, 0, t, :], iota, slots_t[:, 0, bass.ds(at_ + t, 1)], None, ALU.is_equal)
                        ins = dve.tensor_scalar(hot[:, u, 1, t, :], iota, slots_t[:, 1, bass.ds(at_ + t, 1)],
                                                slots_t[:, 2, bass.ds(at_ + t, 1)], ALU.is_equal, ALU.mult)
                    ins.then_inc(sem("hot"), 1)

                for u in range(2):
                    one_hots(u, u * GROUP)
                with dve.Fori(1, NG // 2) as i:
                    for u in range(2):
                        dve.wait_ge(sem("gates_made"), i * 2 + (l * NG + u - 1))
                        one_hots(u, i * (2 * GROUP) + u * GROUP)
                dve.wait_ge(sem("gates_stored"), (l + 1) * NG)
                diagonal(f"g2_{l}", hn_flat, mod(l, 5))
                def high(dst, src):
                    return dve.tensor_copy(dst, src)

                def low(dst, src, h):
                    return dve.tensor_tensor(dst, src, h.bitcast(F32), ALU.subtract)

                def arrived(kind, n, turn=None):
                    s = n % E_SLOTS
                    count = 16 * (l * len(range(s, TILES, E_SLOTS)) + n // E_SLOTS + 1)
                    dve.wait_ge(sem(f"expert_{kind}{s}_arrived"), count if turn is None else turn * (16 * STEP // E_SLOTS) + count)

                settle()
                step(high(ht_high, HT))
                settle()
                low(ht_low, HT, ht_high).then_inc(sem("ht_split"), 1)
                for n in range(2):
                    arrived("u", n)
                    step(high(exp_uh[:, n], exp_u[:, n]))
                    settle()
                    low(exp_ul[:, n], exp_u[:, n], exp_uh[:, n]).then_inc(sem("expert_u"), 1)
                arrived("v", 0)
                step(high(exp_vh[:, 0], exp_v[:, 0]))
                settle()
                low(exp_vl[:, 0], exp_v[:, 0], exp_vh[:, 0]).then_inc(sem("expert_v"), 1)

                def expert(j, turn=None, more_u=True, more_v=True):
                    def at_(n, each=1):
                        return n if turn is None else turn * (STEP * each) + n

                    n = at_(j)
                    done = split_base + 4 * j
                    dve.wait_ge(sem("expert_act"), at_(l * TILES + j + 1))
                    g = gates[:, :, bass.ds(n, 1)].rearrange("p t o -> p (t o)") if turn is not None else gates[:, :, j]
                    dve.tensor_tensor(act_e[:, j % 2], act_e[:, j % 2], g, ALU.mult).then_inc(sem("split_steps"), 1)
                    if more_u:
                        u, ul, uh = exp_u[:, (j + 2) % E_SLOTS], exp_ul[:, (j + 2) % E_SLOTS], exp_uh[:, j % 2]
                        arrived("u", j + 2, turn)
                        high(uh, u).then_inc(sem("split_steps"), 1)
                    dve.wait_ge(sem("split_steps"), at_(done + 1, 4))
                    high(act_h[:, j % 2], act_e[:, j % 2]).then_inc(sem("split_steps"), 1)
                    if more_u:
                        dve.wait_ge(sem("split_steps"), at_(done + 2, 4))
                        low(ul, u, uh).then_inc(sem("expert_u"), 1)
                    dve.wait_ge(sem("split_steps"), at_(done + 2 + more_u, 4))
                    low(act_l[:, j % 2], act_e[:, j % 2], act_h[:, j % 2]).then_inc(sem("expert_gated"), 1)
                    if more_v:
                        v, vl, vh = exp_v[:, (j + 1) % E_SLOTS], exp_vl[:, (j + 1) % E_SLOTS], exp_vh[:, (j + 1) % 2]
                        arrived("v", j + 1, turn)
                        dve.wait_ge(sem("expert_used"), at_(l * (TILES + 1) + j + 1))
                        high(vh, v).then_inc(sem("split_steps"), 1)
                        dve.wait_ge(sem("split_steps"), at_(done + 3 + more_u, 4))
                        low(vl, v, vh).then_inc(sem("expert_v"), 1)

                split_base = l * (4 * TILES - 3)
                with dve.Fori(0, (TILES - 2) // STEP) as i:
                    for j in range(STEP):
                        expert(j, i)
                expert(TILES - 2, more_u=False)
                split_base -= 1
                expert(TILES - 1, more_u=False, more_v=False)
                dve.wait_ge(sem("expert_used"), (l + 1) * (TILES + 1))
                for b in range(NB):
                    for half in range(2):
                        tmp = diag_3[:, half * 512:(half + 1) * 512]
                        settle()
                        step(dve.tensor_tensor(tmp, ps[:, 2 * b + half, :], g2_row[:, half * 512:(half + 1) * 512], ALU.mult))
                        settle()
                        part = X[:, b, half * 512:(half + 1) * 512]
                        step(dve.tensor_tensor(part, part, tmp, ALU.add))
                    settle()
                    dve.sem_inc(sem("x_ready"), 1)

            scale("mix_0")
            g = mod_gain(col("norm_mix_2", 0, 8), 0, 1)
            gain("mix_0", HT, g, mod(0, 0))
            for i in range(3):
                modulation_sum()
                modulation_put()
            modulation_put()
            diagonal("b_s", diag_2, col("b_s"), 4)
            dve.wait_ge(sem("pool_mat"), 32)
            wait_weights(dve, ("evs",))
            w = weights(("evs",))
            step(dve.tensor_tensor(ws_m, r3(w[:, 0:512], 4), tri_2.unsqueeze(1).to_broadcast([P, 4, P]), ALU.mult))
            dve.wait_ge(sem("stored"), STORED["vg"])
            bnv = bn.rearrange("p (b n) -> p b n", b=2)
            for b in range(NB):
                settle()
                step(dve.bn_stats(vec[:, 48:54], vg[:, b, :]))
                settle()
                step(dve.bn_aggr(bnv[:, b, 0:2], vec[:, 48:54]))
            settle()
            dve.sem_inc(sem("v_var"), 1)
            dve.wait_ge(sem("v_root"), 1)
            step(dve.reciprocal(bnv[:, :, 3:4], bnv[:, :, 2:3]))
            settle()
            for b in range(NB):
                step(dve.tensor_scalar(vn[:, b, :], vg[:, b, :], bnv[:, b, 0:1], bnv[:, b, 3:4], ALU.subtract, ALU.mult))
            settle()
            dve.sem_inc(sem("spatial_in"), 1)
            for g in range(0, 4, 2):
                t = wait_tile(dve, ("mixed", g))
                drained(dve.tensor_tensor(HT[:, 4 + g:6 + g, :], r3(t, 2), bc(col("pool_scale", g, 2), T), ALU.mult), ("mixed", g))
            dve.wait_ge(sem("stored"), STORED["ev"])
            for b in range(NB):
                part = HT[:, 0:4, b * P:(b + 1) * P]
                t = wait_tile(dve, ("spatial", b))
                drained(dve.tensor_tensor(part, r3(t, 4), bc(col("g_v"), P), ALU.mult), ("spatial", b))
                wait_own_tile(("spatial", b))
                step(dve.tensor_tensor(part, part, bs_row, ALU.add))
                settle()
                step(dve.tensor_tensor(part, part, ug_t[:, :, b * P:(b + 1) * P], ALU.mult))
            settle()
            dve.sem_inc(sem("h_ready"), 1)
            diagonal("g1_0", hn_flat, mod(0, 2))
            dve.wait_ge(sem("stored"), STORED["g1_0"])
            add_to_x([((b, i), (("evo", i), b)) for i in range(2) for b in range(NB)], diag_2, "peer_0")
            experts(0)

            dve.wait_ge(sem("consts3"), 48)
            step(dve.tensor_copy(posf, pos_i[:, :]))
            settle()
            for b in range(NB):
                step(dve.tensor_scalar(ang[:, 0, b, :], inv_f, posf[:, b:b + 1], None, ALU.mult))
            settle()
            magic, two_pi = 12582912.0, 2 * np.pi
            p1 = 6.28125
            p2 = 0.001934051513671875
            p3 = two_pi - p1 - p2
            step(dve.tensor_scalar(ang[:, 1], ang[:, 0], float(1 / two_pi), magic, ALU.mult, ALU.add))
            settle()
            step(dve.tensor_scalar(ang[:, 1], ang[:, 1], magic, None, ALU.subtract))
            settle()
            for p in (p1, p2, p3):
                step(dve.scalar_tensor_tensor(out=ang[:, 0], in0=ang[:, 1], scalar=-float(p), in1=ang[:, 0], op0=ALU.mult, op1=ALU.add))
                settle()
            lim = 3.1415925
            step(dve.tensor_scalar(ang[:, 2], ang[:, 0], lim, -lim, ALU.min, ALU.max))
            step(dve.tensor_scalar(ang[:, 3], ang[:, 0], float(np.pi / 2), None, ALU.add))
            settle()
            step(dve.tensor_scalar(ang[:, 1], ang[:, 3], float(np.pi), -float(two_pi), ALU.is_gt, ALU.mult))
            settle()
            step(dve.tensor_tensor(ang[:, 3], ang[:, 3], ang[:, 1], ALU.add))
            settle()
            step(dve.tensor_scalar(ang[:, 3], ang[:, 3], lim, -lim, ALU.min, ALU.max))
            settle()
            dve.sem_inc(sem("angles"), 1)
            for i in range(2):
                step(dve.tensor_tensor(lam_p[:, i, :], lam_in[:, 2 * i, :], lam_in[:, 2 * i + 1, :], ALU.mult))
            settle()
            step(dve.tensor_reduce(lam2, lam_p, AX, ALU.add))
            settle()
            dve.sem_inc(sem("lam_in"), 1)
            step(dve.memset(coef, 1.0))
            step(dve.memset(vec[:, 58:59], EPS * SUB * SUB))
            step(dve.tensor_scalar(vec[:, 56:57], col("g_sub"), 1.0 - LAM_INIT, None, ALU.mult))
            scale("mix_1")
            g = mod_gain(col("norm_mix_2", 8, 8), 1, 1)
            gain("mix_1", HT, g, mod(1, 0))
            split_ht()
            for i in range(1, 6):
                low_part(("od", i))
            dve.wait_ge(sem("lam_exp"), 1)
            step(dve.tensor_tensor(vec[:, 57:58], lam2[:, 1:2], lam2[:, 0:1], ALU.subtract))
            settle()
            for i in (2, 3):
                step(dve.tensor_scalar(coef[:, i:i + 1], vec[:, 57:58], LAM_INIT, None, ALU.subtract))
            dve.wait_ge(sem("rotation"), 2)
            for a in range(2):
                dve.wait_ge(sem("stored"), STORED[f"od{2 * a + 1}"])
                for b in range(NB):
                    x = proj[:, b, a * D:(a + 1) * D].rearrange("p (m n) -> p m n", m=16)
                    y = dqk[:, a, b, :].rearrange("p (m n) -> p m n", m=16)
                    c = ang[:, 5, b, :].unsqueeze(1).to_broadcast([P, 16, 32])
                    s = ang[:, 4, b, :].unsqueeze(1).to_broadcast([P, 16, 32])
                    rotate(y[:, :, 0:32], y[:, :, 32:64], x[:, :, 0:32], x[:, :, 32:64], c, s, [r3(rt3[:, i, :], 16) for i in range(4)])
                settle()
                dve.sem_inc(sem("roped"), 1)
            attention(ATT["diff"])
            step(dve.tensor_scalar(do, do, SUB, SUB_MAX, ALU.mult, ALU.min))
            settle()
            step(dve.tensor_scalar(do, do, -SUB_MAX, None, ALU.max))
            settle()
            dve.sem_inc(sem("y_ready"), 1)
            scale("sub")
            gain("sub", HT, vec[:, 56:57].to_broadcast([P, 8]))
            diagonal("g1_1", diag_3, mod(1, 2))
            dve.wait_ge(sem("stored"), STORED["g1_1"])
            add_to_x([((b, i), (("odo", i), b)) for i in range(2) for b in range(NB)],
                     rt3.rearrange("p a n -> p (a n)"), "peer_1")
            experts(1)
            diagonal("end2", diag_3, col("final_norm_2"))
            scale("end2")
            end_rows("end2", HN)

        @block.sync
        def _(sp):
            sp.dma_start(X.rearrange("p b n -> p (b n)"), d["x"]).then_inc(sem("x_loaded"), 16)
            sp.dma_start(cols[:, :], d["cols"]).then_inc(sem("consts"), 16)
            sp.dma_start(ident, d["perm"][:, 0:P]).then_inc(sem("consts"), 16)
            sp.dma_start(iota, d["perm"][:, P:2 * P]).then_inc(sem("consts"), 16)

            def load(i):
                name = STREAM[i]
                if i >= SLOTS:
                    s, v = released[STREAM[i - SLOTS]]
                    sp.wait_ge(s, v)
                sp.dma_start(weights(name), d["stream"][i, :, 0:SIZE.get(name, SLOT)]).then_inc(sem(f"arrived{i % SLOTS}"), 16)

            def load_experts(l):
                for j in range(SLOTS):
                    i = chunk_no[("pq", l, 3)] - j
                    s, v = released[STREAM[i]]
                    sp.wait_ge(s, v)
                base = l * TILES

                def fetch(s, src_u, src_v, scored=None, used=None):
                    if scored is not None:
                        sp.wait_ge(sem("expert_scored"), scored)
                    sp.dma_start(exp_u[:, s, :], src_u).then_inc(sem(f"expert_u{s}_arrived"), 16)
                    if used is not None:
                        sp.wait_ge(sem("expert_used"), used)
                    sp.dma_start(exp_v[:, s, :], src_v).then_inc(sem(f"expert_v{s}_arrived"), 16)

                u, v = d["experts_u"][l], d["experts_v"][l]
                for n in range(E_SLOTS):
                    fetch(n, u[n], v[n])
                turns = (TILES - E_SLOTS) // E_SLOTS
                with sp.Fori(0, turns) as i:
                    for s in range(E_SLOTS):
                        at_ = bass.ds(i * E_SLOTS + (E_SLOTS + s), 1)
                        fetch(s, u[at_].rearrange("o p n -> (o p) n"), v[at_].rearrange("o p n -> (o p) n"),
                              i * E_SLOTS + (base + s + 1), i * E_SLOTS + (base + l + s + 2))
                for n in range((turns + 1) * E_SLOTS, TILES):
                    fetch(n % E_SLOTS, u[n], v[n], base + n - 2, base + l + n - 1)
                sp.wait_ge(sem("expert_used"), (l + 1) * (TILES + 1))

            def load_keys(l):
                sp.dma_start(keys_t.rearrange("p s n -> p (s n)"), d["keys"][l]).then_inc(sem("keys_loaded"), 16)

            load(0)
            sp.dma_start(mem.rearrange("p b n -> p (b n)"), d["mem"]).then_inc(sem("mem_loaded"), 16)
            load(1)
            sp.dma_start(arena[:, 0:3 * 2 * T], d["masks"]).then_inc(sem("masks"), 16)
            sp.dma_start(rot.rearrange("p b n -> p (b n)"), d["rot"]).then_inc(sem("masks"), 16)
            sp.dma_start(relb.rearrange("p b h k -> p (b h k)"), d["rel"]).then_inc(sem("masks"), 16)
            sp.dma_start(pos_i[:, :], d["pos"]).then_inc(sem("masks"), 16)
            for i in range(2, len(STREAM)):
                name = STREAM[i]
                if name == ("evs",):
                    sp.wait_ge(sem("x_ready"), X_READY["end1"])
                    sp.dma_start(pool_mat.rearrange("p s g t -> p (s g t)"), d["pool"]).then_inc(sem("pool_mat"), 16)
                    sp.dma_start(tri_2, d["masks"][:, 4 * T:4 * T + P]).then_inc(sem("pool_mat"), 16)
                if name == ("evs",):
                    load_keys(0)
                if name == ("od", SLOTS):
                    sp.wait_ge(sem("x_ready"), X_READY["peer_0"])
                    load_keys(1)
                load(i)
                if name in (("pq", 0, 3), ("pq", 1, 3)):
                    load_experts(name[1])
                if name == ("pq", 0, 3):
                    sp.dma_start(causal_3.rearrange("p b k -> p (b k)"), d["masks"][:, 0:2 * T]).then_inc(sem("consts3"), 16)
                    sp.dma_start(inv_f, d["inv_f"]).then_inc(sem("consts3"), 16)
                    sp.dma_start(lam_in.rearrange("p a n -> p (a n)"), d["lam"]).then_inc(sem("consts3"), 16)
            sp.wait_ge(sem("x_ready"), X_READY["end2"])
            for b in range(NB):
                sp.dma_start(out[0, b * P:(b + 1) * P, :], HN[:, b, :]).then_inc(sem("written"), 16)
            sp.wait_ge(sem("written"), 16 * NB)


H_READY = {n: i + 1 for i, n in enumerate(("mix", "lat", "mem", "y", "cross", "ffn", "mix_0", "even_y", "peer_0", "mix_1", "sub", "peer_1"))}
X_READY = {n: NB * (i + 1) for i, n in enumerate(("wo", "wco", "down", "end1", "mix_0", "peer_0", "mix_1", "peer_1", "end2"))}
STORED = {n: i + 1 for i, n in enumerate(("pc", "win", "mla", "cv", "wcq", "vg", "ev", "g1_0", *(f"{n}_0_{i}" for i in range(HEADS8) for n in ("pq", "sc")),
                                          "od1", "od3", "od", "g1_1", *(f"{n}_1_{i}" for i in range(HEADS8) for n in ("pq", "sc"))))}
SPREADS = {n: i for i, n in enumerate(("end1", "b_s", "g1_0", "g2_0", "g1_1", "g2_1", "end2"))}


def _tiles(w):
    k, n = w.shape
    return w.reshape(k // P, P, n).transpose(1, 0, 2).reshape(P, -1)


def _layout(a):
    f = np.float32
    m = {k: np.asarray(v) for k, v in a.items()}
    stream = np.zeros((len(STREAM), P, SLOT), f)
    w_in, ckv, gu, down = m["w_in"][0], m["w_ckv"][0], m["w_gu"][0], m["w_down"][0]
    ev, od = m["ev_w_in_2"][0], m["od_w_in_2"][0]
    for i, name in enumerate(STREAM):
        kind, j = name[0], name[1] if len(name) > 1 else 0
        c = slice(512 * j, 512 * j + 512)
        if kind == "win":
            t = _tiles(w_in[:, WIN[j]:WIN[j + 1]])
        elif kind == "mla":
            t = np.concatenate([_tiles(m["w_uq"][0]), _tiles(m["w_ukv"][0])], 1)
        elif kind == "ck":
            t = _tiles(ckv[:, 0:512])
        elif kind == "cv":
            t = _tiles(ckv[:, 512:])
        elif kind == "wo":
            t = _tiles(m["w_o"][0][:, c])
        elif kind == "wcq":
            t = _tiles(m["w_cq"][0])
        elif kind == "wco":
            t = _tiles(m["w_co"][0])
        elif kind == "gu":
            t = _tiles(np.concatenate([gu[:, 256 * j:256 * j + 256], gu[:, FFN + 256 * j:FFN + 256 * j + 256]], 1))
        elif kind == "down":
            t = _tiles(down[512 * j:min(512 * j + 512, FFN)])
        elif kind == "ada":
            t = _tiles(m["ada_w_2"][name[1]][:, 512 * name[2]:512 * name[2] + 512])
        elif kind == "ev":
            t = _tiles(ev[:, c])
        elif kind == "evs":
            t = np.concatenate([m["ev_w_s_2"][0].transpose(2, 0, 1).reshape(P, -1), m["ev_w_pool_2"][0].transpose(1, 0, 2).reshape(P, -1)], 1)
        elif kind == "evo":
            t = _tiles(m["ev_w_out_2"][0][:, c])
        elif kind == "pq":
            t = _tiles(m["peer_w_q_2"][name[1]].reshape(D, -1)[:, 512 * name[2]:512 * name[2] + 512])
        elif kind == "od":
            t = _tiles(od[:, c])
        else:
            t = _tiles(m["od_w_out_2"][0][:, c])
        stream[i, :, 0:t.shape[1]] = t
        assert t.shape[1] == SIZE.get(name, SLOT), name

    def cv(x):
        return np.asarray(x).reshape(-1, P).T

    parts = {"norm_mix": cv(m["norm_mix"]), "q_norm": cv(m["q_norm"]), "kv_norm": cv(m["kv_norm"]), "out_norm": cv(m["out_norm"]),
             "norm_cross": cv(m["norm_cross"]), "norm_mem": cv(m["norm_mem"]), "norm_ffn": cv(m["norm_ffn"]),
             "final_norm": cv(m["final_norm"]), "c": cv(m["c_2"]), "ada_b": cv(m["ada_b_2"]), "norm_mix_2": cv(m["norm_mix_2"]),
             "norm_ffn_2": cv(m["norm_ffn_2"]), "g_v": cv(m["ev_g_v_2"]), "pool_scale": cv(m["ev_pool_scale_2"]),
             "b_s": cv(m["ev_b_s_2"]), "g_sub": cv(m["od_g_sub_2"]), "final_norm_2": cv(m["final_norm_2"]),
             "f_bias": np.repeat(m["f_bias"].reshape(1, 4), P, 0)}
    cols = np.zeros((P, NCOLS), f)
    for name, (a_, n) in COLS.items():
        cols[:, a_:a_ + n] = parts[name]

    q = np.arange(T)
    causal = np.where(q[None, :] <= q[:, None], 0.0, NEG).astype(f)
    chunked = np.where(q[None, :] // 64 <= q[:, None] // 64, 0.0, NEG).astype(f)
    tri = (q[:, None] <= q[None, :]).astype(f)
    masks = np.concatenate([_tiles(causal), _tiles(chunked), _tiles(tri)], 1)
    inv = (np.float32(10000.0) ** (-np.arange(0, ROPE, 2, dtype=f) / f(ROPE))).astype(f)
    turns = (q.astype(f)[:, None] * inv[None, :]).astype(f)
    rot = _tiles(np.concatenate([np.cos(turns), np.sin(turns)], 1).astype(f))
    pool = np.zeros((4, T, T), f)
    for g, w in enumerate(WINDOWS):
        for t in range(T):
            lo = max(0, t + 1 - w)
            pool[g, lo:t + 1, t] = f(1.0) / f(min(t + 1, w))
            pool[g, t, t] -= f(1.0)
    pool = pool.reshape(4, NB, P, T).transpose(2, 1, 0, 3).reshape(P, -1)
    table = m["rel_bias"][0]
    band = np.concatenate([np.repeat(table[:, -1:], T - 1 - 128, 1), table[:, ::-1], np.repeat(table[:, 0:1], T - 1 - 63, 1)], 1)
    rel = np.stack([band[:, T - 1 - i:2 * T - 1 - i] for i in range(T)])
    rel = rel.reshape(NB, P, 4, T).transpose(1, 0, 2, 3).reshape(P, -1)
    lam = np.concatenate([m[f"od_lam_{n}_2"].reshape(1, -1) for n in ("q1", "k1", "q2", "k2")], 1)
    keys = np.stack([m["peer_sub_keys_2"][l].reshape(SETS, NKEYS, P).transpose(2, 0, 1).reshape(P, -1) for l in range(2)])
    experts_u = m["peer_u_2"].reshape(2, TILES, P, KT, P).transpose(0, 1, 4, 3, 2).reshape(2, TILES, P, D)
    inv3 = (f(1.0) / (f(10000.0) ** (np.arange(0, 64, 2, dtype=f) / f(64)))).astype(f)
    return {
        "x": _tiles(m["x"][0]), "mem": _tiles(m["mem"][0]), "cols": cols, "stream": stream,
        "perm": np.concatenate([np.eye(P, dtype=f), np.repeat(np.arange(P, dtype=f)[None], P, 0)], 1),
        "masks": masks, "rot": rot, "rel": rel, "pos": m["positions_2"].reshape(NB, P).T.astype(np.int32),
        "pool": pool, "inv_f": np.repeat(inv3[None], P, 0), "lam": np.repeat(lam, P, 0),
        "keys": keys, "experts_u": experts_u, "experts_v": m["peer_v_2"].reshape(2, TILES, P, D),
    }


def kernel(**inputs):
    import concourse.bacc as bacc
    from concourse.bass_utils import run_bass_kernel_spmd

    arrays = {k: np.ascontiguousarray(v) for k, v in _layout(inputs).items()}
    nc = bacc.Bacc("TRN2", target_bir_lowering=False, num_devices=1)
    d = {k: nc.dram_tensor(f"in_{k}", v.shape, mybir.dt.from_np(v.dtype), kind="ExternalInput").ap() for k, v in arrays.items()}
    out = nc.dram_tensor("out_0", (1, T, D), F32, kind="ExternalOutput").ap()
    program(nc, d, out)
    r = run_bass_kernel_spmd(nc, [{f"in_{k}": v for k, v in arrays.items()}], core_ids=[0])
    return r.results[0]["out_0"]
```
